# Optimizing a Trainium2 kernel written in Bass

```python
import math
import jax, jax.numpy as jnp
from jax import lax
import numpy as np

D_MODEL = 1024
BATCH = 1
SEQ = 256
DEPTH = 2
DEC_BATCH = 8
DEC_SEQ = 4
PAST_LEN = 1024
PAGE_SIZE = 128

N_AB = (DEPTH + 1) // 2
N_C = DEPTH // 2
MLA_HEADS = 8
Q_LORA = 384
KV_LORA = 256
NOPE_DIM = 64
ROPE_DIM = 32
QK_DIM = NOPE_DIM + ROPE_DIM
V_DIM = 64
ROPE_THETA = 10000.0
Q_BLOCK = 128
GLA_HEADS = 4
GLA_DK = 128
GLA_DV = 128
GLA_GATE_RANK = 16
GLA_TAU = 16.0
GLA_CHUNK = 64
S5_GROUP = 16
S5_GROUPS = D_MODEL // S5_GROUP
S5_STATE = 64
DT_MIN = 0.001
DT_MAX = 0.1
D_FF = 4 * D_MODEL
PLE_DIM = 256
EPS = 1e-6

IN_SPLITS = (Q_LORA, KV_LORA, ROPE_DIM, GLA_HEADS * GLA_DK, GLA_HEADS * GLA_DK,
             GLA_HEADS * GLA_DV, GLA_GATE_RANK, GLA_HEADS * GLA_DV)
IN_AB = sum(IN_SPLITS)
MIX_AB = MLA_HEADS * V_DIM + GLA_HEADS * GLA_DV

kernel_name = 'mla_gla_s5_hybrid_step'

def rmsnorm(x, g):
    xf = x.astype(jnp.float32)
    y = xf * lax.rsqrt(jnp.mean(xf * xf, axis=-1, keepdims=True) + EPS)
    return (y * g.astype(jnp.float32)).astype(x.dtype)

def rope_tail(x, pos):
    half = ROPE_DIM // 2
    freqs = ROPE_THETA ** (-jnp.arange(half, dtype=jnp.float32) / half)
    ang = pos.astype(jnp.float32)[:, None] * freqs[None, :]
    cos = jnp.cos(ang)[:, None, :]
    sin = jnp.sin(ang)[:, None, :]
    xr = x[..., NOPE_DIM:].astype(jnp.float32)
    x1, x2 = xr[..., :half], xr[..., half:]
    rot = jnp.concatenate([x1 * cos - x2 * sin, x2 * cos + x1 * sin], axis=-1).astype(x.dtype)
    return jnp.concatenate([x[..., :NOPE_DIM], rot], axis=-1)

def mla_queries(c_q, pos, g_qlat, w_uq, g_qh):
    bt, l = c_q.shape[:2]
    q = jnp.einsum('blr,rz->blz', rmsnorm(c_q, g_qlat), w_uq).reshape(bt, l, MLA_HEADS, QK_DIM)
    return rope_tail(rmsnorm(q, g_qh), pos)

def mla_keys_values(c_kv, k_pe, pos, w_ukv, g_kh):
    bt, l = c_kv.shape[:2]
    kv = jnp.einsum('blr,rz->blz', c_kv, w_ukv).reshape(bt, l, MLA_HEADS, NOPE_DIM + V_DIM)
    k_nope, v = kv[..., :NOPE_DIM], kv[..., NOPE_DIM:]
    k_rot = jnp.broadcast_to(k_pe[:, :, None, :], (bt, l, MLA_HEADS, ROPE_DIM)).astype(k_nope.dtype)
    k = jnp.concatenate([k_nope, k_rot], axis=-1)
    return rope_tail(rmsnorm(k, g_kh), pos), v

def mla_prompt_attention(q, k, v):
    bt, s = q.shape[:2]
    nb = s // Q_BLOCK
    scale = QK_DIM ** -0.5
    qb = q.reshape(bt, nb, Q_BLOCK, MLA_HEADS, QK_DIM).swapaxes(0, 1)
    kpos = jnp.arange(s)

    def block(args):
        qi, bi = args
        sc = jnp.einsum('bqhd,bkhd->bhqk', qi, k).astype(jnp.float32) * scale
        qpos = bi * Q_BLOCK + jnp.arange(Q_BLOCK)
        sc = jnp.where(kpos[None, :] <= qpos[:, None], sc, -jnp.inf)
        p = jax.nn.softmax(sc, axis=-1).astype(v.dtype)
        return jnp.einsum('bhqk,bkhv->bqhv', p, v)

    o = lax.map(block, (qb, jnp.arange(nb)))
    return o.swapaxes(0, 1).reshape(bt, s, MLA_HEADS * V_DIM)

def mla_sample_attention(q, k_new, v_new, cache_ckv_l, cache_kpe_l, page_table, w_ukv, g_kh):
    bd, t = q.shape[:2]
    scale = QK_DIM ** -0.5
    n_pages = page_table.shape[1]

    def page_step(carry, xs):
        m, l, acc = carry
        phys, j = xs
        kpos = j * PAGE_SIZE + jnp.arange(PAGE_SIZE)
        k, v = mla_keys_values(cache_ckv_l[phys], cache_kpe_l[phys], kpos, w_ukv, g_kh)
        sc = jnp.einsum('bthd,bkhd->bhtk', q, k).astype(jnp.float32) * scale
        m_new = jnp.maximum(m, sc.max(axis=-1))
        corr = jnp.exp(m - m_new)
        p = jnp.exp(sc - m_new[..., None])
        l = l * corr + p.sum(axis=-1)
        acc = acc * corr[..., None] + jnp.einsum('bhtk,bkhv->bhtv', p, v.astype(jnp.float32))
        return (m_new, l, acc), None

    init = (jnp.full((bd, MLA_HEADS, t), -jnp.inf, jnp.float32),
            jnp.zeros((bd, MLA_HEADS, t), jnp.float32),
            jnp.zeros((bd, MLA_HEADS, t, V_DIM), jnp.float32))
    (m, l, acc), _ = lax.scan(page_step, init, (page_table.T, jnp.arange(n_pages)))
    sc = jnp.einsum('bthd,bkhd->bhtk', q, k_new).astype(jnp.float32) * scale
    causal = jnp.tril(jnp.ones((t, t), dtype=bool))
    sc = jnp.where(causal, sc, -jnp.inf)
    m_new = jnp.maximum(m, sc.max(axis=-1))
    corr = jnp.exp(m - m_new)
    p = jnp.exp(sc - m_new[..., None])
    l = l * corr + p.sum(axis=-1)
    acc = acc * corr[..., None] + jnp.einsum('bhtk,bkhv->bhtv', p, v_new.astype(jnp.float32))
    o = acc / l[..., None]
    return o.transpose(0, 2, 1, 3).reshape(bd, t, MLA_HEADS * V_DIM).astype(q.dtype)

def gla_recurrence(q, k, v, lg, s0):
    bt, l = q.shape[:2]
    c = GLA_CHUNK if l % GLA_CHUNK == 0 else l
    n = l // c

    def chunks(a):
        return a.reshape(bt, n, c, *a.shape[2:]).swapaxes(0, 1)

    causal = jnp.tril(jnp.ones((c, c), dtype=bool))[None, :, :, None, None]

    def step(s, inp):
        qc, kc, vc, gc = inp
        b = jnp.cumsum(gc, axis=1)
        inter = jnp.einsum('bthk,bhkv->bthv', qc * jnp.exp(b), s)
        decay = jnp.exp(jnp.where(causal, b[:, :, None] - b[:, None, :], -jnp.inf))
        att = jnp.einsum('btshk,bshk->bhts', qc[:, :, None] * decay, kc)
        o = inter + jnp.einsum('bhts,bshv->bthv', att, vc)
        bl = b[:, -1]
        s = jnp.exp(bl)[..., None] * s + jnp.einsum('bshk,bshv->bhkv', kc * jnp.exp(bl[:, None] - b), vc)
        return s, o

    s, o = lax.scan(step, s0, (chunks(q), chunks(k), chunks(v), chunks(lg)))
    return o.swapaxes(0, 1).reshape(bt, l, GLA_HEADS, GLA_DV), s

def ab_mixer(n, pos, s0, past, w_in, g_qlat, w_uq, g_kvlat, w_ukv, g_qh, g_kh, w_a2, b_a, g_o, w_out):
    f32 = jnp.float32
    bt, l, _ = n.shape
    z = jnp.einsum('bld,dz->blz', n, w_in)
    idx = [int(i) for i in np.cumsum(IN_SPLITS)[:-1]]
    c_q, c_kv, k_pe, gq, gk, gv, ga, gr = jnp.split(z, idx, axis=-1)
    q = mla_queries(c_q, pos, g_qlat, w_uq, g_qh)
    c_kv = rmsnorm(c_kv, g_kvlat)
    k, v = mla_keys_values(c_kv, k_pe, pos, w_ukv, g_kh)
    if past is None:
        attn = mla_prompt_attention(q, k, v)
    else:
        cache_ckv_l, cache_kpe_l, page_table = past
        attn = mla_sample_attention(q, k, v, cache_ckv_l, cache_kpe_l, page_table, w_ukv, g_kh)
    gq = gq.reshape(bt, l, GLA_HEADS, GLA_DK).astype(f32) * (GLA_DK ** -0.5)
    gk = gk.reshape(bt, l, GLA_HEADS, GLA_DK).astype(f32)
    gv = gv.reshape(bt, l, GLA_HEADS, GLA_DV).astype(f32)
    logit = (jnp.einsum('blr,rz->blz', ga, w_a2) + b_a).astype(f32)
    lg = jax.nn.log_sigmoid(logit).reshape(bt, l, GLA_HEADS, GLA_DK) / GLA_TAU
    o, s = gla_recurrence(gq, gk, gv, lg, s0.astype(f32))
    o = rmsnorm(o, g_o).astype(n.dtype).reshape(bt, l, GLA_HEADS * GLA_DV) * jax.nn.silu(gr)
    y = jnp.einsum('blz,zd->bld', jnp.concatenate([attn, o], axis=-1), w_out)
    return y, c_kv, k_pe, s.astype(s0.dtype)

def s5_combine(e1, e2):
    a1r, a1i, b1r, b1i = e1
    a2r, a2i, b2r, b2i = e2
    return (a2r * a1r - a2i * a1i, a2r * a1i + a2i * a1r,
            a2r * b1r - a2i * b1i + b2r, a2r * b1i + a2i * b1r + b2i)

def s5_mixer(n, x0_re, x0_im, a_re, a_im, log_dt, b_re, b_im, c_re, c_im, d, w_glu):
    f32 = jnp.float32
    bt, l, _ = n.shape
    u = n.astype(f32).reshape(bt, l, S5_GROUPS, S5_GROUP)
    a_re = a_re.astype(f32)
    a_im = a_im.astype(f32)
    dt = jnp.exp(log_dt.astype(f32))[:, None]
    mag = jnp.exp(a_re * dt)
    lr = mag * jnp.cos(a_im * dt)
    li = mag * jnp.sin(a_im * dt)
    den = a_re * a_re + a_im * a_im
    cr = ((lr - 1.0) * a_re + li * a_im) / den
    ci = (li * a_re - (lr - 1.0) * a_im) / den
    b_re = b_re.astype(f32)
    b_im = b_im.astype(f32)
    bbr = cr[..., None] * b_re - ci[..., None] * b_im
    bbi = cr[..., None] * b_im + ci[..., None] * b_re
    bur = jnp.einsum('blgc,gpc->lbgp', u, bbr)
    bui = jnp.einsum('blgc,gpc->lbgp', u, bbi)
    x0r = x0_re.astype(f32)
    x0i = x0_im.astype(f32)
    bur = bur.at[0].add(lr * x0r - li * x0i)
    bui = bui.at[0].add(lr * x0i + li * x0r)
    ar = jnp.broadcast_to(lr, (l, 1, S5_GROUPS, S5_STATE))
    ai = jnp.broadcast_to(li, (l, 1, S5_GROUPS, S5_STATE))
    _, _, xr, xi = lax.associative_scan(s5_combine, (ar, ai, bur, bui), axis=0)
    y = (jnp.einsum('lbgp,gcp->blgc', xr, c_re.astype(f32))
         - jnp.einsum('lbgp,gcp->blgc', xi, c_im.astype(f32)))
    y = y.reshape(bt, l, D_MODEL) + d.astype(f32) * n.astype(f32)
    g = jax.nn.gelu(y).astype(n.dtype)
    zg = jnp.einsum('bld,dz->blz', g, w_glu)
    out = zg[..., :D_MODEL] * jax.nn.sigmoid(zg[..., D_MODEL:])
    return out, xr[-1].astype(x0_re.dtype), xi[-1].astype(x0_im.dtype)

def channel_mixer(h, g, w_up, w_down):
    a = jax.nn.relu(jnp.einsum('bld,df->blf', rmsnorm(h, g), w_up))
    return jnp.einsum('blf,fd->bld', a * a, w_down)

def per_layer_embedding(h, p, g, w_gate, w_proj):
    gate = jax.nn.sigmoid(jnp.einsum('bld,de->ble', rmsnorm(h, g), w_gate))
    return gate * jnp.einsum('blr,rd->bld', p, w_proj)

def setup_inputs(seed: int = 0) -> dict:
    key = jax.random.key(seed)
    ks = iter(jax.random.split(key, 64))
    f32 = jnp.float32

    def nrm(shape, scale):
        return jax.random.normal(next(ks), shape, f32) * scale

    def gain(shape):
        return 1.0 + nrm(shape, 0.02)

    n_pages = PAST_LEN // PAGE_SIZE
    n_used = DEC_BATCH * n_pages
    n_pool = n_used + max(1, n_used // 4)
    page_table = jax.random.permutation(next(ks), n_pool)[:n_used].reshape(DEC_BATCH, n_pages).astype(jnp.int32)
    a_im = jnp.broadcast_to(math.pi * jnp.arange(S5_STATE, dtype=f32), (N_C, S5_GROUPS, S5_STATE))
    a_re = -0.5 * jnp.exp(nrm((N_C, S5_GROUPS, S5_STATE), 0.05))
    log_dt = jax.random.uniform(next(ks), (N_C, S5_GROUPS), f32, math.log(DT_MIN), math.log(DT_MAX))
    return {
        'x_prompt': nrm((BATCH, SEQ, D_MODEL), 1.0),
        'x_sample': nrm((DEC_BATCH, DEC_SEQ, D_MODEL), 1.0),
        'cache_ckv': nrm((N_AB, n_pool, PAGE_SIZE, KV_LORA), 1.0),
        'cache_kpe': nrm((N_AB, n_pool, PAGE_SIZE, ROPE_DIM), 1.0),
        'state_gla': nrm((N_AB, DEC_BATCH, GLA_HEADS, GLA_DK, GLA_DV), 0.1),
        'state_s5_re': nrm((N_C, DEC_BATCH, S5_GROUPS, S5_STATE), 0.1),
        'state_s5_im': nrm((N_C, DEC_BATCH, S5_GROUPS, S5_STATE), 0.1),
        'page_table': page_table,
        'p_prompt': nrm((DEPTH, BATCH, SEQ, PLE_DIM), 1.0),
        'p_sample': nrm((DEPTH, DEC_BATCH, DEC_SEQ, PLE_DIM), 1.0),
        'g_norm_ab': gain((N_AB, D_MODEL)),
        'w_in_ab': nrm((N_AB, D_MODEL, IN_AB), D_MODEL ** -0.5),
        'g_qlat': gain((N_AB, Q_LORA)),
        'w_uq': nrm((N_AB, Q_LORA, MLA_HEADS * QK_DIM), Q_LORA ** -0.5),
        'g_kvlat': gain((N_AB, KV_LORA)),
        'w_ukv': nrm((N_AB, KV_LORA, MLA_HEADS * (NOPE_DIM + V_DIM)), KV_LORA ** -0.5),
        'g_qh': gain((N_AB, QK_DIM)),
        'g_kh': gain((N_AB, QK_DIM)),
        'w_gla_a2': nrm((N_AB, GLA_GATE_RANK, GLA_HEADS * GLA_DK), GLA_GATE_RANK ** -0.5),
        'b_gla_a': nrm((N_AB, GLA_HEADS * GLA_DK), 0.1),
        'g_gla_o': gain((N_AB, GLA_DV)),
        'w_out_ab': nrm((N_AB, MIX_AB, D_MODEL), MIX_AB ** -0.5),
        'g_norm_c': gain((N_C, D_MODEL)),
        's5_a_re': a_re,
        's5_a_im': a_im,
        's5_log_dt': log_dt,
        's5_b_re': nrm((N_C, S5_GROUPS, S5_STATE, S5_GROUP), (2 * S5_GROUP) ** -0.5),
        's5_b_im': nrm((N_C, S5_GROUPS, S5_STATE, S5_GROUP), (2 * S5_GROUP) ** -0.5),
        's5_c_re': nrm((N_C, S5_GROUPS, S5_GROUP, S5_STATE), S5_STATE ** -0.5),
        's5_c_im': nrm((N_C, S5_GROUPS, S5_GROUP, S5_STATE), S5_STATE ** -0.5),
        's5_d': nrm((N_C, D_MODEL), 1.0),
        'w_glu': nrm((N_C, D_MODEL, 2 * D_MODEL), D_MODEL ** -0.5),
        'g_norm_mlp': gain((DEPTH, D_MODEL)),
        'w_up': nrm((DEPTH, D_MODEL, D_FF), D_MODEL ** -0.5),
        'w_down': nrm((DEPTH, D_FF, D_MODEL), D_FF ** -0.5),
        'g_norm_ple': gain((DEPTH, D_MODEL)),
        'w_ple_gate': nrm((DEPTH, D_MODEL, D_MODEL), D_MODEL ** -0.5),
        'w_ple_proj': nrm((DEPTH, PLE_DIM, D_MODEL), PLE_DIM ** -0.5),
    }

def reference(x_prompt, x_sample, cache_ckv, cache_kpe, state_gla, state_s5_re, state_s5_im, page_table,
              p_prompt, p_sample, g_norm_ab, w_in_ab, g_qlat, w_uq, g_kvlat, w_ukv, g_qh, g_kh,
              w_gla_a2, b_gla_a, g_gla_o, w_out_ab, g_norm_c, s5_a_re, s5_a_im, s5_log_dt,
              s5_b_re, s5_b_im, s5_c_re, s5_c_im, s5_d, w_glu, g_norm_mlp, w_up, w_down,
              g_norm_ple, w_ple_gate, w_ple_proj):
    lp = x_prompt.shape[1]
    t = x_sample.shape[1]
    past_len = page_table.shape[1] * PAGE_SIZE
    pos_p = jnp.arange(lp)
    pos_s = past_len + jnp.arange(t)
    hp, hs = x_prompt, x_sample
    ckv_p, kpe_p, gla_p, s5r_p, s5i_p = [], [], [], [], []
    ckv_s, kpe_s, gla_s, s5r_s, s5i_s = [], [], [], [], []
    for i in range(DEPTH):
        j = i // 2
        if i % 2 == 0:
            wts = (w_in_ab[j], g_qlat[j], w_uq[j], g_kvlat[j], w_ukv[j], g_qh[j], g_kh[j],
                   w_gla_a2[j], b_gla_a[j], g_gla_o[j], w_out_ab[j])
            s0 = jnp.zeros((hp.shape[0], GLA_HEADS, GLA_DK, GLA_DV), state_gla.dtype)
            mp, c1, c2, c3 = ab_mixer(rmsnorm(hp, g_norm_ab[j]), pos_p, s0, None, *wts)
            ms, d1, d2, d3 = ab_mixer(rmsnorm(hs, g_norm_ab[j]), pos_s, state_gla[j],
                                      (cache_ckv[j], cache_kpe[j], page_table), *wts)
            ckv_p.append(c1)
            kpe_p.append(c2)
            gla_p.append(c3)
            ckv_s.append(d1)
            kpe_s.append(d2)
            gla_s.append(d3)
        else:
            wts = (s5_a_re[j], s5_a_im[j], s5_log_dt[j], s5_b_re[j], s5_b_im[j],
                   s5_c_re[j], s5_c_im[j], s5_d[j], w_glu[j])
            z0 = jnp.zeros((hp.shape[0], S5_GROUPS, S5_STATE), state_s5_re.dtype)
            mp, c1, c2 = s5_mixer(rmsnorm(hp, g_norm_c[j]), z0, z0, *wts)
            ms, d1, d2 = s5_mixer(rmsnorm(hs, g_norm_c[j]), state_s5_re[j], state_s5_im[j], *wts)
            s5r_p.append(c1)
            s5i_p.append(c2)
            s5r_s.append(d1)
            s5i_s.append(d2)
        hp = hp + mp
        hs = hs + ms
        hp = hp + channel_mixer(hp, g_norm_mlp[i], w_up[i], w_down[i])
        hs = hs + channel_mixer(hs, g_norm_mlp[i], w_up[i], w_down[i])
        hp = hp + per_layer_embedding(hp, p_prompt[i], g_norm_ple[i], w_ple_gate[i], w_ple_proj[i])
        hs = hs + per_layer_embedding(hs, p_sample[i], g_norm_ple[i], w_ple_gate[i], w_ple_proj[i])
    y_prompt, y_sample = hp, hs
    ckv_prompt, kpe_prompt, gla_prompt = jnp.stack(ckv_p), jnp.stack(kpe_p), jnp.stack(gla_p)
    s5re_prompt, s5im_prompt = jnp.stack(s5r_p), jnp.stack(s5i_p)
    ckv_sample, kpe_sample, gla_sample = jnp.stack(ckv_s), jnp.stack(kpe_s), jnp.stack(gla_s)
    s5re_sample, s5im_sample = jnp.stack(s5r_s), jnp.stack(s5i_s)
    return (y_prompt, y_sample, ckv_prompt, kpe_prompt, gla_prompt, s5re_prompt, s5im_prompt,
            ckv_sample, kpe_sample, gla_sample, s5re_sample, s5im_sample)


_drawn_inputs = setup_inputs


def setup_inputs(seed=0):
    import zlib

    import numpy as np

    out = dict(_drawn_inputs(seed))
    spreads = {}
    factors = {'cache_kpe': 3.093,
     'g_qlat': 8.0,
     'g_kvlat': 2.743,
     'g_qh': 8.0,
     'g_kh': 8.0,
     'g_gla_o': 7.999,
     'g_norm_c': 2.766,
     's5_c_re': 2.869,
     's5_c_im': 2.865,
     'g_norm_mlp': 2.694,
     'g_norm_ple': 8.0}
    for name, (base, spread) in spreads.items():
        noise = np.random.default_rng([zlib.crc32(name.encode()), seed]).standard_normal(out[name].shape)
        drawn = base * np.exp(spread * noise) if base else spread * noise
        out[name] = __import__('jax').numpy.asarray(drawn.astype(out[name].dtype))
    for name, factor in factors.items():
        out[name] = (out[name] * factor).astype(out[name].dtype)
    return out
```

```python
from contextlib import ExitStack

import numpy as np

import concourse.bass as bass
from concourse import mybir

F32 = mybir.dt.float32
I32 = mybir.dt.int32
ALU = mybir.AluOpType
ACT = mybir.ActivationFunctionType
AX = mybir.AxisListType

P = 128
D, DB = 1024, 8
TP, NS, TS = 256, 8, 4
TN = NS * TS
T = TP + TN
H, NOPE, ROPE, VD = 8, 64, 32, 64
QK = NOPE + ROPE
QB, KB = 3, 2
PAGE, NPG, POOL = 128, 8, 80
NG = NS * NPG // 4
GH, GD, GC = 4, 128, 64
NCH = TP // GC
FB = 32
SB = 32
J = TP // TS + NS
JP = TP // TS
EPS = 1e-6
SCALE = float(QK) ** -0.5
RING = 5
UNIT = 2048
NEG = -1e30

UNITS = (["cq01", "cq2kv0", "kv1x"] + ["gq0", "gq1", "gk0", "gk1", "gv0", "gv1", "gr0", "gr1"]
         + [f"out{i}" for i in range(4)]
         + [f"up0_{i}" for i in range(16)] + [f"down0_{i}" for i in range(16)] + ["proj0"] + [f"gate0_{i}" for i in range(4)]
         + [f"glu{i}" for i in range(8)]
         + [f"up1_{i}" for i in range(16)] + [f"down1_{i}" for i in range(16)] + ["proj1"] + [f"gate1_{i}" for i in range(4)])
U = {n: i for i, n in enumerate(UNITS)}


def lay(sizes):
    at, out = 0, {}
    for name, n in sizes:
        out[name] = (at, n)
        at += n
    return out, at


CONST, NCONST = lay([("ident", 128), ("tri", 128), ("tri4", 32), ("causal", 384), ("newmask", 32),
                     ("perm", 128), ("cosN", T), ("sinN", T), ("cosC", 256), ("sinC", 256), ("head2", 2), ("page4", 4),
                     ("seqmask", 8)])
PARAM, NPARAM = lay([("g_ab", 8), ("g_mlp0", 8), ("g_ple0", 8), ("g_c", 8), ("g_mlp1", 8), ("g_ple1", 8),
                     ("g_qlat", 3), ("g_kvlat", 2), ("g_qh", 1), ("g_kh", 1), ("g_kpe", 1), ("g_o", 1),
                     ("s5_d", 32), ("a_re", 32), ("a_im", 32), ("log_dt", 32)])

AB, NAB = lay([("wuq", QB * H * QK), ("wuk", KB * 512), ("wuv", KB * 512), ("cqn", QB * T), ("ckvn", KB * T),
               ("qh", H * T), ("kh", H * T), ("gq", GH * T), ("gk", GH * T), ("gr", GH * T), ("gv", 3 * 512),
               ("S", NPG * NS * 32), ("kT", 4096), ("ksq", 4096), ("pages", 2048), ("kpe", NG * PAGE),
               ("qbd", NS * 4 * 8), ("qpe", NS * 4 * 32), ("ga", T), ("kpen", T), ("ctok", 256), ("snew", 256), ("kpss", 64), ("stat", 64)])
S5A, NS5 = lay([("Bre", SB * 128), ("Bim", SB * 128), ("Cre", SB * 5 * 32), ("Cim", SB * 5 * 32), ("toep", SB * 128),
                ("a2", FB * T), ("coef", 20 * 32)])
NARENA = max(NAB, NS5)


class Groups:

    def __init__(self):
        self.of = {}
        self.order = {"main": 0, "side": 0}
        self.freed = [0] * 8

    def add(self, name, kind, readers=1):
        n = self.order[kind]
        bank = n % 4 + (4 if kind == "side" else 0)
        self.of[name] = (kind, bank, n + 1, self.freed[bank], readers)
        self.order[kind] += 1
        self.freed[bank] += readers


def plan():
    g = Groups()
    side = lambda name, r=1: g.add(name, "side", r)
    main = lambda name, r=1: g.add(name, "main", r)
    side(("ss", 0))
    for n in ("cq0", "cq1", "cq2"):
        main(n, 2)
    main("ckv0", 2)
    main("ckv1", 2)
    main("kpe")
    main("ga")
    side("cqss")
    side("ckvss")
    for n in ("gq", "gk"):
        for i in range(4):
            main((n, i))
    for u in range(2):
        for tt in range(3):
            main(("gv", u, tt))
    for i in range(4):
        main(("gr", i), 2)
    for h in range(H):
        main(("q", h), 2)
    for h in range(H):
        main(("k", h), 2)
    for h in range(H):
        side(("qss", h))
        side(("qrot", h))
    side("krot")
    for h in range(H):
        side(("kss", h))
    for tt in range(2):
        main(("v", tt))
    side("ctok")
    side("snew", H)
    for h in range(H):
        main(("att", h))
        side(("attT", h))
        if h % 2:
            main(("atto", h // 2))
    for tt in range(3):
        main(("lg", tt), 2)
    for h in range(GH):
        main(("b", h))
    for h in range(GH):
        side(("ktok", h), 2)
        side(("gatt", h), 2)
    for h in range(GH):
        side(("gs", h, 0), 2)
        side(("gs", h, 1), 2)
    for h in range(GH):
        main(("go", h), 2)
        side(("oss", h))
        side(("su", h, 0))
        side(("su", h, 1))
    main("kpss")
    for c in range(4):
        main(("krotc", c))
    for i in range(NG):
        for blk in range(4):
            main(("ke", i, blk), 2)
        side(("sc", i), 4)
    side("mT0")
    side("mT1")
    side("mB", 2)
    side("l")
    main("ol0")
    main("ol1")
    side("oa")
    for i in range(8):
        main(("out", i))
    for L in range(2):
        if L == 1:
            side(("ss", 3))
            for i in range(16):
                main(("v5", i))
            for i in range(8):
                main(("y5", i))
            for i in range(8):
                main(("glu_a", i))
                main(("glu_g", i))
        side(("ss", 1 + 3 * L))
        for i in range(FB):
            main(("up", L, i), 2)
        if L == 0:
            for i in range(8):
                side(("G", i), 4)
            for i in range(16):
                side(("BT", i))
        for i in range(8):
            main(("down", L, i))
        side(("ss", 2 + 3 * L))
        for i in range(8):
            main(("proj", L, i))
            main(("gate", L, i), 1)
    return g


def program(nc, ins, outs):
    g = plan()
    ctx = ExitStack()
    with ctx:
        sb = lambda name, n, dt=F32: ctx.enter_context(nc.sbuf_tensor(name, [P, n], dt))
        sem = lambda name: ctx.enter_context(nc.semaphore(name))

        ring = [sb(f"ring{i}", UNIT) for i in range(RING)]
        hT = sb("hT", DB * T)
        nT = sb("nT", DB * T)
        sq = sb("sq", 4 * T)
        rs = sb("rs", T)
        const = sb("const", NCONST)
        par = sb("par", NPARAM)
        ones = sb("ones", 4 * P)
        pT = sb("pT", 2 * T)
        eps = sb("eps", 1)
        table = sb("table", NS * NPG, I32)
        arena = sb("arena", NARENA)
        tmp = sb("tmp", 600)
        PS = [ctx.enter_context(nc.psum_tensor(f"ps{i}", [P, 512], F32)) for i in range(8)]

        def view(buf, offset, size, **shape):
            v = buf[:, offset:offset + size]
            if shape:
                keys = list(shape)
                v = v.rearrange("p (" + " ".join(keys) + ") -> p " + " ".join(keys), **{k: shape[k] for k in keys})
            return v

        ab = lambda name, **s: view(arena, *AB[name], **s)
        s5 = lambda name, **s: view(arena, *S5A[name], **s)
        cst = lambda name, **s: view(const, *CONST[name], **s)
        prm = lambda name, **s: view(par, *PARAM[name], **s)
        bc = lambda ap, shape: ap.broadcast_to(shape)

        h3 = view(hT, 0, DB * T, b=DB, t=T)
        n3 = view(nT, 0, DB * T, b=DB, t=T)
        sq3 = view(sq, 0, 4 * T, b=4, t=T)
        o1024, o96, o128, o1 = (ones[:, i * P:(i + 1) * P] for i in range(4))
        p3 = view(pT, 0, 2 * T, b=2, t=T)
        tA = tmp[:, 0:T]
        tB = tmp[:, T:2 * T]

        wuq = ab("wuq", k=QB, n=H * QK)
        wuk = ab("wuk", k=KB, n=512)
        wuv = ab("wuv", k=KB, n=512)
        cqn = ab("cqn", b=QB, t=T)
        ckvn = ab("ckvn", b=KB, t=T)
        qh = ab("qh", h=H, t=T)
        kh = ab("kh", h=H, t=T)
        gq = ab("gq", h=GH, t=T)
        gk = ab("gk", h=GH, t=T)
        gr = ab("gr", h=GH, t=T)
        gv = ab("gv", t=3, n=512)
        S = ab("S", k=NPG, b=NS, c=32)
        kT = ab("kT", s=2, b=4, k=512)
        ksq = ab("ksq", s=2, b=4, k=512)
        pages = ab("pages", s=2, j=4, k=KB, n=PAGE)
        cpages = ab("ksq", s=16, n=256)
        kpe = ab("kpe", g=NG, k=PAGE)
        qbd = ab("qbd", b=NS, k=4, c=8)
        ga = ab("ga")
        kpen = ab("kpen")
        ctok = ab("ctok", k=KB, n=P)
        snew = ab("snew", b=NS, h=H, t=TS)
        kpss = ab("kpss", g=NG, j=4)
        stat = ab("stat")
        kto, kso, pgo, So = AB["kT"][0], AB["ksq"][0], AB["pages"][0], AB["S"][0]
        sq96 = view(arena, kto, H * T, h=H, t=T)
        r96 = view(arena, kto + H * T, H * T, h=H, t=T)
        sq96k = view(arena, kto + 2 * H * T, H * T, h=H, t=T)
        sqlat = view(arena, kto, 5 * T, b=5, t=T)
        vtok = view(arena, pgo, 1024, t=2, n=512)
        patt = view(arena, kto, 2 * 384, s=2, n=384)
        pTt = view(arena, kto + 768, 2 * 384, s=2, n=384)
        at = kto

        def gtemp(size, **s):
            nonlocal at
            v = view(arena, at, size, **s)
            at += size
            return v

        lgs = gtemp(3 * 512, t=3, n=512)
        lgmin = view(arena, at, 3 * 512, t=3, n=512)
        bT = gtemp(GH * T, h=GH, t=T)
        dT = gtemp(GH * T, h=GH, t=T)
        qt = gtemp(GH * T, h=GH, t=T)
        kt = gtemp(GH * T, h=GH, t=T)
        qb = gtemp(GH * T, h=GH, t=T)
        kd = gtemp(GH * T, h=GH, t=T)
        ktok = gtemp(GH * 384, h=GH, n=384)
        attm = view(arena, So, GH * TP, h=GH, n=TP)
        attms = view(arena, AB["qh"][0] + 2048, GH * TN, h=GH, n=TN)
        assert at <= AB["kpe"][0], at
        st = view(arena, AB["qh"][0], GH * 512, h=GH, c=4, v=GD)
        s0 = [view(arena, AB["kh"][0], 1024, b=NS, v=GD), view(arena, AB["kh"][0] + 1024, 1024, b=NS, v=GD)]
        vmask = view(arena, So + GH * TP, 1024, b=NS, v=GD)
        ebl = view(arena, AB["wuq"][0], GH * T, h=GH, t=T)
        ogt = view(arena, AB["wuq"][0] + GH * T, GH * T, h=GH, t=T)
        qpe = ab("qpe", b=NS, j=4, c=32)
        mx = view(arena, pgo, 256)
        diag = view(arena, pgo + 256, 256)
        rl = view(arena, AB["qh"][0] + 1280, 256, b=NS, h=H, t=TS)
        olat = view(arena, AB["qh"][0] + 1536, 512, k=KB, h=H, b=NS, t=TS)
        lin = view(arena, AB["kh"][0], 1024)
        mix = n3
        Bre, Bim = s5("Bre", s=SB, i=4, c=32), s5("Bim", s=SB, i=4, c=32)
        Cre, Cim = s5("Cre", s=SB, i=5, c=32), s5("Cim", s=SB, i=5, c=32)
        toep = s5("toep", s=SB, i=4, c=32)
        a2 = s5("a2", f=FB, t=T)
        to0, a20, b0 = S5A["toep"][0], S5A["a2"][0], S5A["Bre"][0]
        braw = [view(arena, to0 + 512 * i, 512, s=SB, c=16) for i in range(2)]
        craw = [view(arena, to0 + 1024 + 512 * i, 512, s=SB, c=16) for i in range(2)]
        cur = [view(arena, to0 + 2048 + 512 * i, 512, s=SB, c=16) for i in range(2)]
        t16 = [view(arena, to0 + 3072 + 512 * i, 512, s=SB, c=16) for i in range(2)]
        vb = view(arena, a20, J * 64, j=J, r=2, s=SB)
        ustk = view(arena, a20 + J * 64, SB * J, s=SB, j=J)
        X = view(arena, b0, 2 * SB * J, r=2, s=SB, j=J)
        coef = s5("coef")
        cf = lambda i: coef[:, 32 * i:32 * (i + 1)]
        xs0 = a20 + J * 64 + SB * J
        fin0 = xs0 + 512 + 1024
        prod = view(arena, fin0 + 64, 128, o=2, r=2, s=SB)
        fin = view(arena, fin0, 64, r=2, s=SB)
        part = view(arena, fin0 + 192, 64, r=2, s=SB)
        xs = view(arena, a20 + J * 64 + SB * J, 512, r=2, s=SB, b=NS)
        xt = view(arena, a20 + J * 64 + SB * J + 512, 1024, o=2, r=2, s=SB, b=NS)

        def sems(names):
            return [sem(n) for n in names.split()]

        (const_in, params_in, x_in, w_in, lin_in, p_in0, p_in1, kpe_in, table_in, s5raw_in, x0_in, stack_in,
         unstack_in, out_done) = sems("const_in params_in x_in w_in lin_in p_in0 p_in1 kpe_in table_in s5raw_in x0_in "
                                      "stack_in unstack_in out_done")
        main_ready, side_ready, sumsq_step, atto_half, cpage_used = sems("main_ready side_ready sumsq_step atto_half cpage_used")
        dve_step, act_step = sems("dve_step act_step")
        (ones_set, qbd_zero, s5_zero, toep_zero, sq_ready, n_ready, cqn_ready, ckvn_ready, kpeg_ready, kpe_squared, kper_ready, qh_ready, kh_ready,
         qbd_ready, qpe_ready, negmax_ready, p_exp, p_ready, softplus_ready, lg_ready, diff_ready, decay_ready, gla_ready,
         vmask_ready, gmix_ready, ckpe_squared, ckpe_scaled, ckpe_ready, m_ready, diag_ready, p_all, states_ready, ksum_ready, kfactor_ready,
         gate_exp, h_gated, s5_exp, s5_sin, s5_lambda, s5_angle, b_power, c_power, b_copied, c_copied, pow_done, x_start, scan_ready,
         y_ready, gelu_ready, final_ready, cpow_used) = sems(
            "ones_set qbd_zero s5_zero toep_zero sq_ready n_ready cqn_ready ckvn_ready kpeg_ready kpe_squared kper_ready qh_ready kh_ready "
            "qbd_ready qpe_ready negmax_ready p_exp p_ready softplus_ready lg_ready diff_ready decay_ready gla_ready "
            "vmask_ready gmix_ready ckpe_squared ckpe_scaled ckpe_ready m_ready diag_ready p_all states_ready ksum_ready kfactor_ready "
            "gate_exp h_gated s5_exp s5_sin s5_lambda s5_angle b_power c_power b_copied c_copied pow_done x_start scan_ready "
            "y_ready gelu_ready final_ready cpow_used")
        unit_in = [sem(f"unit_in{i}") for i in range(RING)]
        s0_in = [sem(f"s0_in{i}") for i in range(2)]
        s0_out = [sem(f"s0_out{i}") for i in range(2)]
        page_in = [sem(f"page_in{i}") for i in range(2)]
        cpage_in = [sem(f"cpage_in{i}") for i in range(16)]
        evacuated = [sem(f"evacuated{i}") for i in range(8)]

        block = ctx.enter_context(nc.Block())

        def result(eng, name):
            kind, bank, n = g.of[name][:3]
            eng.wait_ge(main_ready if kind == "main" else side_ready, n)
            return PS[bank]

        def bank_of(name):
            return evacuated[g.of[name][1]]

        def copied(eng, name, n=None):
            _, bank, _, before, readers = g.of[name]
            eng.wait_ge(evacuated[bank], before + (readers if n is None else n))

        def unit_done(u):
            n = UNITS[u]
            last = {"cq01": "cq1", "cq2kv0": "ckv0", "kv1x": "ga"}.get(n)
            if last is None:
                if n[:2] in ("gq", "gk", "gr"):
                    last = (n[:2], 2 * int(n[2]) + 1)
                elif n[:2] == "gv":
                    last = ("gv", int(n[2]), 2)
                elif n[:3] == "out":
                    last = ("out", 2 * int(n[3:]) + 1)
                elif n[:2] == "up":
                    last = ("up", int(n[2]), 2 * int(n[4:]) + 1)
                elif n[:4] == "down":
                    last = ("down", int(n[4]), int(n[6:]) // 2)
                elif n[:4] == "proj":
                    last = ("proj", int(n[4]), 7)
                elif n[:4] == "gate":
                    last = ("gate", int(n[4]), 2 * int(n[6:]) + 1)
                else:
                    last = ("glu_g", int(n[3:]))
            return g.of[last][2]

        @block.sync
        def _(sp):
            sp.dma_start(const[:, :], ins["const"]).then_inc(const_in, 16)
            sp.dma_start(par[:, :], ins["param"]).then_inc(params_in, 16)
            sp.dma_start(hT[:, :], ins["x"]).then_inc(x_in, 16)
            for u in range(len(UNITS)):
                if u >= RING:
                    sp.wait_ge(main_ready, unit_done(u - RING))
                sp.dma_start(ring[u % RING][:, :], ins["stream"][u]).then_inc(unit_in[u % RING], 16)

        @block.gpsimd
        def _(pool):
            for i, v in enumerate((1.0 / 1024, 1.0 / 96, 1.0 / 128, 1.0)):
                pool.memset(ones[:, i * P:(i + 1) * P], v).then_inc(ones_set, 1)
            pool.memset(eps[:, :], EPS).then_inc(ones_set, 1)
            pool.memset(ab("qbd"), 0.0).then_inc(qbd_zero, 1)
            pool.memset(ab("qpe"), 0.0).then_inc(qbd_zero, 1)
            pool.dma_start(table[0:1, :], ins["table"]).then_inc(table_in, 16)
            pool.dma_start(arena[:, 0:AB["cqn"][0]], ins["wu"]).then_inc(w_in, 16)
            pool.dma_start(pT[:, :], ins["p"][0]).then_inc(p_in0, 16)
            pool.wait_ge(table_in, 16)

            def page(b, k):
                return pool.value_load(table[0:1, b * NPG + k:b * NPG + k + 1], min_val=0, max_val=POOL - 1)

            for i in range(NG):
                for j in range(4):
                    pg = page(i // 2, 4 * (i % 2) + j)
                    pool.dma_start(kpe[32 * j:32 * j + 32, i, :], ins["kpeT"][bass.ds(pg, 1)].rearrange("o p k -> (o p) k")).then_inc(kpe_in, 16)
            pool.wait_ge(ckvn_ready, 1)
            pool.dma_start(outs["ckv"], ab("ckvn")).then_inc(out_done, 16)
            copied(pool, "kpe")
            pool.dma_start(outs["kpe"], kpen[64:96, :]).then_inc(out_done, 16)
            pool.wait_ge(main_ready, g.of[("att", H - 1)][2])
            pool.wait_ge(qpe_ready, 4)
            pool.dma_start(lin[0:16, 0:512], ins["wa2"]).then_inc(lin_in, 16)
            pool.dma_start(lin[0:1, 512:1024], ins["ba"]).then_inc(lin_in, 16)
            pool.wait_ge(main_ready, g.of[("lg", 2)][2])
            for h in range(GH + 1):
                if h >= 2:
                    copied(pool, ("su", h - 2, 0))
                    copied(pool, ("su", h - 2, 1))
                    pool.dma_start(outs["gla_s"][h - 2], s0[h % 2].rearrange("p b v -> p (b v)")).then_inc(s0_out[h % 2], 16)
                if h < GH:
                    if h >= 2:
                        pool.wait_ge(s0_out[h % 2], 16 * (h // 2))
                    pool.dma_start(s0[h % 2].rearrange("p b v -> p (b v)"), ins["s0"][h]).then_inc(s0_in[h % 2], 16)
            for h in range(GH):
                copied(pool, ("gs", h, 1))
            for h in range(GH):
                pool.dma_start(outs["gla_p"][h], st[:, h, 3]).then_inc(out_done, 16)
            copied(pool, ("su", GH - 1, 0))
            copied(pool, ("su", GH - 1, 1))
            pool.dma_start(outs["gla_s"][GH - 1], s0[(GH - 1) % 2].rearrange("p b v -> p (b v)")).then_inc(s0_out[(GH - 1) % 2], 16)
            pool.wait_ge(gmix_ready, GH)
            for i in range(NG):
                if i >= 2:
                    pool.wait_ge(main_ready, g.of[("ke", i - 2, 3)][2])
                for j in range(4):
                    pg = page(i // 2, 4 * (i % 2) + j)
                    pool.dma_start(pages[:, i % 2, j].rearrange("p k n -> p (k n)"), ins["ckvT"][bass.ds(pg, 1)].rearrange("o p n -> (o p) n")).then_inc(page_in[i % 2], 16)
            pool.wait_ge(side_ready, g.of[("sc", NG - 1)][2])
            for n in range(NS * NPG):
                if n >= 16:
                    pool.wait_ge(cpage_used, n - 15)
                pg = page(n // NPG, n % NPG)
                pool.dma_start(cpages[:, n % 16], ins["ckv"][bass.ds(pg, 1)].rearrange("o p n -> (o p) n")).then_inc(cpage_in[n % 16], 16)
            copied(pool, "oa")
            pool.wait_ge(out_done, 16 * (2 + GH))
            for i in range(2):
                pool.wait_ge(s0_out[i], 16 * GH // 2)
            for i, n in enumerate(("b_re", "b_im")):
                pool.dma_start(arena[:, to0 + 512 * i:to0 + 512 * i + 512], ins[n]).then_inc(s5raw_in, 16)
            for i, n in enumerate(("c_re", "c_im")):
                pool.dma_start(arena[:, to0 + 1024 + 512 * i:to0 + 1536 + 512 * i], ins[n]).then_inc(s5raw_in, 16)
            pool.memset(arena[:, b0:to0], 0.0).then_inc(s5_zero, 1)
            pool.wait_ge(c_copied, 20)
            pool.memset(arena[:, to0:to0 + SB * 128], 0.0).then_inc(toep_zero, 1)
            pool.wait_ge(main_ready, g.of[("proj", 0, 7)][2])
            pool.dma_start(pT[:, :], ins["p"][1]).then_inc(p_in1, 16)
            pool.wait_ge(n_ready, 32)
            for i in range(4):
                for q in range(4):
                    pool.dma_start(ustk[32 * i:32 * i + 32].rearrange("p (b q) j -> p b q j", q=4)[:, :, q],
                                   n3[32 * q:32 * q + 32, :, i * J:(i + 1) * J]).then_inc(stack_in, 16)
            pool.wait_ge(main_ready, g.of[("v5", 15)][2])
            for r in range(2):
                pool.dma_start(X[:, r, :, JP:J], ins["x0"][r].rearrange("p (s b) -> p s b", b=NS)).then_inc(x0_in, 16)
            pool.wait_ge(gelu_ready, 8)
            for i in range(4):
                for q in range(4):
                    pool.dma_start(n3[32 * q:32 * q + 32, :, i * J:(i + 1) * J],
                                   ustk[32 * i:32 * i + 32].rearrange("p (b q) j -> p b q j", q=4)[:, :, q]).then_inc(unstack_in, 16)
            pool.wait_ge(states_ready, 2)
            pool.dma_start(outs["s5_p"], arena[:, fin0:fin0 + 64]).then_inc(out_done, 16)
            pool.dma_start(outs["s5_s"], arena[:, xs0:xs0 + 512]).then_inc(out_done, 16)
            pool.wait_ge(h_gated, 24)
            pool.dma_start(outs["y"], hT[:, :]).then_inc(out_done, 16)
            pool.wait_ge(out_done, 16 * (2 + GH + 2 + 1))

        @block.tensor
        def _(pe):
            def bank(name):
                _, b, _, before, _ = g.of[name]
                if before:
                    pe.wait_ge(evacuated[b], before)
                return PS[b]

            def ready(ins, name):
                ins.then_inc(main_ready if g.of[name][0] == "main" else side_ready, 1)

            def unit(name):
                u = U[name]
                pe.wait_ge(unit_in[u % RING], 16 * (u // RING + 1))
                return ring[u % RING]

            def sumsq(k):
                ps = bank(("ss", k))
                for b in range(DB):
                    pe.wait_ge(sq_ready, 8 * k + b + 1)
                    mm = pe.matmul(ps[:, 0:T], o1024, sq3[:, b % 4], start=b == 0, stop=b == DB - 1)
                    if b == DB - 1:
                        ready(mm, ("ss", k))
                    else:
                        mm.then_inc(sumsq_step, 1)

            def project(name, w, col, m, width, rhs, wait=None, base=0, off=0, blocks=DB, last=True, first=True):
                ps = bank(name) if first else PS[g.of[name][1]]
                wv = w[:, off:off + blocks * width].rearrange("p (k n) -> p k n", n=width)
                for k in range(blocks):
                    if wait:
                        wait(k)
                    mm = pe.matmul(ps[base:base + m, 0:T], wv[:, k, col:col + m], rhs(k), start=first and k == 0, stop=last and k == blocks - 1)
                if last:
                    ready(mm, name)

            nk = lambda k: n3[:, k]

            def norm_wait(k):
                return lambda b: pe.wait_ge(n_ready, 8 * k + b + 1)

            pe.wait_ge(ones_set, 4)
            sumsq(0)
            w = unit("cq01")
            project("cq0", w, 0, P, 256, nk, norm_wait(0))
            project("cq1", w, P, P, 256, nk)
            w = unit("cq2kv0")
            project("cq2", w, 0, P, 256, nk)
            project("ckv0", w, P, P, 256, nk)
            w = unit("kv1x")
            project("ckv1", w, 0, P, 176, nk)
            project("kpe", w, 128, 32, 176, nk, base=64)
            project("ga", w, 160, 16, 176, nk)
            for name, first, n in (("cqss", 0, QB), ("ckvss", QB, KB)):
                ps = bank(name)
                for i in range(n):
                    copied(pe, f"cq{i}" if first == 0 else f"ckv{i}")
                    mm = pe.matmul(ps[:, 0:T], o1, sqlat[:, first + i], start=i == 0, stop=i == n - 1)
                ready(mm, name)
            for n in ("gq", "gk"):
                for u in range(2):
                    w = unit(f"{n}{u}")
                    for c in range(2):
                        project((n, 2 * u + c), w, P * c, P, 256, nk)
            for u in range(2):
                w = unit(f"gv{u}")[:, 0:2048].rearrange("p (k n) -> p k n", n=256)
                for tt in range(3):
                    m = P if tt < 2 else TN
                    ps = bank(("gv", u, tt))
                    for k in range(DB):
                        mm = pe.matmul(ps[0:m, 0:256], n3[:, k, tt * P:tt * P + m], w[:, k], start=k == 0, stop=k == DB - 1)
                    ready(mm, ("gv", u, tt))
            for u in range(2):
                w = unit(f"gr{u}")
                for c in range(2):
                    project(("gr", 2 * u + c), w, P * c, P, 256, nk)

            pe.wait_ge(w_in, 16)
            pe.wait_ge(cqn_ready, 1)
            for h in range(H):
                ps = bank(("q", h))
                for k in range(QB):
                    mm = pe.matmul(ps[0:QK, 0:T], wuq[:, k, QK * h:QK * h + QK], cqn[:, k], start=k == 0, stop=k == QB - 1)
                ready(mm, ("q", h))
            pe.wait_ge(ckvn_ready, 1)
            for h in range(H):
                ps = bank(("k", h))
                for k in range(KB):
                    mm = pe.matmul(ps[0:NOPE, 0:T], wuk[:, k, NOPE * h:NOPE * h + NOPE], ckvn[:, k], start=k == 0, stop=k == KB - 1)
                ready(mm, ("k", h))
            pe.wait_ge(const_in, 16)
            perm = cst("perm")
            for h in range(H):
                ps = bank(("qss", h))
                copied(pe, ("q", h))
                ready(pe.matmul(ps[0:QK, 0:T], o96[0:QK, 0:QK], sq96[0:QK, h], start=True, stop=True), ("qss", h))
                ps = bank(("qrot", h))
                ready(pe.matmul(ps[64:96, 0:T], perm[64:96, 64:96], qh[64:96, h], start=True, stop=True), ("qrot", h))
            ps = bank("krot")
            pe.wait_ge(kpeg_ready, 1)
            ready(pe.matmul(ps[64:96, 0:T], perm[64:96, 64:96], kh[64:96, 0], start=True, stop=True), "krot")
            for h in range(H):
                ps = bank(("kss", h))
                copied(pe, ("k", h))
                pe.wait_ge(kpe_squared, 1)
                ready(pe.matmul(ps[0:QK, 0:T], o96[0:QK, 0:QK], sq96k[0:QK, h], start=True, stop=True), ("kss", h))
            for tt in range(2):
                ps = bank(("v", tt))
                for k in range(KB):
                    mm = pe.matmul(ps[:, :], ckvn[:, k, tt * P:tt * P + P], wuv[:, k], start=k == 0, stop=k == KB - 1)
                ready(mm, ("v", tt))
            ident = cst("ident")
            ps = bank("ctok")
            for k in range(KB):
                mm = pe.transpose(ps[0:TN, k * P:k * P + P], ckvn[:, k, TP:T], ident)
            ready(mm, "ctok")

            pe.wait_ge(qh_ready, 1)
            pe.wait_ge(kh_ready, 2)
            ps = bank("snew")
            for h in range(H):
                mm = pe.matmul(ps[0:TN, h * TN:h * TN + TN], kh[0:QK, h, TP:T], qh[0:QK, h, TP:T], start=h == 0, stop=h == H - 1,
                               skip_group_check=True)
            ready(mm, "snew")

            def scores(h):
                ps = bank(("att", h))
                pe.matmul(ps[:, 0:P], qh[0:QK, h, 0:P], kh[0:QK, h, 0:P], start=True, stop=False, skip_group_check=True)
                ready(pe.matmul(ps[:, P:3 * P], qh[0:QK, h, P:TP], kh[0:QK, h, 0:TP], start=False, stop=True, skip_group_check=True), ("att", h))

            def turn(h):
                ps = bank(("attT", h))
                pe.wait_ge(p_ready, 2 * h + 2)
                for c in range(3):
                    mm = pe.transpose(ps[:, c * P:c * P + P], patt[:, h % 2, c * P:c * P + P], ident)
                ready(mm, ("attT", h))

            def values(h):
                if h % 2 == 0:
                    bank(("atto", h // 2))
                    copied(pe, ("v", 0))
                    copied(pe, ("v", 1))
                ps = PS[g.of[("atto", h // 2)][1]]
                lo = 64 * (h % 2)
                copied(pe, ("attT", h))
                pe.matmul(ps[lo:lo + 64, 0:TP], vtok[:, 0, VD * h:VD * h + VD], pTt[:, h % 2, 0:TP], start=True, stop=False, skip_group_check=True)
                mm = pe.matmul(ps[lo:lo + 64, P:TP], vtok[:, 1, VD * h:VD * h + VD], pTt[:, h % 2, TP:3 * P], start=False, stop=True, skip_group_check=True)
                if h % 2:
                    ready(mm, ("atto", h // 2))
                else:
                    mm.then_inc(atto_half, 1)

            for h in range(H):
                scores(h)
                turn(h)
                values(h)

            pe.wait_ge(lin_in, 32)
            copied(pe, "ga")
            for tt in range(3):
                m = P if tt < 2 else TN
                ps = bank(("lg", tt))
                pe.matmul(ps[0:m, :], ga[0:16, tt * P:tt * P + m], lin[0:16, 0:512], start=True, stop=False)
                ready(pe.matmul(ps[0:m, :], o1[0:1, 0:m], lin[0:1, 512:1024], start=False, stop=True), ("lg", tt))
            tri, tri4 = cst("tri"), cst("tri4")
            pe.wait_ge(lg_ready, 3)
            for h in range(GH):
                ps = bank(("b", h))
                for tt in range(2):
                    pe.matmul(ps[:, tt * P:tt * P + P], lgs[:, tt, GD * h:GD * h + GD], tri, start=tt == 0, stop=False, skip_group_check=True)
                ready(pe.matmul(ps[:, TP:T], lgs[0:TN, 2, GD * h:GD * h + GD], tri4[0:TN, :], start=False, stop=True, skip_group_check=True), ("b", h))
            pe.wait_ge(gla_ready, 4)
            for h in range(GH):
                ps = bank(("ktok", h))
                for tt in range(2):
                    pe.transpose(ps[:, tt * P:tt * P + P], kd[:, h, tt * P:tt * P + P], ident)
                ready(pe.transpose(ps[0:TN, TP:TP + P], kd[:, h, TP:T], ident), ("ktok", h))
                ps = bank(("gatt", h))
                for tt in range(2):
                    pe.matmul(ps[:, P * tt:P * tt + P], kt[:, h, P * tt:P * tt + P], qt[:, h, P * tt:P * tt + P],
                              start=tt == 0, stop=False, skip_group_check=True)
                ready(pe.matmul(ps[0:TN, TP:T], kt[:, h, TP:T], qt[:, h, TP:T], start=False, stop=True, skip_group_check=True), ("gatt", h))
            for h in range(GH):
                copied(pe, ("ktok", h))
                for half in range(2):
                    ps = bank(("gs", h, half))
                    lo = 64 * half
                    for tt in range(2):
                        mm = pe.matmul(ps[:, tt * P:tt * P + P], ktok[lo:lo + 64, h, tt * P:tt * P + P], gv[lo:lo + 64, tt, GD * h:GD * h + GD],
                                       start=tt == 0, stop=tt == 1, skip_group_check=True)
                    ready(mm, ("gs", h, half))
            for h in range(GH):
                ps = bank(("go", h))
                copied(pe, ("gatt", h))
                for tt in range(2):
                    pe.matmul(ps[:, P * tt:P * tt + P], gv[:, tt, GD * h:GD * h + GD], attm[:, h, P * tt:P * tt + P],
                              start=tt == 0, stop=False, skip_group_check=True)
                pe.matmul(ps[:, TP:T], gv[0:TN, 2, GD * h:GD * h + GD], attms[0:TN, h], start=False, stop=False, skip_group_check=True)
                pe.wait_ge(s0_in[h % 2], 16 * (h // 2 + 1))
                for b in range(NS):
                    lo = TP + TS * b
                    pe.matmul(ps[:, lo:lo + TS], s0[h % 2][:, b], qb[:, h, lo:lo + TS], start=False, stop=False, skip_group_check=True)
                copied(pe, ("gs", h, 0))
                copied(pe, ("gs", h, 1))
                for c in range(1, NCH):
                    mm = pe.matmul(ps[:, GC * c:GC * c + GC], st[:, h, c - 1], qb[:, h, GC * c:GC * c + GC], start=False, stop=c == NCH - 1,
                                   skip_group_check=True)
                ready(mm, ("go", h))
                ps = bank(("oss", h))
                copied(pe, ("go", h))
                ready(pe.matmul(ps[:, 0:T], o128, dT[:, h], start=True, stop=True), ("oss", h))
                pe.wait_ge(vmask_ready, h + 1)
                for c in range(2):
                    ps = bank(("su", h, c))
                    ready(pe.matmul(ps[:, :], ktok[0:TN, h, TP:TP + P], vmask[0:TN, 4 * c:4 * c + 4].rearrange("p b v -> p (b v)"),
                                    start=True, stop=True), ("su", h, c))

            ps = bank("kpss")
            pe.wait_ge(ckpe_squared, 1)
            kpesq = view(arena, kto, NG * PAGE, g=NG, k=PAGE)
            for i in range(NG):
                mm = pe.matmul(ps[:, 4 * i:4 * i + 4], kpesq[:, i], cst("page4"), start=i == 0, stop=i == NG - 1, skip_group_check=True)
            ready(mm, "kpss")
            pe.wait_ge(ckpe_scaled, 1)
            for c in range(4):
                ps = bank(("krotc", c))
                ready(pe.matmul(ps[:, :], perm, kpe[:, 4 * c:4 * c + 4].rearrange("p g k -> p (g k)"), start=True, stop=True), ("krotc", c))
            pe.wait_ge(ckpe_ready, 4)
            pe.wait_ge(qbd_ready, 2)
            pe.wait_ge(qpe_ready, 4)

            def expand(i):
                pe.wait_ge(page_in[i % 2], 64 * (i // 2 + 1))
                for blk in range(4):
                    ps = bank(("ke", i, blk))
                    for k in range(KB):
                        mm = pe.matmul(ps[:, :], wuk[:, k, P * blk:P * blk + P], pages[:, i % 2, :, k], start=k == 0, stop=k == KB - 1)
                    ready(mm, ("ke", i, blk))

            def score(i):
                b = i // 2
                ps = bank(("sc", i))
                for blk in range(4):
                    copied(pe, ("ke", i, blk))
                pe.matmul(ps[:, 0:128], kpe[:, i], qpe[:, b].rearrange("p j c -> p (j c)"), start=True, stop=False, skip_group_check=True)
                for j in range(4):
                    for blk in range(4):
                        pe.matmul(ps[:, 32 * j + 8 * blk:32 * j + 8 * blk + 8], kT[:, i % 2, blk, PAGE * j:PAGE * j + PAGE], qbd[:, b, blk],
                                  start=False, stop=False, skip_group_check=True)
                        mm = pe.matmul(ps[:, 128 + 8 * j + 2 * blk:128 + 8 * j + 2 * blk + 2], ksq[:, i % 2, blk, PAGE * j:PAGE * j + PAGE],
                                       cst("head2"), start=False, stop=j == 3 and blk == 3, skip_group_check=True)
                ready(mm, ("sc", i))

            for i in range(NG + 1):
                if i < NG:
                    expand(i)
                if i >= 1:
                    score(i - 1)
            pe.wait_ge(m_ready, 1)
            for c in range(2):
                ps = bank(f"mT{c}")
                ready(pe.transpose(ps[:, 0:P], mx[:, P * c:P * c + P], ident), f"mT{c}")
            pe.wait_ge(diag_ready, 2)
            ps = bank("mB")
            ready(pe.matmul(ps[:, 0:256], o1, diag, start=True, stop=True), "mB")
            pe.wait_ge(p_all, 2)
            ps = bank("l")
            for k in range(NPG):
                pe.matmul(ps[:, 0:256], o1, S[:, k].rearrange("p b c -> p (b c)"), start=k == 0, stop=False)
            snf = ab("snew")
            ready(pe.matmul(ps[:, 0:256], o1[0:TN, :], snf[0:TN, :], start=False, stop=True), "l")
            copied(pe, "ctok")
            ol = [bank("ol0"), bank("ol1")]
            for k in range(KB):
                pe.matmul(ol[k][:, 0:256], ctok[0:TN, k], snf[0:TN, :], start=True, stop=False, skip_group_check=True)
            for n in range(NS * NPG):
                pe.wait_ge(cpage_in[n % 16], 16 * (n // 16 + 1))
                b, kk = n // NPG, n % NPG
                for k in range(KB):
                    mm = pe.matmul(ol[k][:, 32 * b:32 * b + 32], cpages[:, n % 16, P * k:P * k + P], S[:, kk, b], start=False,
                                   stop=n == NS * NPG - 1, skip_group_check=True)
                    if n == NS * NPG - 1:
                        ready(mm, f"ol{k}")
                    elif k == 1:
                        mm.then_inc(cpage_used, 1)
            ps = bank("oa")
            copied(pe, "ol0")
            copied(pe, "ol1")
            for h in range(H):
                lo, co = 64 * (h % 2), TN * (h // 2)
                for k in range(KB):
                    mm = pe.matmul(ps[lo:lo + 64, co:co + TN], wuv[:, k, VD * h:VD * h + VD], olat[:, k, h].rearrange("p b t -> p (b t)"),
                                   start=h < 2 and k == 0, stop=k == KB - 1, skip_group_check=True)
            ready(mm, "oa")
            copied(pe, "oa")
            copied(pe, ("atto", 3))
            pe.wait_ge(gmix_ready, GH)
            for u in range(4):
                w = unit(f"out{u}")
                for c in range(2):
                    project(("out", 2 * u + c), w, P * c, P, 256, nk)

            def mlp(L):
                sumsq(1 + 3 * L)
                for u in range(16):
                    w = unit(f"up{L}_{u}")
                    for c in range(2):
                        project(("up", L, 2 * u + c), w, P * c, P, 256, nk, norm_wait(1 + 3 * L) if u == 0 and c == 0 else None)
                if L == 0:
                    s5_matrices()
                for i in range(8):
                    for half in range(2):
                        w = unit(f"down{L}_{2 * i + half}")
                        if i == 0:
                            for f in range(16 * half, 16 * half + 16):
                                copied(pe, ("up", L, f))
                        project(("down", L, i), w, 0, P, P, lambda k: a2[:, 16 * half + k], blocks=16, first=half == 0, last=half == 1)

            def s5_matrices():
                pe.wait_ge(b_copied, 16)
                pe.wait_ge(c_copied, 20)
                for i in range(8):
                    ps = bank(("G", i))
                    for s in range(4):
                        for n, (bm, cm) in enumerate(((Bre, Cre), (Bim, Cim))):
                            blk = 4 * i + s
                            mm = pe.matmul(ps[0:32, P * s:P * s + P], bm[:, blk, 3], cm[:, blk, 0:4].rearrange("p i c -> p (i c)"),
                                           start=s == 0 and n == 0, stop=s == 3 and n == 1, skip_group_check=True)
                    ready(mm, ("G", i))
                for i in range(16):
                    ps = bank(("BT", i))
                    bm = (Bre, Bim)[i % 2]
                    for s in range(4):
                        mm = pe.transpose(ps[:, P * s:P * s + P], bm[:, 4 * (i // 2) + s].rearrange("p i c -> p (i c)"), ident)
                    ready(mm, ("BT", i))

            def ple(L):
                sumsq(2 + 3 * L)
                pe.wait_ge(p_in1 if L else p_in0, 16)
                wp = unit(f"proj{L}")
                for i in range(8):
                    project(("proj", L, i), wp, P * i, P, D, lambda k: p3[:, k], blocks=2)
                    if i % 2 == 0:
                        w = unit(f"gate{L}_{i // 2}")
                    project(("gate", L, i), w, P * (i % 2), P, 256, nk, norm_wait(2 + 3 * L) if i == 0 else None)

            mlp(0)
            ple(0)

            sumsq(3)
            pe.wait_ge(stack_in, 256)
            for i in range(16):
                copied(pe, ("BT", i))
            for i in range(16):
                ps = bank(("v5", i))
                for s in range(2):
                    for r, bm in enumerate((Bre, Bim)):
                        blk = 2 * i + s
                        mm = pe.matmul(ps[:, (2 * s + r) * J:(2 * s + r) * J + J], bm[:, blk].rearrange("p i c -> p (i c)"), ustk[:, blk],
                                       start=s == 0 and r == 0, stop=s == 1 and r == 1, skip_group_check=True)
                ready(mm, ("v5", i))
            pe.wait_ge(scan_ready, 1)
            pe.wait_ge(x0_in, 32)
            for i in range(8):
                copied(pe, ("G", i))
            for i in range(8):
                ps = bank(("y5", i))
                for s in range(4):
                    blk = 4 * i + s
                    o = ps[:, s * J:s * J + J]
                    pe.matmul(o, Cre[:, blk, 1:5].rearrange("p i c -> p (i c)"), X[:, 0, blk], start=s == 0, stop=False, skip_group_check=True)
                    pe.matmul(o, Cim[:, blk, 1:5].rearrange("p i c -> p (i c)"), X[:, 1, blk], start=False, stop=False, skip_group_check=True)
                    mm = pe.matmul(o, toep[:, blk].rearrange("p i c -> p (i c)"), ustk[:, blk], start=False, stop=s == 3, skip_group_check=True)
                ready(mm, ("y5", i))
            pe.wait_ge(unstack_in, 256)
            for i in range(8):
                w = unit(f"glu{i}")
                project(("glu_a", i), w, 0, P, 256, nk)
                project(("glu_g", i), w, P, P, 256, nk)
            mlp(1)
            ple(1)

        @block.scalar
        def _(act):
            step = [0]

            def link(ins):
                step[0] += 1
                ins.then_inc(act_step, 1)
                act.wait_ge(act_step, step[0])

            def squares(k):
                for b in range(DB):
                    if k == 0:
                        act.wait_ge(x_in, 16)
                    elif k in (1, 2, 5):
                        copied(act, ("out", b) if k == 1 else ("down", k // 3, b))
                    else:
                        act.wait_ge(h_gated, 8 * (k - 3) + b + 1)
                    if b >= 4:
                        act.wait_ge(sumsq_step, 7 * k + b - 3)
                    act.activation(sq3[:, b % 4], h3[:, b], ACT.Square).then_inc(sq_ready, 1)

            def rsqrt(out, name, rows=P, scale=1.0):
                ps = result(act, name)
                link(act.activation(out, ps[0:rows, 0:T], ACT.Ln, scale=scale, bias=eps[0:rows, :]))
                act.activation(out, out, ACT.Exp, scale=-0.5).then_inc(bank_of(name), 1)

            act.wait_ge(ones_set, 5)
            squares(0)
            rsqrt(rs[:, :], ("ss", 0))
            for i, n in enumerate(("cq0", "cq1", "cq2", "ckv0", "ckv1")):
                ps = result(act, n)
                act.activation(sqlat[:, i], ps[:, 0:T], ACT.Square).then_inc(bank_of(n), 1)
            ps = result(act, "kpe")
            act.activation(kpen[64:96, :], ps[64:96, 0:T], ACT.Copy).then_inc(bank_of("kpe"), 1)
            ps = result(act, "ga")
            act.activation(ga[0:16, :], ps[0:16, 0:T], ACT.Copy).then_inc(bank_of("ga"), 1)
            copied(act, "kpe")
            act.activation(sq96k[64:96], bc(kpen[64:96, :].unsqueeze(1), [32, H, T]), ACT.Square).then_inc(kpe_squared, 1)
            rsqrt(tA, "cqss", scale=1.0 / (QB * P))
            rsqrt(tB, "ckvss", scale=1.0 / (KB * P))
            for i in range(GH):
                ps = result(act, ("gq", i))
                act.activation(gq[:, i], ps[:, 0:T], ACT.Copy, scale=float(GD) ** -0.5).then_inc(bank_of(("gq", i)), 1)
            for i in range(GH):
                ps = result(act, ("gr", i))
                act.activation(gr[:, i], ps[:, 0:T], ACT.Exp, scale=-1.0).then_inc(bank_of(("gr", i)), 1)
            for h in range(H):
                ps = result(act, ("q", h))
                act.activation(sq96[0:QK, h], ps[0:QK, 0:T], ACT.Square).then_inc(bank_of(("q", h)), 1)
            for h in range(H):
                ps = result(act, ("k", h))
                act.activation(sq96k[0:NOPE, h], ps[0:NOPE, 0:T], ACT.Square).then_inc(bank_of(("k", h)), 1)
            for h in range(H):
                rsqrt(r96[0:QK, h], ("qss", h), QK)
            act.wait_ge(qh_ready, 1)
            for h in range(H):
                rsqrt(r96[0:QK, h], ("kss", h), QK)
            for tt in range(2):
                ps = result(act, ("v", tt))
                act.activation(vtok[:, tt], ps[:, :], ACT.Copy).then_inc(bank_of(("v", tt)), 1)
            ps = result(act, "ctok")
            act.activation(ab("ctok")[0:TN, :], ps[0:TN, 0:256], ACT.Copy).then_inc(bank_of("ctok"), 1)
            for h in range(H):
                o = 32 * (h % 2)
                act.wait_ge(negmax_ready, h + 1)
                for c, (lo, hi) in enumerate(((0, P), (P, 3 * P))):
                    act.activation(patt[:, h % 2, lo:hi], patt[:, h % 2, lo:hi], ACT.Exp, bias=stat[:, o + 2 + c:o + 3 + c], scale=SCALE,
                                   accum_out=stat[:, o + 4 + c:o + 5 + c]).then_inc(p_exp, 1)
                ps = result(act, ("attT", h))
                if h >= 2:
                    if h % 2 == 0:
                        act.wait_ge(atto_half, h // 2)
                    else:
                        act.wait_ge(main_ready, g.of[("atto", (h - 2) // 2)][2])
                act.activation(pTt[:, h % 2], ps[:, 0:384], ACT.Copy).then_inc(bank_of(("attT", h)), 1)
            for tt in range(3):
                m = P if tt < 2 else TN
                ps = result(act, ("lg", tt))
                act.activation(lgs[0:m, tt], ps[0:m, :], ACT.Abs).then_inc(bank_of(("lg", tt)), 1)
                copied(act, ("lg", tt), 1)
                link(act.activation(lgs[0:m, tt], lgs[0:m, tt], ACT.Exp, scale=-1.0))
                act.activation(lgs[0:m, tt], lgs[0:m, tt], ACT.Ln, bias=1.0).then_inc(softplus_ready, 1)
            act.wait_ge(diff_ready, 1)
            for h in range(GH):
                copied(act, ("b", h))
            act.activation(qt, dT, ACT.Exp, scale=1 / 16).then_inc(decay_ready, 1)
            act.activation(kt, dT, ACT.Exp, scale=-1 / 16).then_inc(decay_ready, 1)
            act.activation(ebl, bT, ACT.Exp, scale=1 / 16).then_inc(decay_ready, 1)
            act.activation(kd, kd, ACT.Exp, scale=1 / 16).then_inc(decay_ready, 1)
            for h in range(GH):
                ps = result(act, ("ktok", h))
                act.activation(ktok[:, h, 0:TP], ps[:, 0:TP], ACT.Copy).then_inc(bank_of(("ktok", h)), 1)
                act.activation(ktok[0:TN, h, TP:384], ps[0:TN, TP:384], ACT.Copy).then_inc(bank_of(("ktok", h)), 1)
            act.wait_ge(decay_ready, 4)
            for h in range(GH):
                ps = result(act, ("go", h))
                act.activation(dT[:, h], ps[:, 0:T], ACT.Square).then_inc(bank_of(("go", h)), 1)
                if h >= 2:
                    act.wait_ge(gmix_ready, h - 1)
                rsqrt((tA, tB)[h % 2], ("oss", h))

            def key_factors(i):
                r = tA[:, 32 * (i % 2):32 * (i % 2) + 32]
                act.wait_ge(ksum_ready, i + 1)
                link(act.activation(r, r, ACT.Ln, bias=eps[:, :]))
                act.activation(r, r, ACT.Exp, scale=-0.5).then_inc(kfactor_ready, 1)

            act.wait_ge(kpe_in, 16 * NS * NPG)
            act.wait_ge(gmix_ready, GH)
            copied(act, ("su", GH - 1, 1))
            act.activation(view(arena, kto, NG * PAGE), ab("kpe"), ACT.Square).then_inc(ckpe_squared, 1)
            act.wait_ge(ckpe_ready, 4)
            for i in range(NG):
                for blk in range(4):
                    ps = result(act, ("ke", i, blk))
                    if i >= 2 and blk == 0:
                        act.wait_ge(side_ready, g.of[("sc", i - 2)][2])
                    act.activation(ksq[:, i % 2, blk], ps[:, :], ACT.Square).then_inc(bank_of(("ke", i, blk)), 1)
                if i >= 1:
                    key_factors(i - 1)
            key_factors(NG - 1)
            copied(act, "mB")
            act.activation(S, S, ACT.Exp, scale=SCALE).then_inc(p_all, 1)
            act.activation(ab("snew")[0:TN, :], ab("snew")[0:TN, :], ACT.Exp, scale=SCALE).then_inc(p_all, 1)

            def relu(L, i):
                ps = result(act, ("up", L, i))
                act.activation(a2[:, i], ps[:, 0:T], ACT.Relu).then_inc(bank_of(("up", L, i)), 1)

            def gates(base, names):
                for i in range(8):
                    n = base + i
                    ps = result(act, names[i])
                    if n >= 2:
                        act.wait_ge(h_gated, n - 1)
                    act.activation((tA, tB)[n % 2], ps[:, 0:T], ACT.Exp, scale=-1.0).then_inc(bank_of(names[i]), 1)

            squares(1)
            rsqrt(rs[:, :], ("ss", 1))
            act.wait_ge(params_in, 16)
            copied(act, "oa")
            act.wait_ge(out_done, 16 * (2 + GH))
            act.activation(cf(0), prm("log_dt"), ACT.Exp).then_inc(s5_exp, 1)
            relu(0, 0)
            relu(0, 1)
            act.wait_ge(s5_angle, 1)
            act.activation(cf(4), cf(1), ACT.Exp).then_inc(s5_sin, 1)
            act.activation(cf(5), cf(2), ACT.Sin).then_inc(s5_sin, 1)
            act.activation(cf(6), cf(2), ACT.Sin, scale=0.5).then_inc(s5_sin, 1)
            act.wait_ge(s5_zero, 1)
            for e in range(4):
                relu(0, 2 + 2 * e)
                relu(0, 3 + 2 * e)
                act.wait_ge(b_power, e + 1)
                src = (cur, braw)[e % 2]
                for r, dst in enumerate((Bre, Bim)):
                    for half in range(2):
                        lo = 64 * half
                        act.activation(dst[lo:lo + 64, :, 3 - e, 16 * half:16 * half + 16], src[r][lo:lo + 64], ACT.Copy).then_inc(b_copied, 1)
            for e in range(5):
                relu(0, 10 + 2 * e)
                relu(0, 11 + 2 * e)
                act.wait_ge(c_power, e + 1)
                src = craw if e == 0 else (cur, braw)[e % 2]
                for r, dst in enumerate((Cre, Cim)):
                    for half in range(2):
                        lo = 64 * half
                        act.activation(dst[lo:lo + 64, :, e, 16 * half:16 * half + 16], src[r][lo:lo + 64], ACT.Copy,
                                       scale=1.0 if r == 0 else -1.0).then_inc(c_copied, 1)
            for i in range(20, FB):
                relu(0, i)
            act.wait_ge(toep_zero, 1)
            for i in range(8):
                ps = result(act, ("G", i))
                copied(act, ("G", i), 2)
                for k in (2, 3):
                    act.activation(toep[32 * k:32 * k + 32, 4 * i:4 * i + 4, k:4], ps[0:32, :].rearrange("p (s i c) -> p s i c", s=4, i=4)[:, :, 0:4 - k],
                                   ACT.Copy).then_inc(bank_of(("G", i)), 1)
            for i in range(0, 16, 2):
                ps = result(act, ("BT", i))
                act.activation(Bre[:, 2 * i:2 * i + 4].rearrange("p s i c -> p (s i c)"), ps[:, :], ACT.Copy).then_inc(bank_of(("BT", i)), 1)
            squares(2)
            rsqrt(rs[:, :], ("ss", 2))
            gates(0, [("gate", 0, i) for i in range(8)])
            squares(3)
            rsqrt(rs[:, :], ("ss", 3))
            act.wait_ge(stack_in, 256)
            for i in range(0, 16, 2):
                ps = result(act, ("v5", i))
                act.activation(vb[:, :, :, 2 * i:2 * i + 2].rearrange("p j r s -> p s r j"), ps[:, 0:4 * J].rearrange("p (s r j) -> p s r j", s=2, r=2),
                               ACT.Copy).then_inc(bank_of(("v5", i)), 1)
            for i in range(8):
                copied(act, ("y5", i))
                act.activation(ustk[:, 4 * i:4 * i + 4], ustk[:, 4 * i:4 * i + 4], ACT.Gelu_apprx_tanh).then_inc(gelu_ready, 1)
            gates(8, [("glu_g", i) for i in range(8)])
            squares(4)
            rsqrt(rs[:, :], ("ss", 4))
            for i in range(FB):
                relu(1, i)
            squares(5)
            rsqrt(rs[:, :], ("ss", 5))
            gates(16, [("gate", 1, i) for i in range(8)])

        @block.vector
        def _(dve):
            step = [0]
            V = nc.vector

            def link(ins):
                step[0] += 1
                ins.then_inc(dve_step, 1)
                dve.wait_ge(dve_step, step[0])

            def norm(k, gain):
                copied(dve, ("ss", k))
                for b in range(DB):
                    if k == 3:
                        o, x, r = n3[:, b].rearrange("p (i j) -> p j i", i=TS), h3[:, b].rearrange("p (j i) -> p j i", i=TS), rs[:, :].rearrange("p (j i) -> p j i", i=TS)
                    else:
                        o, x, r = n3[:, b], h3[:, b], rs[:, :]
                    V.scalar_tensor_tensor(o, x, gain[:, b:b + 1], r, ALU.mult, ALU.mult).then_inc(n_ready, 1)

            dve.wait_ge(params_in, 16)
            dve.wait_ge(x_in, 16)
            norm(0, prm("g_ab"))
            for i in range(3):
                ps = result(dve, f"cq{i}")
                copied(dve, f"cq{i}", 1)
                V.tensor_scalar(cqn[:, i], ps[:, 0:T], prm("g_qlat")[:, i:i + 1], None, ALU.mult).then_inc(bank_of(f"cq{i}"), 1)
            for i in range(2):
                ps = result(dve, f"ckv{i}")
                copied(dve, f"ckv{i}", 1)
                V.tensor_scalar(ckvn[:, i], ps[:, 0:T], prm("g_kvlat")[:, i:i + 1], None, ALU.mult).then_inc(bank_of(f"ckv{i}"), 1)
            for name, n, x, done in (("cqss", QB, cqn, cqn_ready), ("ckvss", KB, ckvn, ckvn_ready)):
                copied(dve, name)
                V.tensor_tensor(x, x, bc((tA if n == QB else tB).unsqueeze(1), [P, n, T]), ALU.mult).then_inc(done, 1)
            for i in range(GH):
                ps = result(dve, ("gk", i))
                V.tensor_copy(gk[:, i], ps[:, 0:T]).then_inc(bank_of(("gk", i)), 1)
            for u in range(2):
                for tt in range(3):
                    m = P if tt < 2 else TN
                    ps = result(dve, ("gv", u, tt))
                    V.tensor_copy(gv[0:m, tt, 256 * u:256 * u + 256], ps[0:m, 0:256]).then_inc(bank_of(("gv", u, tt)), 1)
            for i in range(GH):
                ps = result(dve, ("gr", i))
                copied(dve, ("gr", i), 1)
                link(V.tensor_scalar(gr[:, i], gr[:, i], 1.0, None, ALU.add))
                link(V.reciprocal(gr[:, i], gr[:, i]))
                V.tensor_tensor(gr[:, i], gr[:, i], ps[:, 0:T], ALU.mult).then_inc(bank_of(("gr", i)), 1)
            for h in range(H):
                ps = result(dve, ("q", h))
                copied(dve, ("q", h), 1)
                V.tensor_scalar(qh[0:QK, h], ps[0:QK, 0:T], prm("g_qh")[0:QK], None, ALU.mult).then_inc(bank_of(("q", h)), 1)
            copied(dve, "kpe")
            V.tensor_scalar(kh[64:96, 0], kpen[64:96, :], prm("g_kh")[64:96], None, ALU.mult).then_inc(kpeg_ready, 1)
            for h in range(H):
                ps = result(dve, ("k", h))
                copied(dve, ("k", h), 1)
                V.tensor_scalar(kh[0:NOPE, h], ps[0:NOPE, 0:T], prm("g_kh")[0:NOPE], None, ALU.mult).then_inc(bank_of(("k", h)), 1)
            cosN, sinN = cst("cosN")[64:96], cst("sinN")[64:96]
            dve.wait_ge(const_in, 16)
            for h in range(H):
                ps = result(dve, ("qrot", h))
                V.tensor_tensor(tA[64:96], ps[64:96, 0:T], sinN, ALU.mult).then_inc(bank_of(("qrot", h)), 1)
                link(V.tensor_tensor(qh[64:96, h], qh[64:96, h], cosN, ALU.mult))
                copied(dve, ("qrot", h))
                link(V.tensor_tensor(qh[64:96, h], qh[64:96, h], tA[64:96], ALU.add))
            for h in range(H):
                copied(dve, ("qss", h))
            V.tensor_tensor(qh[0:QK], qh[0:QK], r96[0:QK], ALU.mult).then_inc(qh_ready, 1)
            ps = result(dve, "krot")
            V.tensor_tensor(tA[64:96], ps[64:96, 0:T], sinN, ALU.mult).then_inc(bank_of("krot"), 1)
            dve.wait_ge(kpeg_ready, 1)
            link(V.tensor_tensor(tB[64:96], kh[64:96, 0], cosN, ALU.mult))
            copied(dve, "krot")
            link(V.tensor_tensor(tB[64:96], tB[64:96], tA[64:96], ALU.add))
            for h in range(H):
                copied(dve, ("kss", h))
            V.tensor_tensor(kh[0:NOPE], kh[0:NOPE], r96[0:NOPE], ALU.mult).then_inc(kh_ready, 1)
            V.tensor_tensor(kh[64:96], r96[64:96], bc(tB[64:96].unsqueeze(1), [32, H, T]), ALU.mult).then_inc(kh_ready, 1)
            dve.wait_ge(qbd_zero, 2)
            for par2 in range(2):
                lo = 64 * par2
                for b in range(NS):
                    q = V.tensor_scalar(qbd[lo:lo + 64, b, :, 4 * par2:4 * par2 + 4],
                                        qh[0:64, par2::2, TP + TS * b:TP + TS * b + TS], prm("g_kh")[0:64], None, ALU.mult)
                q.then_inc(qbd_ready, 1)
            for j in range(4):
                for b in range(NS):
                    q = V.tensor_copy(qpe[32 * j:32 * j + 32, b, j].rearrange("p (h t) -> p h t", t=TS), qh[64:96, :, TP + TS * b:TP + TS * b + TS])
                q.then_inc(qpe_ready, 1)
            ps = result(dve, "snew")
            nm = cst("newmask")[0:TN].rearrange("p (b t) -> p b t", t=TS)
            for h in range(H):
                V.tensor_tensor(snew[0:TN, :, h], ps[0:TN, TN * h:TN * h + TN].rearrange("p (b t) -> p b t", t=TS), nm, ALU.add).then_inc(bank_of("snew"), 1)
            for h in range(H):
                o = 32 * (h % 2)
                ps = result(dve, ("att", h))
                if h >= 2:
                    dve.wait_ge(side_ready, g.of[("attT", h - 2)][2])
                V.tensor_tensor(patt[:, h % 2], ps[:, 0:384], cst("causal"), ALU.add).then_inc(bank_of(("att", h)), 1)
                copied(dve, ("att", h))
                V.tensor_reduce(stat[:, o:o + 1], patt[:, h % 2, 0:P], AX.X, ALU.max)
                link(V.tensor_reduce(stat[:, o + 1:o + 2], patt[:, h % 2, P:384], AX.X, ALU.max))
                V.tensor_scalar(stat[:, o + 2:o + 4], stat[:, o:o + 2], -SCALE, None, ALU.mult).then_inc(negmax_ready, 1)
                dve.wait_ge(p_exp, 2 * h + 2)
                link(V.reciprocal(stat[:, o + 6:o + 8], stat[:, o + 4:o + 6]))
                V.tensor_scalar(patt[:, h % 2, 0:P], patt[:, h % 2, 0:P], stat[:, o + 6:o + 7], None, ALU.mult).then_inc(p_ready, 1)
                V.tensor_scalar(patt[:, h % 2, P:384], patt[:, h % 2, P:384], stat[:, o + 7:o + 8], None, ALU.mult).then_inc(p_ready, 1)
                if h % 2:
                    ps = result(dve, ("atto", h // 2))
                    V.tensor_copy(mix[:, h // 2, 0:TP], ps[:, 0:TP]).then_inc(bank_of(("atto", h // 2)), 1)
            for tt in range(3):
                m = P if tt < 2 else TN
                ps = result(dve, ("lg", tt))
                copied(dve, ("lg", tt), 1)
                V.tensor_scalar(lgmin[0:m, tt], ps[0:m, :], 0.0, None, ALU.min).then_inc(bank_of(("lg", tt)), 1)
                copied(dve, ("lg", tt))
                dve.wait_ge(softplus_ready, tt + 1)
                V.tensor_tensor(lgs[0:m, tt], lgmin[0:m, tt], lgs[0:m, tt], ALU.subtract).then_inc(lg_ready, 1)
            for h in range(GH):
                ps = result(dve, ("b", h))
                V.tensor_copy(bT[:, h], ps[:, 0:T]).then_inc(bank_of(("b", h)), 1)
            for h in range(GH):
                copied(dve, ("b", h))
            for c in range(NCH):
                lo = GC * c
                V.tensor_tensor(dT[:, :, lo:lo + GC], bT[:, :, lo:lo + GC], bc(bT[:, :, lo + GC // 2 - 1:lo + GC // 2], [P, GH, GC]), ALU.subtract)
                V.tensor_tensor(kd[:, :, lo:lo + GC], bc(bT[:, :, lo + GC - 1:lo + GC], [P, GH, GC]), bT[:, :, lo:lo + GC], ALU.subtract)
            for b in range(NS):
                lo = TP + TS * b
                V.tensor_tensor(kd[:, :, lo:lo + TS], bc(bT[:, :, lo + TS - 1:lo + TS], [P, GH, TS]), bT[:, :, lo:lo + TS], ALU.subtract)
            V.tensor_copy(dT[:, :, TP:T], bT[:, :, TP:T]).then_inc(diff_ready, 1)
            dve.wait_ge(decay_ready, 4)
            V.tensor_tensor(qt, qt, gq, ALU.mult).then_inc(gla_ready, 1)
            V.tensor_tensor(kt, kt, gk, ALU.mult).then_inc(gla_ready, 1)
            V.tensor_tensor(qb, ebl, gq, ALU.mult).then_inc(gla_ready, 1)
            V.tensor_tensor(kd, kd, gk, ALU.mult).then_inc(gla_ready, 1)
            for h in range(GH):
                ps = result(dve, ("gatt", h))
                V.tensor_tensor(attm[:, h].rearrange("p (c t) -> p c t", c=2), ps[:, 0:TP].rearrange("p (c t) -> p c t", c=2),
                                bc(cst("tri").unsqueeze(1), [P, 2, P]), ALU.mult).then_inc(bank_of(("gatt", h)), 1)
                V.tensor_tensor(attms[0:TN, h], ps[0:TN, TP:T], cst("tri4")[0:TN], ALU.mult).then_inc(bank_of(("gatt", h)), 1)
            for h in range(GH):
                for c in range(NCH):
                    name = ("gs", h, c % 2)
                    ps = result(dve, name)
                    add = ps[:, P * (c // 2):P * (c // 2) + P]
                    if c == 0:
                        V.tensor_copy(st[:, h, 0], add).then_inc(bank_of(name), 1)
                    else:
                        copied(dve, ("gs", h, 1 - c % 2), (c + 1) // 2)
                        V.scalar_tensor_tensor(st[:, h, c], st[:, h, c - 1], ebl[:, h, GC * c + GC - 1:GC * c + GC], add,
                                               ALU.mult, ALU.add).then_inc(bank_of(name), 1)
            for h in range(GH):
                if h >= 1:
                    dve.wait_ge(side_ready, g.of[("su", h - 1, 1)][2])
                V.tensor_tensor(vmask[0:TN], bc(gv[0:TN, 2, GD * h:GD * h + GD].unsqueeze(1), [TN, NS, GD]),
                                bc(cst("seqmask")[0:TN].unsqueeze(2), [TN, NS, GD]), ALU.mult).then_inc(vmask_ready, 1)
                ps = result(dve, ("go", h))
                copied(dve, ("go", h), 1)
                V.tensor_scalar(ogt[:, h], ps[:, 0:T], prm("g_o"), None, ALU.mult).then_inc(bank_of(("go", h)), 1)
                copied(dve, ("go", h))
                copied(dve, ("oss", h))
                link(V.tensor_tensor(ogt[:, h], ogt[:, h], (tA, tB)[h % 2], ALU.mult))
                V.tensor_tensor(mix[:, 4 + h], ogt[:, h], gr[:, h], ALU.mult).then_inc(gmix_ready, 1)
                link(V.tensor_tensor(s0[h % 2], s0[h % 2], bc(ebl[:, h, TP + TS - 1:T:TS].unsqueeze(2), [P, NS, GD]), ALU.mult))
                for c in range(2):
                    ps = result(dve, ("su", h, c))
                    V.tensor_tensor(s0[h % 2][:, 4 * c:4 * c + 4], s0[h % 2][:, 4 * c:4 * c + 4], ps[:, :].rearrange("p (b v) -> p b v", v=GD),
                                    ALU.add).then_inc(bank_of(("su", h, c)), 1)
            ps = result(dve, "kpss")
            V.tensor_copy(ab("kpss"), ps[:, 0:64]).then_inc(bank_of("kpss"), 1)
            V.tensor_scalar(ab("kpe"), ab("kpe"), prm("g_kpe"), None, ALU.mult).then_inc(ckpe_scaled, 1)
            dve.wait_ge(ckpe_scaled, 1)
            krt = view(arena, kso, 2048, c=4, b=2, n=256)
            kpc = ab("kpe", c=4, b=2, n=256)
            for c in range(4):
                ps = result(dve, ("krotc", c))
                V.tensor_tensor(krt[:, c], ps[:, :].rearrange("p (b n) -> p b n", b=2), bc(cst("sinC").unsqueeze(1), [P, 2, 256]), ALU.mult).then_inc(bank_of(("krotc", c)), 1)
                link(V.tensor_tensor(kpc[:, c], kpc[:, c], bc(cst("cosC").unsqueeze(1), [P, 2, 256]), ALU.mult))
                copied(dve, ("krotc", c))
                V.tensor_tensor(kpc[:, c], kpc[:, c], krt[:, c], ALU.add).then_inc(ckpe_ready, 1)

            def key_sums(i):
                ps = result(dve, ("sc", i))
                ssum = tA[:, 32 * (i % 2):32 * (i % 2) + 32]
                V.tensor_tensor(ssum.rearrange("p (j h) -> p j h", j=4), ps[:, 128:160].rearrange("p (j h) -> p j h", j=4),
                                bc(kpss[:, i].unsqueeze(2), [P, 4, H]), ALU.add).then_inc(ksum_ready, 1)

            def scores(i):
                b, half = i // 2, i % 2
                ps = PS[g.of[("sc", i)][1]]
                ssum = tA[:, 32 * half:32 * half + 32]
                dve.wait_ge(kfactor_ready, i + 1)
                for j in range(4):
                    V.tensor_tensor(S[:, 4 * half + j, b].rearrange("p (h t) -> p h t", t=TS), ps[:, 32 * j:32 * j + 32].rearrange("p (h t) -> p h t", t=TS),
                                    bc(ssum[:, 8 * j:8 * j + 8].unsqueeze(2), [P, H, TS]), ALU.mult).then_inc(bank_of(("sc", i)), 1)

            for i in range(NG + 1):
                if i < NG:
                    for blk in range(4):
                        ps = result(dve, ("ke", i, blk))
                        copied(dve, ("ke", i, blk), 1)
                        if i >= 2 and blk == 0:
                            dve.wait_ge(side_ready, g.of[("sc", i - 2)][2])
                        V.tensor_copy(kT[:, i % 2, blk], ps[:, :]).then_inc(bank_of(("ke", i, blk)), 1)
                if i >= 2:
                    scores(i - 2)
                if i >= 1:
                    key_sums(i - 1)
            scores(NG - 1)
            for i in range(NG - 4, NG):
                copied(dve, ("sc", i))
            link(V.tensor_reduce(mx, S.rearrange("p k b c -> p b c k").rearrange("p b c k -> p (b c) k"), AX.X, ALU.max))
            V.tensor_tensor(mx[0:TN, :], mx[0:TN, :], ab("snew")[0:TN, :], ALU.max).then_inc(m_ready, 1)
            for c in range(2):
                ps = result(dve, f"mT{c}")
                V.tensor_reduce(stat[:, c:c + 1], ps[:, 0:P], AX.X, ALU.max).then_inc(bank_of(f"mT{c}"), 1)
                copied(dve, f"mT{c}")
                V.tensor_scalar(diag[:, P * c:P * c + P], cst("ident"), stat[:, c:c + 1], None, ALU.mult).then_inc(diag_ready, 1)
            ps = result(dve, "mB")
            Sf = S.rearrange("p k b c -> p k (b c)")
            V.tensor_tensor(Sf, Sf, bc(ps[:, 0:256].unsqueeze(1), [P, NPG, 256]), ALU.subtract).then_inc(bank_of("mB"), 1)
            V.tensor_tensor(ab("snew")[0:TN, :], ab("snew")[0:TN, :], ps[0:TN, 0:256], ALU.subtract).then_inc(bank_of("mB"), 1)
            ps = result(dve, "l")
            V.reciprocal(rl, ps[:, 0:256].rearrange("p (b h t) -> p b h t", b=NS, h=H)).then_inc(bank_of("l"), 1)
            copied(dve, "l")
            for k in range(KB):
                ps = result(dve, f"ol{k}")
                V.tensor_tensor(olat[:, k].rearrange("p h b t -> p b h t"), ps[:, 0:256].rearrange("p (b h t) -> p b h t", b=NS, h=H), rl, ALU.mult).then_inc(bank_of(f"ol{k}"), 1)
            ps = result(dve, "oa")
            V.tensor_copy(mix[:, 0:4, TP:T], ps[:, 0:128].rearrange("p (k t) -> p k t", k=4)).then_inc(bank_of("oa"), 1)

            def add_to_h(names):
                for i, n in enumerate(names):
                    ps = result(dve, n)
                    V.tensor_tensor(h3[:, i], h3[:, i], ps[:, 0:T], ALU.add).then_inc(bank_of(n), 1)

            def up(L, which):
                for i in which:
                    ps = result(dve, ("up", L, i))
                    copied(dve, ("up", L, i), 1)
                    V.tensor_tensor(a2[:, i], a2[:, i], ps[:, 0:T], ALU.mult).then_inc(bank_of(("up", L, i)), 1)

            def gated(base, values, gates, permuted=False):
                for i in range(8):
                    e = (tA, tB)[(base + i) % 2]
                    ps = result(dve, values[i])
                    copied(dve, gates[i])
                    link(V.tensor_scalar(e, e, 1.0, None, ALU.add))
                    link(V.reciprocal(e, e))
                    V.tensor_tensor(e, e, ps[:, 0:T], ALU.mult).then_inc(bank_of(values[i]), 1)
                    copied(dve, values[i])
                    h, x = h3[:, i], e
                    if permuted:
                        h, x = h.rearrange("p (j i) -> p i j", i=TS), e.rearrange("p (i j) -> p i j", i=TS)
                    V.tensor_tensor(h, h, x, ALU.add).then_inc(h_gated, 1)

            add_to_h([("out", i) for i in range(8)])
            norm(1, prm("g_mlp0"))

            def s5_prepare():
                TWO_PI = 2 * np.pi
                C1 = 6.28125
                C2 = float(TWO_PI - C1)
                MAGIC = 12582912.0
                are, aim = prm("a_re"), prm("a_im")
                t0, t1 = tA[:, 0:32], tA[:, 32:64]
                tt = lambda o, a, b, op: link(V.tensor_tensor(o, a, b, op))
                dve.wait_ge(s5_exp, 1)
                tt(cf(1), are, cf(0), ALU.mult)
                tt(cf(2), aim, cf(0), ALU.mult)
                link(V.tensor_scalar(cf(3), cf(2), float(1 / TWO_PI), MAGIC, ALU.mult, ALU.add))
                link(V.tensor_scalar(cf(3), cf(3), MAGIC, None, ALU.subtract))
                link(V.scalar_tensor_tensor(cf(2), cf(3), -C1, cf(2), ALU.mult, ALU.add))
                link(V.scalar_tensor_tensor(cf(2), cf(3), -C2, cf(2), ALU.mult, ALU.add))
                V.tensor_scalar(cf(2), cf(2), 3.1415925, -3.1415925, ALU.min, ALU.max).then_inc(s5_angle, 1)
                up(0, range(0, 2))
                dve.wait_ge(s5_sin, 3)
                tt(cf(6), cf(6), cf(6), ALU.mult)
                link(V.tensor_scalar(cf(6), cf(6), -2.0, 1.0, ALU.mult, ALU.add))
                lr, li, l2r, l2i, l4r, l4i = (cf(i) for i in range(7, 13))
                tt(lr, cf(4), cf(6), ALU.mult)
                tt(li, cf(4), cf(5), ALU.mult)
                for (pr, pi), (xr, xi) in (((l2r, l2i), (lr, li)), ((l4r, l4i), (l2r, l2i))):
                    tt(t0, xr, xr, ALU.mult)
                    tt(t1, xi, xi, ALU.mult)
                    tt(pr, t0, t1, ALU.subtract)
                    tt(t0, xr, xi, ALU.mult)
                    tt(pi, t0, t0, ALU.add)
                for i, (x, s) in enumerate(((l4r, 1.0), (l4i, -1.0), (l4i, 1.0), (l4r, 1.0))):
                    link(V.tensor_scalar(cf(16 + i), x, s, None, ALU.mult))
                tt(t0, are, are, ALU.mult)
                tt(t1, aim, aim, ALU.mult)
                tt(cf(13), t0, t1, ALU.add)
                link(V.reciprocal(cf(13), cf(13)))
                link(V.tensor_scalar(cf(14), lr, -1.0, None, ALU.add))
                tt(t0, cf(14), are, ALU.mult)
                tt(t1, li, aim, ALU.mult)
                tt(cf(15), t0, t1, ALU.add)
                tt(cf(15), cf(15), cf(13), ALU.mult)
                tt(t0, li, are, ALU.mult)
                tt(t1, cf(14), aim, ALU.mult)
                tt(t0, t0, t1, ALU.subtract)
                tt(cf(14), t0, cf(13), ALU.mult)

                def cmul(out, x, cr, ci, done):
                    cr, ci = (bc(c.unsqueeze(2), [P, SB, 16]) for c in (cr, ci))
                    tt(t16[0], x[0], cr, ALU.mult)
                    tt(t16[1], x[1], ci, ALU.mult)
                    tt(out[0], t16[0], t16[1], ALU.subtract)
                    tt(t16[0], x[0], ci, ALU.mult)
                    tt(t16[1], x[1], cr, ALU.mult)
                    V.tensor_tensor(out[1], t16[0], t16[1], ALU.add).then_inc(done, 1)

                dve.wait_ge(s5raw_in, 64)
                cmul(cur, braw, cf(15), cf(14), b_power)
                up(0, range(2, 4))
                for e in range(1, 4):
                    dve.wait_ge(b_power, e)
                    if e >= 2:
                        dve.wait_ge(b_copied, 4 * (e - 1))
                    cmul((cur, braw)[e % 2], (cur, braw)[1 - e % 2], lr, li, b_power)
                    up(0, range(2 + 2 * e, 4 + 2 * e))
                V.tensor_copy(t0[:, 0:1], cf(0)[:, 0:1]).then_inc(c_power, 1)
                up(0, range(10, 12))
                dve.wait_ge(b_copied, 16)
                for e in range(1, 5):
                    dve.wait_ge(c_power, e)
                    if e >= 3:
                        dve.wait_ge(c_copied, 4 * (e - 1))
                    cmul((cur, braw)[e % 2], craw if e == 1 else (cur, braw)[1 - e % 2], lr, li, c_power)
                    up(0, range(10 + 2 * e, 12 + 2 * e))

            s5_prepare()
            up(0, range(20, FB))
            dve.wait_ge(toep_zero, 1)
            for i in range(8):
                ps = result(dve, ("G", i))
                for k in (0, 1):
                    V.tensor_copy(toep[32 * k:32 * k + 32, 4 * i:4 * i + 4, k:4], ps[0:32, :].rearrange("p (s i c) -> p s i c", s=4, i=4)[:, :, 0:4 - k]
                                  ).then_inc(bank_of(("G", i)), 1)
            for i in range(1, 16, 2):
                ps = result(dve, ("BT", i))
                V.tensor_copy(Bim[:, 2 * i - 2:2 * i + 2].rearrange("p s i c -> p (s i c)"), ps[:, :]).then_inc(bank_of(("BT", i)), 1)
            add_to_h([("down", 0, i) for i in range(8)])
            norm(2, prm("g_ple0"))
            gated(0, [("proj", 0, i) for i in range(8)], [("gate", 0, i) for i in range(8)])
            norm(3, prm("g_c"))
            for i in range(1, 16, 2):
                ps = result(dve, ("v5", i))
                V.tensor_copy(vb[:, :, :, 2 * i:2 * i + 2].rearrange("p j r s -> p s r j"), ps[:, 0:4 * J].rearrange("p (s r j) -> p s r j", s=2, r=2)
                              ).then_inc(bank_of(("v5", i)), 1)
            for i in range(12, 16):
                copied(dve, ("v5", i))
            M = coef[:, 16 * 32:20 * 32].rearrange("p (o r s) -> p o r s", o=2, r=2)
            link(V.memset(X[:, :, :, 0:1], 0.0))
            for j in range(JP):
                link(V.tensor_tensor(prod, M, bc(X[:, :, :, j].unsqueeze(1), [P, 2, 2, SB]), ALU.mult))
                link(V.tensor_tensor(part, prod[:, :, 0], prod[:, :, 1], ALU.add))
                if j < JP - 1:
                    link(V.tensor_tensor(X[:, :, :, j + 1], part, vb[:, j], ALU.add))
                else:
                    V.tensor_tensor(fin, part, vb[:, j], ALU.add).then_inc(states_ready, 1)
            dve.wait_ge(x0_in, 32)
            for o in range(2):
                link(V.tensor_tensor(xt[:, o], X[:, :, :, JP:J], bc(M[:, o].unsqueeze(3), [P, 2, SB, NS]), ALU.mult))
            link(V.tensor_tensor(xs, xt[:, :, 0], xt[:, :, 1], ALU.add))
            V.tensor_tensor(xs, xs, vb[:, JP:J].rearrange("p b r s -> p r s b"), ALU.add).then_inc(states_ready, 1)
            V.tensor_copy(rs[:, 0:1], rs[:, 1:2]).then_inc(scan_ready, 1)
            for i in range(8):
                ps = result(dve, ("y5", i))
                link(V.tensor_tensor(ustk[:, 4 * i:4 * i + 4], ustk[:, 4 * i:4 * i + 4], bc(prm("s5_d")[:, 4 * i:4 * i + 4].unsqueeze(2), [P, 4, J]), ALU.mult))
                V.tensor_tensor(ustk[:, 4 * i:4 * i + 4], ustk[:, 4 * i:4 * i + 4], ps[:, 0:4 * J].rearrange("p (s j) -> p s j", s=4), ALU.add).then_inc(bank_of(("y5", i)), 1)
            gated(8, [("glu_a", i) for i in range(8)], [("glu_g", i) for i in range(8)], permuted=True)
            norm(4, prm("g_mlp1"))
            dve.wait_ge(out_done, 16 * (2 + GH + 2))
            up(1, range(FB))
            add_to_h([("down", 1, i) for i in range(8)])
            norm(5, prm("g_ple1"))
            gated(16, [("proj", 1, i) for i in range(8)], [("gate", 1, i) for i in range(8)])



def constants():
    c = np.zeros((P, NCONST), np.float32)

    def put(name, rows, a):
        at, n = CONST[name]
        c[rows, at:at + n] = a

    p = np.arange(P)
    put("ident", slice(None), np.eye(P))
    put("tri", slice(None), (p[:, None] <= p[None, :]) & (p[:, None] // GC == p[None, :] // GC))
    q = np.arange(TN)
    same = (q[:, None] // TS == q[None, :] // TS) & (q[:, None] <= q[None, :])
    put("tri4", slice(0, TN), same)
    put("newmask", slice(0, TN), np.where(same, 0.0, NEG))
    causal = np.where(p[None, :] <= p[:, None], 0.0, NEG)
    put("causal", slice(None), np.concatenate([causal, np.zeros((P, P)), causal], 1))
    half = ROPE // 2
    perm = np.zeros((P, P))
    for j in range(0, P, ROPE):
        for m in range(half):
            perm[j + m + half, j + m] = -1
            perm[j + m, j + m + half] = 1
    put("perm", slice(None), perm)
    freqs = np.float32(10000.0) ** (-np.arange(half, dtype=np.float32) / np.float32(half))
    posn = np.concatenate([np.arange(TP), np.tile(NPG * PAGE + np.arange(TS), NS)]).astype(np.float32)
    ang = np.tile(freqs, 2)[:, None] * posn[None, :]
    put("cosN", slice(64, 96), np.cos(ang))
    put("sinN", slice(64, 96), np.sin(ang))
    for j in range(4):
        posc = ((4 * np.arange(2)[:, None] + j) * PAGE + np.arange(PAGE)[None, :]).reshape(-1).astype(np.float32)
        ang = np.tile(freqs, 2)[:, None] * posc[None, :]
        put("cosC", slice(32 * j, 32 * j + 32), np.cos(ang))
        put("sinC", slice(32 * j, 32 * j + 32), np.sin(ang))
    put("head2", slice(None), (p[:, None] // 64 == np.arange(2)[None, :]) / 96.0)
    put("page4", slice(None), (p[:, None] // 32 == np.arange(4)[None, :]) / 96.0)
    put("seqmask", slice(0, TN), q[:, None] // TS == np.arange(NS)[None, :])
    return c


def arrays(a):
    a = {k: np.asarray(v) for k, v in a.items()}
    f = np.float32

    def blocks(w):
        k, n = w.shape
        return w.reshape(k // P, P, n).transpose(1, 0, 2).reshape(P, -1)

    def cols(v):
        return v.reshape(-1, P).T

    def units(w, width):
        return [blocks(w[:, i:i + width]) for i in range(0, w.shape[1], width)]

    win = a["w_in_ab"][0]
    at = np.cumsum([0, 384, 256, 32, 512, 512, 512, 16, 512])
    cq, ckv, kpe, gq, gk, gv, ga, gr = (win[:, at[i]:at[i + 1]] for i in range(8))
    third = blocks(np.concatenate([ckv[:, P:], kpe, ga], 1))
    stream = [blocks(cq[:, 0:256]), blocks(np.concatenate([cq[:, 256:], ckv[:, :P]], 1)),
              np.concatenate([third, np.zeros((P, UNIT - third.shape[1]), f)], 1)]
    for w in (gq, gk, gv, gr):
        stream += units(w, 256)
    stream += units(a["w_out_ab"][0], 256)

    def layer(i):
        out = units(a["w_up"][i], 256)
        for n in range(8):
            w = blocks(a["w_down"][i][:, P * n:P * n + P])
            out += [w[:, :UNIT], w[:, UNIT:]]
        out += [blocks(a["w_ple_proj"][i])] + units(a["w_ple_gate"][i], 256)
        return out

    stream += layer(0)
    glu = a["w_glu"][0]
    for i in range(8):
        stream.append(blocks(np.concatenate([glu[:, P * i:P * i + P], glu[:, D + P * i:D + P * i + P]], 1)))
    stream += layer(1)
    par = np.zeros((P, NPARAM), f)

    def put(name, v, rows=slice(None)):
        o, n = PARAM[name]
        par[rows, o:o + n] = v

    put("g_ab", cols(a["g_norm_ab"][0]))
    put("g_c", cols(a["g_norm_c"][0]))
    for i in range(2):
        put(f"g_mlp{i}", cols(a["g_norm_mlp"][i]))
        put(f"g_ple{i}", cols(a["g_norm_ple"][i]))
    put("g_qlat", cols(a["g_qlat"][0]))
    put("g_kvlat", cols(a["g_kvlat"][0]))
    put("g_qh", a["g_qh"][0][:, None], slice(0, QK))
    put("g_kh", a["g_kh"][0][:, None], slice(0, QK))
    put("g_kpe", np.tile(a["g_kh"][0][NOPE:], 4)[:, None])
    put("g_o", a["g_gla_o"][0][:, None])
    put("s5_d", np.tile(a["s5_d"][0].reshape(SB, 32).T, (4, 1)))
    put("a_re", cols(a["s5_a_re"][0].reshape(-1)))
    put("a_im", cols(a["s5_a_im"][0].reshape(-1)))
    put("log_dt", cols(np.repeat(a["s5_log_dt"][0], 64)))
    x = np.concatenate([a["x_prompt"][0], a["x_sample"].reshape(TN, D)], 0)
    ukv = a["w_ukv"][0].reshape(256, H, NOPE + VD)
    wu = [blocks(a["w_uq"][0]), blocks(np.ascontiguousarray(ukv[:, :, :NOPE]).reshape(256, 512)), blocks(np.ascontiguousarray(ukv[:, :, NOPE:]).reshape(256, 512))]
    pool = a["cache_ckv"].shape[1]
    states = lambda w: w.reshape(SB, P, 16).transpose(1, 0, 2).reshape(P, -1)
    r = {
        "const": constants(), "param": par, "x": blocks(x.T), "stream": np.stack(stream),
        "table": a["page_table"].reshape(1, -1),
        "wu": np.concatenate(wu, 1),
        "p": np.stack([blocks(np.concatenate([a["p_prompt"][i][0], a["p_sample"][i].reshape(TN, -1)], 0).T) for i in range(2)]),
        "kpeT": a["cache_kpe"][0].transpose(0, 2, 1),
        "ckvT": a["cache_ckv"][0].reshape(pool, PAGE, KB, P).transpose(0, 3, 2, 1).reshape(pool, P, KB * PAGE),
        "ckv": a["cache_ckv"][0],
        "wa2": a["w_gla_a2"][0], "ba": a["b_gla_a"],
        "s0": a["state_gla"][0].transpose(1, 2, 0, 3).reshape(GH, P, NS * GD),
        "b_re": states(a["s5_b_re"][0]), "b_im": states(a["s5_b_im"][0]),
        "c_re": states(a["s5_c_re"][0].transpose(0, 2, 1)), "c_im": states(a["s5_c_im"][0].transpose(0, 2, 1)),
        "x0": np.stack([a[n][0].reshape(NS, SB, P).transpose(2, 1, 0).reshape(P, -1) for n in ("state_s5_re", "state_s5_im")]),
    }
    return {k: np.ascontiguousarray(v) for k, v in r.items()}


OUTS = {"y": (P, DB * T), "ckv": (P, KB * T), "kpe": (32, T), "gla_p": (GH, P, GD), "gla_s": (GH, P, NS * GD),
        "s5_p": (P, 64), "s5_s": (P, 512)}


def kernel(**inputs):
    import concourse.bacc as bacc
    from concourse.bass_utils import run_bass_kernel_spmd

    nc = bacc.Bacc("TRN2", target_bir_lowering=False, num_devices=1)
    data = arrays(inputs)
    ins = {k: nc.dram_tensor(f"in_{k}", v.shape, mybir.dt.from_np(v.dtype), kind="ExternalInput").ap() for k, v in data.items()}
    outs = {k: nc.dram_tensor(f"out_{k}", s, F32, kind="ExternalOutput").ap() for k, s in OUTS.items()}
    program(nc, ins, outs)
    got = run_bass_kernel_spmd(nc, [{f"in_{k}": v for k, v in data.items()}], core_ids=[0]).results[0]
    got = {k: np.asarray(got[f"out_{k}"]) for k in OUTS}

    def tokens(m, b):
        return m.reshape(-1, b, T).transpose(2, 1, 0).reshape(T, -1)

    y, ckv, kpe = tokens(got["y"], DB), tokens(got["ckv"], KB), got["kpe"].T
    c = np.ascontiguousarray
    s5p = got["s5_p"].reshape(P, 2, SB).transpose(1, 2, 0).reshape(2, 1, 1, 64, 64)
    s5s = got["s5_s"].reshape(P, 2, SB, NS).transpose(1, 3, 2, 0).reshape(2, 1, NS, 64, 64)
    return (c(y[:TP])[None], c(y[TP:]).reshape(NS, TS, D), c(ckv[:TP])[None, None], c(kpe[:TP])[None, None],
            c(got["gla_p"])[None, None], c(s5p[0]), c(s5p[1]),
            c(ckv[TP:]).reshape(1, NS, TS, 256), c(kpe[TP:]).reshape(1, NS, TS, 32),
            c(got["gla_s"].reshape(GH, P, NS, GD).transpose(2, 0, 1, 3))[None], c(s5s[0]), c(s5s[1]))
```

```python
from contextlib import ExitStack

import numpy as np

import concourse.bass as bass
from concourse import mybir

F32 = mybir.dt.float32
F32R = mybir.dt.float32r
I32 = mybir.dt.int32
ALU = mybir.AluOpType
ACT = mybir.ActivationFunctionType
AX = mybir.AxisListType

P = 128
D, DB = 1024, 8
TP, NS, TS = 256, 8, 4
TN = NS * TS
T = TP + TN
H, NOPE, ROPE, VD = 8, 64, 32, 64
QK = NOPE + ROPE
QB, KB = 3, 2
PAGE, NPG, POOL = 128, 8, 80
NG = NS * NPG // 4
NP = NS * NPG // 2
SLOTS = 34
GH, GD, GC = 4, 128, 64
NCH = TP // GC
FB = 32
SB = 32
J = TP // TS + NS
JP = TP // TS
EPS = 1e-6
SCALE = float(QK) ** -0.5
RING = 5
UNIT = 2048
NEG = -1e30

UNITS = (["cq01", "cq2kv0", "kv1x"] + ["gq0", "gq1", "gk0", "gk1", "gv0", "gv1", "gr0", "gr1"]
         + [f"out{i}" for i in range(4)]
         + [f"up0_{i}" for i in range(16)] + [f"down0_{i}" for i in range(16)] + ["proj0"] + [f"gate0_{i}" for i in range(4)]
         + [f"glu{i}" for i in range(8)]
         + [f"up1_{i}" for i in range(16)] + [f"down1_{i}" for i in range(16)] + ["proj1"] + [f"gate1_{i}" for i in range(4)])
U = {n: i for i, n in enumerate(UNITS)}
SPLITS = [i for i in range(len(UNITS)) if i <= U["gr1"] or U["up0_0"] <= i <= U["up0_15"] or i >= U["glu0"]]
NIN = U["gr1"] + 1
NUP = 16
HI = (3, 3, 5)


def lay(sizes):
    at, out = 0, {}
    for name, n in sizes:
        out[name] = (at, n)
        at += n
    return out, at


CONST, NCONST = lay([("ident", 128), ("tri", 128), ("tri4", 32), ("causal", 384), ("newmask", 32),
                     ("perm", 128), ("cosN", T), ("sinN", T), ("cosC", 256), ("sinC", 256), ("page4", 4),
                     ("seqmask", 8)])
PARAM, NPARAM = lay([("g_ab", 8), ("g_mlp0", 8), ("g_ple0", 8), ("g_c", 8), ("g_mlp1", 8), ("g_ple1", 8),
                     ("g_qlat", 3), ("g_kvlat", 2), ("g_qh", 1), ("g_kh", 1), ("g_kpe", 1), ("g_o", 1),
                     ("s5_d", 32), ("a_re", 32), ("a_im", 32), ("log_dt", 32)])

AB, NAB = lay([("wuq", QB * H * QK), ("wuk", KB * 512), ("wuv", KB * 512), ("cqn", QB * T), ("ckvn", KB * T),
               ("qh", H * T), ("kh", H * T), ("gq", GH * T), ("gk", GH * T), ("gr", GH * T), ("gv", 3 * 512),
               ("temp", 6144), ("ksq", 1024), ("ssq", 512), ("qabs", 512), ("pages", 2048), ("S", NPG * NS * 32), ("kpe", NG * PAGE),
               ("qbd", NS * 4 * 8), ("qpe", NS * 4 * 32), ("ga", T), ("kpen", T), ("ctok", 257), ("snew", 256), ("kpss", 64), ("stat", 64), ("lin", 512)])
S5A, NS5 = lay([("Bre", SB * 128), ("Bim", SB * 128), ("Cre", SB * 5 * 32), ("Cim", SB * 5 * 32), ("toep", SB * 128),
                ("a2", FB * T), ("coef", 20 * 32)])
NARENA = max(NAB, NS5)


class Groups:

    def __init__(self):
        self.of = {}
        self.order = {"main": 0, "side": 0}
        self.freed = [0] * 8

    def add(self, name, kind, readers=1):
        n = self.order[kind]
        bank = n % 4 + (4 if kind == "side" else 0)
        self.of[name] = (kind, bank, n + 1, self.freed[bank], readers)
        self.order[kind] += 1
        self.freed[bank] += readers


def plan():
    g = Groups()
    side = lambda name, r=1: g.add(name, "side", r)
    main = lambda name, r=1: g.add(name, "main", r)
    side(("ss", 0))
    for n in ("cq0", "cq1", "cq2"):
        main(n, 2)
    main("ckv0", 2)
    main("ckv1", 2)
    main("kpe", 2)
    side("cqss")
    side("ckvss")
    for n in ("gq", "gk"):
        for i in range(4):
            main((n, i))
    for u in range(2):
        for tt in range(3):
            main(("gv", u, tt))
    for i in range(4):
        main(("gr", i), 2)
    main("kpss")
    for c in range(4):
        main(("krotc", c))
    for h in range(H):
        main(("q", h), 2)
    for h in range(H):
        main(("k", h), 2)
    for h in range(H):
        side(("qss", h))
        side(("qrot", h))
    side("krot")
    for h in range(H):
        side(("kss", h))
    for tt in range(2):
        main(("v", tt))
    side("ctok")
    side("snew", H)
    main("qa")

    def pairs(lo, hi):
        for p in range(lo, hi):
            main(("ke", p, 0))
            main(("ke", p, 1))
            side(("sc", p))

    main(("att", 0))
    for h in range(H):
        pairs(h, h + 1)
        if h and h % 2 == 0:
            main(("atto", h // 2 - 1))
        if h + 1 < H:
            main(("att", h + 1))
        side(("attT", h))
    main(("atto", 3))
    for tt in range(3):
        main(("lg", tt), 2)
    pairs(8, 10)
    for h in range(GH):
        main(("b", h))
    pairs(10, 13)
    for h in range(GH):
        side(("ktok", h), 2)
        side(("gatt", h), 2)
    pairs(13, 14)
    for h in range(GH):
        side(("gs", h, 0), 2)
        side(("gs", h, 1), 2)
    for h in range(GH):
        main(("go", h), 2)
        pairs(14 + h, 15 + h)
        side(("oss", h))
        side(("su", h, 0))
        side(("su", h, 1))
    pairs(18, 21)
    side("mT0")
    pairs(21, 22)
    side("mB0", 2)
    pairs(22, 27)
    main("ol0")
    pairs(27, 28)
    side("oT0", 2)
    pairs(28, NP)
    side("mT1")
    side("mB1", 2)
    main("ol1")
    side("oT1", 2)
    side("oa")
    for i in range(8):
        main(("out", i))
    for L in range(2):
        if L == 1:
            side(("ss", 3))
            for i in range(-3, 8):
                for j in range(2):
                    if i + 3 < 8:
                        main(("v5", 2 * i + 6 + j), 4)
                if i >= 0:
                    main(("y5", i), 2)
                if i >= 1:
                    side(("yT", i - 1))
            side(("yT", 7))
            for i in range(8):
                main(("glu_a", i))
                main(("glu_g", i))
        side(("ss", 1 + 3 * L))
        for i in range(FB):
            main(("up", L, i), 2)
        for i in range(8):
            main(("down", L, i))
        if L == 0:
            for i in range(8):
                side(("G", i), 4)
            for i in range(16):
                side(("BT", i))
        side(("ss", 2 + 3 * L))
        for i in range(8):
            main(("proj", L, i))
            main(("gate", L, i), 1)
    return g


def program(nc, ins, outs):
    g = plan()
    ctx = ExitStack()
    with ctx:
        sb = lambda name, n, dt=F32: ctx.enter_context(nc.sbuf_tensor(name, [P, n], dt))
        sem = lambda name: ctx.enter_context(nc.semaphore(name))

        shared = [(f"ring{i}", UNIT) for i in range(RING)] + [("nT", DB * T), ("pT", 2 * T), ("arena", NARENA)]
        with ExitStack() as names:
            inside, used = ([("a2hi", FB * T)] + [(f"hi{i}", UNIT) for i in range(HI[2])] + [("nhi", DB * T), ("phi", 2 * T)]), S5A["Bre"][0]
            assert used == 0
            used = sum(size for _, size in inside)
            inside += [("between", S5A["a2"][0] - used), ("a2lo", FB * T)]
            assert inside[-2][1] > 0
            split = {n: names.enter_context(nc.sbuf_tensor(f"{n}_split", [P, size], F32R)) for n, size in shared[:-1] + inside}
        with ExitStack() as names:
            inside = [("before", sum(size for _, size in shared[:-1]) + AB["temp"][0])] + [(f"in_hi{i}", UNIT) for i in range(HI[0])] + [("in_nhi", DB * T)]
            assert HI[0] * UNIT <= AB["temp"][1]
            for n, size in inside:
                split[n] = names.enter_context(nc.sbuf_tensor(f"{n}_split", [P, size], F32R))
        with ExitStack() as names:
            inside = [("to_c", sum(size for _, size in shared[:-1]) + S5A["Cre"][0])] + [(f"up_hi{i}", UNIT) for i in range(HI[1])] + [("up_nhi", DB * T)]
            assert HI[1] * UNIT + DB * T <= 2 * S5A["Cre"][1]
            for n, size in inside:
                split[n] = names.enter_context(nc.sbuf_tensor(f"{n}_split", [P, size], F32R))
        whole = {n: sb(n, size) for n, size in shared}
        ring = [whole[f"ring{i}"] for i in range(RING)]
        nT, pT, arena = whole["nT"], whole["pT"], whole["arena"]
        hT = sb("hT", DB * T)
        sq = sb("sq", 4 * T)
        rs = sb("rs", T)
        const = sb("const", NCONST)
        par = sb("par", NPARAM)
        ones = sb("ones", 4 * P)
        eps = sb("eps", 1)
        table = sb("table", NS * NPG, I32)
        table2 = sb("table2", NS * NPG, I32)
        tmp = sb("tmp", 600)
        PS = [ctx.enter_context(nc.psum_tensor(f"ps{i}", [P, 512], F32)) for i in range(8)]

        def view(buf, offset, size, **shape):
            v = buf[:, offset:offset + size]
            if shape:
                keys = list(shape)
                v = v.rearrange("p (" + " ".join(keys) + ") -> p " + " ".join(keys), **{k: shape[k] for k in keys})
            return v

        ab = lambda name, **s: view(arena, *AB[name], **s)
        s5 = lambda name, **s: view(arena, *S5A[name], **s)
        cst = lambda name, **s: view(const, *CONST[name], **s)
        prm = lambda name, **s: view(par, *PARAM[name], **s)
        bc = lambda ap, shape: ap.broadcast_to(shape)

        h3 = view(hT, 0, DB * T, b=DB, t=T)
        n3 = view(nT, 0, DB * T, b=DB, t=T)
        sq3 = view(sq, 0, 4 * T, b=4, t=T)
        o1024, o96, o128, o1 = (ones[:, i * P:(i + 1) * P] for i in range(4))
        p3 = view(pT, 0, 2 * T, b=2, t=T)
        tA = tmp[:, 0:T]
        tB = tmp[:, T:2 * T]

        wuq = ab("wuq", k=QB, n=H * QK)
        wuk = ab("wuk", k=KB, n=512)
        wuv = ab("wuv", k=KB, n=512)
        cqn = ab("cqn", b=QB, t=T)
        ckvn = ab("ckvn", b=KB, t=T)
        qh = ab("qh", h=H, t=T)
        kh = ab("kh", h=H, t=T)
        gq = ab("gq", h=GH, t=T)
        gk = ab("gk", h=GH, t=T)
        gr = ab("gr", h=GH, t=T)
        gv = ab("gv", t=3, n=512)
        S = ab("S", k=NPG, b=NS, c=32)
        ksq = ab("ksq", s=2, h=H, n=NOPE)
        ssq = ab("ssq", n=NS * NPG, h=H)
        qabs = ab("qabs", k=KB, b=NS, c=32)
        pages = ab("pages", s=4, j=2, k=KB, n=PAGE)
        cpages = view(arena, AB["gr"][0], SLOTS * 257, s=SLOTS, n=257)
        assert AB["gr"][0] + SLOTS * 257 <= AB["ksq"][0]
        kpe = ab("kpe", g=NG, k=PAGE)
        qbd = ab("qbd", b=NS, k=4, c=8)
        ga = ab("ga")
        kpen = ab("kpen")
        ctok = ab("ctok")
        snew = ab("snew", b=NS, h=H, t=TS)
        kpss = ab("kpss")
        lin = ab("lin")
        stat = ab("stat")
        kto, pgo, So = AB["temp"][0], AB["pages"][0], AB["S"][0]
        sq96 = view(arena, kto, H * T, h=H, t=T)
        r96 = view(arena, kto + H * T, H * T, h=H, t=T)
        sq96k = view(arena, kto + 2 * H * T, H * T, h=H, t=T)
        sqlat = view(arena, AB["kh"][0], 5 * T, b=5, t=T)
        vtok = view(arena, kto + 2 * H * T, 1024, t=2, n=512)
        patt = view(arena, kto, 2 * 384, s=2, n=384)
        pTt = view(arena, kto + 768, 2 * 384, s=2, n=384)
        at = kto

        def gtemp(size, **s):
            nonlocal at
            v = view(arena, at, size, **s)
            at += size
            return v

        lgs = gtemp(3 * 512, t=3, n=512)
        lgmin = view(arena, at, 3 * 512, t=3, n=512)
        bT = gtemp(GH * T, h=GH, t=T)
        dT = gtemp(GH * T, h=GH, t=T)
        qt = bT
        kt = gtemp(GH * T, h=GH, t=T)
        qb = gq
        kd = gtemp(GH * T, h=GH, t=T)
        ktok = view(arena, kto, GH * 384, h=GH, n=384)
        attm = bT
        assert at <= AB["ksq"][0], at
        kpesq = view(arena, AB["ksq"][0] + DB * T, NG * PAGE, g=NG, k=PAGE)
        krt = view(arena, So, 1024, c=2, b=2, n=256)
        wukT = view(arena, So + 1024, 1024, q=4, n=256)
        st = view(arena, AB["qh"][0], GH * 512, h=GH, c=4, v=GD)
        s0 = [view(arena, AB["kh"][0], 1024, b=NS, v=GD), view(arena, AB["kh"][0] + 1024, 1024, b=NS, v=GD)]
        vmask = view(arena, AB["temp"][0] + 3 * 512 + 2 * GH * T, 1024, b=NS, v=GD)
        ebl = view(arena, AB["wuq"][0], GH * T, h=GH, t=T)
        ogt = view(arena, AB["wuq"][0] + GH * T, GH * T, h=GH, t=T)
        qpe = ab("qpe", b=NS, j=4, c=32)
        mx = view(arena, AB["gk"][0], 256)
        diag = view(arena, AB["gk"][0] + 256, 256)
        rl = view(arena, AB["gk"][0] + 512, 2)
        onorm = view(arena, AB["gk"][0] + 520, 512, c=2, n=256)
        olat = view(arena, AB["gq"][0], 512, k=KB, h=H, b=NS, t=TS)
        mix = n3
        Bre, Bim = s5("Bre", s=SB, i=4, c=32), s5("Bim", s=SB, i=4, c=32)
        Cre, Cim = s5("Cre", s=SB, i=5, c=32), s5("Cim", s=SB, i=5, c=32)
        toep = s5("toep", s=SB, i=4, c=32)
        a2 = s5("a2", f=FB, t=T)
        to0, a20, b0 = S5A["toep"][0], S5A["a2"][0], S5A["Bre"][0]
        braw = [view(arena, to0 + 512 * i, 512, s=SB, c=16) for i in range(2)]
        craw = [view(arena, to0 + 1024 + 512 * i, 512, s=SB, c=16) for i in range(2)]
        cur = [view(arena, to0 + 2048 + 512 * i, 512, s=SB, c=16) for i in range(2)]
        t16 = [view(arena, to0 + 3072 + 512 * i, 512, s=SB, c=16) for i in range(2)]
        a2hi = view(split["a2hi"], 0, FB * T, f=FB, t=T)
        a2lo = view(split["a2lo"], 0, FB * T, f=FB, t=T)
        nlo = view(split["nT"], 0, DB * T, b=DB, t=T)
        plo = view(split["pT"], 0, 2 * T, b=2, t=T)
        lo_parts = [split[f"ring{i}"] for i in range(RING)]
        in_nhi = view(split["in_nhi"], 0, DB * T, b=DB, t=T)

        up_nhi = view(split["up_nhi"], 0, DB * T, b=DB, t=T)

        def phase(v):
            if v < NIN:
                return 0, HI[0], "in_hi"
            return (NIN, HI[1], "up_hi") if v < NIN + NUP else (NIN + NUP, HI[2], "hi")

        def hi_part(v):
            first, slots, name = phase(v)
            return split[f"{name}{(v - first) % slots}"]

        nhi = view(split["nhi"], 0, DB * T, b=DB, t=T)
        phi = view(split["phi"], 0, 2 * T, b=2, t=T)
        as_whole = lambda ap: ap.bitcast(F32)
        ustk = view(arena, a20, SB * J, s=SB, j=J)
        to = a20 + SB * J
        rcos, rsin, mag = (view(arena, to + SB * JP * i, SB * JP, s=SB, j=JP) for i in range(3))
        rt = [view(arena, to + SB * JP * 2 + 1024 * i, 1024) for i in range(2)]
        vs0 = to + 3 * SB * JP
        vs = view(arena, vs0, 512, r=2, s=SB, b=NS)
        fin0 = vs0 + 512
        fin = view(arena, fin0, 64, r=2, s=SB)
        X = view(arena, b0, 2 * SB * 128, r=2, s=SB, j=128)
        x0v = view(pT, 0, 512, r=2, s=SB, b=NS)
        zq = [view(const, P, 512, r=2, s=4, j=JP), view(nT, 6 * T, 512, r=2, s=4, j=JP)]
        assert CONST["ident"][0] == 0 and CONST["perm"][0] >= P + 512
        ystep = view(arena, to, 2 * SB * JP, h=2, n=SB * JP)
        zs = [view(const, CONST["perm"][0] + 512 * i, 512, r=2, s=4, j=JP) for i in range(2)]
        assert CONST["perm"][0] + 1024 <= CONST["page4"][0]
        zt = view(tmp, 0, 512, r=2, s=4, j=JP)
        pq = [view(sq, 512 * i, 512, r=2, s=4, j=JP) for i in range(2)]
        xt = view(sq, 0, 1024, o=2, r=2, s=SB, b=NS)
        coef = s5("coef")
        cf = lambda i: coef[:, 32 * i:32 * (i + 1)]

        def sems(names):
            return [sem(n) for n in names.split()]

        (const_in, params_in, w_in, lin_in, p_in0, p_in1, kpe_in, table_in, wukT_in, s5raw_in, x0_in, out_done) = sems("const_in params_in w_in lin_in p_in0 p_in1 kpe_in table_in wukT_in s5raw_in x0_in  out_done")
        main_ready, side_ready, sumsq_step, atto_half = sems("main_ready side_ready sumsq_step atto_half")
        dve_step, act_step = sems("dve_step act_step")
        (ones_set, gr_gate, ga_one, value_ones, qbd_zero, s5_zero, toep_zero, sq_ready, n_ready, cqn_ready, ckvn_ready, kpeg_ready, kpe_squared, kper_ready, qh_ready, kh_ready,
         qbd_ready, qpe_ready, negmax_ready, p_exp, p_ready, softplus_ready, lg_ready, diff_ready, decay_ready, gla_ready,
         vmask_ready, gmix_ready, ckpe_squared, ckpe_scaled, ckpe_ready, m_ready, diag_ready, p_all, states_ready, ksum_ready, ssq_ready, kfactor_ready,
         gate_exp, h_gated, s5_exp, s5_sin, s5_lambda, s5_angle, b_power, c_power, b_copied, c_copied, pow_done, x_start, scan_ready,
         hi_ready, unit_split, n_hi, n_split, a_hi, a_split, p_hi, p_split, gate_ready, pool_step, rotation_ready, turned_back, toep_d, x_ready) = sems(
            "ones_set gr_gate ga_one value_ones qbd_zero s5_zero toep_zero sq_ready n_ready cqn_ready ckvn_ready kpeg_ready kpe_squared kper_ready qh_ready kh_ready "
            "qbd_ready qpe_ready negmax_ready p_exp p_ready softplus_ready lg_ready diff_ready decay_ready gla_ready "
            "vmask_ready gmix_ready ckpe_squared ckpe_scaled ckpe_ready m_ready diag_ready p_all states_ready ksum_ready ssq_ready kfactor_ready "
            "gate_exp h_gated s5_exp s5_sin s5_lambda s5_angle b_power c_power b_copied c_copied pow_done x_start scan_ready "
            "hi_ready unit_split n_hi n_split a_hi a_split p_hi p_split gate_ready pool_step rotation_ready turned_back toep_d x_ready")
        unit_in = [sem(f"unit_in{i}") for i in range(RING)]
        s0_in = [sem(f"s0_in{i}") for i in range(2)]
        s0_out = [sem(f"s0_out{i}") for i in range(2)]
        page_in = [sem(f"page_in{i}") for i in range(4)]
        x_in = [sem(f"x_in{i}") for i in range(2)]
        stack_in, stack_in_pool = ([sem(f"{n}_in{i}") for i in range(2)] for n in ("stack", "stack_pool"))
        table2_in = sem("table2_in")
        y_out = sem("y_out")
        values_in_odd = sem("values_in_odd")
        odd_pages = range(SLOTS + 1, NS * NPG, 2)
        values_in = [sem(f"values_in{i}") for i in range(2)]
        evacuated = [sem(f"evacuated{i}") for i in range(8)]

        block = ctx.enter_context(nc.Block())

        def result(eng, name):
            kind, bank, n = g.of[name][:3]
            eng.wait_ge(main_ready if kind == "main" else side_ready, n)
            return PS[bank]

        def bank_of(name):
            return evacuated[g.of[name][1]]

        def copied(eng, name, n=None):
            _, bank, _, before, readers = g.of[name]
            eng.wait_ge(evacuated[bank], before + (readers if n is None else n))

        def unit_done(u):
            n = UNITS[u]
            last = {"cq01": "cq1", "cq2kv0": "ckv0", "kv1x": "kpe"}.get(n)
            if last is None:
                if n[:2] in ("gq", "gk", "gr"):
                    last = (n[:2], 2 * int(n[2]) + 1)
                elif n[:2] == "gv":
                    last = ("gv", int(n[2]), 2)
                elif n[:3] == "out":
                    last = ("out", 2 * int(n[3:]) + 1)
                elif n[:2] == "up":
                    last = ("up", int(n[2]), 2 * int(n[4:]) + 1)
                elif n[:4] == "down":
                    last = ("down", int(n[4]), int(n[6:]) // 2)
                elif n[:4] == "proj":
                    last = ("proj", int(n[4]), 7)
                elif n[:4] == "gate":
                    last = ("gate", int(n[4]), 2 * int(n[6:]) + 1)
                else:
                    last = ("glu_g", int(n[3:]))
            return g.of[last][2]

        def value_pages(eng, page, which, done):
            for n in which:
                if n >= SLOTS:
                    eng.wait_ge(main_ready, g.of["ol0"][2])
                eng.dma_start(cpages[:, n % SLOTS, 0:256], ins["ckv"][bass.ds(page(n), 1)].rearrange("o p n -> (o p) n")).then_inc(done(n), 16)

        MOVES = [(i, q) for i in range(TS) for q in range(4)]
        SP_MOVES, ACT_MOVES, POOL_MOVES = MOVES[:5], MOVES[5:10], MOVES[10:]
        STACK = ((0, 2), (2, DB))

        def stacked(i, q, lo, hi):
            return (ustk[32 * i:32 * i + 32].rearrange("p (b q) j -> p b q j", q=4)[:, lo:hi, q],
                    n3[32 * q:32 * q + 32, lo:hi, i * J:(i + 1) * J])

        def stack(eng, moves, part, done):
            lo, hi = STACK[part]
            eng.wait_ge(n_ready, 24 + hi)
            for i, q in moves:
                to, frm = stacked(i, q, lo, hi)
                eng.dma_start(to, frm).then_inc(done[part], 16)

        @block.sync
        def _(sp):
            half = DB * T // 2
            for i in range(2):
                sp.dma_start(hT[:, half * i:half * i + half], ins["x"][:, half * i:half * i + half]).then_inc(x_in[i], 16)
            sp.dma_start(par[:, :], ins["param"]).then_inc(params_in, 16)

            def weights(lo, hi):
                for u in range(lo, hi):
                    if u >= RING:
                        sp.wait_ge(main_ready, unit_done(u - RING))
                    sp.dma_start(ring[u % RING][:, :], ins["stream"][u]).then_inc(unit_in[u % RING], 16)

            def page(n):
                return sp.value_load(table2[0:1, n:n + 1], min_val=0, max_val=POOL - 1)

            def page_pairs(lo, hi):
                for p in range(lo, hi):
                    if p >= 4:
                        sp.wait_ge(side_ready, g.of[("sc", p - 4)][2])
                    for j in range(2):
                        sp.dma_start(pages[:, p % 4, j].rearrange("p k n -> p (k n)"),
                                     ins["ckvT"][bass.ds(page(2 * p + j), 1)].rearrange("o p n -> (o p) n")).then_inc(page_in[p % 4], 16)

            first = U["up0_0"] + 1
            weights(0, RING)
            sp.dma_start(const[:, :], ins["const"]).then_inc(const_in, 16)
            sp.dma_start(table2[0:1, :], ins["table"]).then_inc(table2_in, 16)
            weights(RING, first)
            sp.wait_ge(table2_in, 16)
            sp.wait_ge(main_ready, g.of["kpss"][2])
            page_pairs(0, NP)
            value_pages(sp, page, odd_pages, lambda n: values_in_odd)
            weights(first, U["glu4"] + 1)
            for part in range(2):
                stack(sp, SP_MOVES, part, stack_in)
            weights(U["glu4"] + 1, len(UNITS))
            for lo, hi in ((0, 2), (2, 4), (4, 6), (6, 7), (7, 8)):
                sp.wait_ge(h_gated, 16 + hi)
                sp.dma_start(outs["y"][:, lo * T:hi * T], hT[:, lo * T:hi * T]).then_inc(y_out, 16)
            sp.wait_ge(y_out, 16 * 5)

        @block.gpsimd
        def _(pool):
            for i, v in enumerate((1.0 / 1024, 1.0 / 96, 1.0 / 128, 1.0)):
                pool.memset(ones[:, i * P:(i + 1) * P], v).then_inc(ones_set, 1)
            pool.memset(eps[:, :], EPS).then_inc(ones_set, 1)
            pool.memset(ga[0:32, :], 1.0).then_inc(ga_one, 1)
            pool.memset(ctok[:, 256:257], 1.0).then_inc(value_ones, 1)
            pool.memset(ab("qbd"), 0.0).then_inc(qbd_zero, 1)
            pool.memset(ab("qpe"), 0.0).then_inc(qbd_zero, 1)
            pool.dma_start(table[0:1, :], ins["table"]).then_inc(table_in, 16)
            pool.wait_ge(table_in, 16)

            def page(n):
                return pool.value_load(table[0:1, n:n + 1], min_val=0, max_val=POOL - 1)

            for i in range(NG):
                for j in range(4):
                    pg = page(4 * i + j)
                    pool.dma_start(kpe[32 * j:32 * j + 32, i, :], ins["kpeT"][bass.ds(pg, 1)].rearrange("o p k -> (o p) k")).then_inc(kpe_in, 16)
            pool.dma_start(arena[:, 0:AB["cqn"][0]], ins["wu"]).then_inc(w_in, 16)
            pool.dma_start(arena[:, So + 1024:So + 2048], ins["wukT"]).then_inc(wukT_in, 16)
            pool.dma_start(lin[0:17, :], ins["lin"]).then_inc(lin_in, 16)
            pool.dma_start(pT[:, :], ins["p"][0]).then_inc(p_in0, 16)
            pool.wait_ge(ckvn_ready, 1)
            pool.dma_start(outs["ckv"], ab("ckvn")).then_inc(out_done, 16)
            copied(pool, "kpe")
            pool.dma_start(outs["kpe"], kpen[64:96, :]).then_inc(out_done, 16)
            pool.wait_ge(main_ready, g.of[("att", H - 1)][2])
            for h in range(GH + 1):
                if h >= 2:
                    copied(pool, ("su", h - 2, 0))
                    copied(pool, ("su", h - 2, 1))
                    pool.dma_start(outs["gla_s"][h - 2], s0[h % 2].rearrange("p b v -> p (b v)")).then_inc(s0_out[h % 2], 16)
                if h < GH:
                    if h >= 2:
                        pool.wait_ge(s0_out[h % 2], 16 * (h // 2))
                    pool.dma_start(s0[h % 2].rearrange("p b v -> p (b v)"), ins["s0"][h]).then_inc(s0_in[h % 2], 16)
            for h in range(GH):
                copied(pool, ("gs", h, 1))
            for h in range(GH):
                pool.dma_start(outs["gla_p"][h], st[:, h, 3]).then_inc(out_done, 16)
            copied(pool, ("su", GH - 1, 0))
            copied(pool, ("su", GH - 1, 1))
            pool.dma_start(outs["gla_s"][GH - 1], s0[(GH - 1) % 2].rearrange("p b v -> p (b v)")).then_inc(s0_out[(GH - 1) % 2], 16)
            pool.wait_ge(gmix_ready, GH)
            pool.memset(cpages[:, :, 256:257], 1.0).then_inc(value_ones, 1)
            value_pages(pool, page, [n for n in range(NS * NPG) if n not in odd_pages], lambda n: values_in[n // 32])
            copied(pool, "oa")
            pool.wait_ge(out_done, 16 * (2 + GH))
            for i in range(2):
                pool.wait_ge(s0_out[i], 16 * GH // 2)
            for i, n in enumerate(("b_re", "b_im")):
                pool.dma_start(arena[:, to0 + 512 * i:to0 + 512 * i + 512], ins[n]).then_inc(s5raw_in, 16)
            for i, n in enumerate(("c_re", "c_im")):
                pool.dma_start(arena[:, to0 + 1024 + 512 * i:to0 + 1536 + 512 * i], ins[n]).then_inc(s5raw_in, 16)
            c0 = S5A["Cre"][0]
            pool.memset(arena[:, b0:c0], 0.0).then_inc(s5_zero, 1)
            pool.wait_ge(main_ready, g.of[("up", 0, FB - 1)][2])
            pool.memset(arena[:, c0:to0], 0.0).then_inc(s5_zero, 1)
            pool.wait_ge(c_copied, 20)
            pool.memset(arena[:, to0:to0 + SB * 128], 0.0).then_inc(toep_zero, 1)
            for i in range(8):
                pool.wait_ge(main_ready, g.of[("down", 0, i)][2])
            step = [0]

            def link(ins):
                step[0] += 1
                ins.then_inc(pool_step, 1)
                pool.wait_ge(pool_step, step[0])

            tt = lambda o, x, y, op: link(pool.tensor_tensor(o, x, y, op))
            small = [rt[i][:, 0:32] for i in range(2)]

            def squared(out, x):
                tt(small[0], x[0], x[0], ALU.mult)
                tt(small[1], x[1], x[1], ALU.mult)
                tt(out[0], small[0], small[1], ALU.subtract)
                tt(small[0], x[0], x[1], ALU.mult)
                tt(out[1], small[0], small[0], ALU.add)

            power = [(cf(0), cf(1)), (cf(2), cf(3))]
            squared(power[0], (cf(6), cf(5)))
            squared(power[1], power[0])
            for _ in range(2):
                tt(cf(4), cf(4), cf(4), ALU.mult)
            link(pool.memset(rcos[:, :, 0:1], 1.0))
            link(pool.memset(rsin[:, :, 0:1], 0.0))
            n, at = 1, 1
            while n < JP:
                pr, pi = (bc(x.unsqueeze(2), [P, SB, n]) for x in power[at])
                a, b = (rt[i][:, 0:SB * n].rearrange("p (s n) -> p s n", n=n) for i in range(2))
                for out, cr, ci, op in ((rcos, pr, pi, ALU.subtract), (rsin, pi, pr, ALU.add)):
                    tt(a, rcos[:, :, 0:n], cr, ALU.mult)
                    tt(b, rsin[:, :, 0:n], ci, ALU.mult)
                    tt(out[:, :, n:2 * n], a, b, op)
                n *= 2
                if n < JP:
                    squared(power[1 - at], power[at])
                at = 1 - at
            link(pool.tensor_copy(mag, bc(cf(4).unsqueeze(2), [P, SB, JP])))
            pool.memset(mag[:, :, 0:1], 0.0).then_inc(rotation_ready, 1)
            pool.wait_ge(main_ready, g.of[("proj", 0, 7)][2])
            pool.dma_start(pT[:, 0:512], ins["x0"]).then_inc(x0_in, 16)
            for part in range(2):
                stack(pool, POOL_MOVES, part, stack_in_pool)
            for i in range(8):
                blk = slice(4 * i, 4 * i + 4)
                pool.wait_ge(scan_ready, i + 1)
                if i == 0:
                    pool.wait_ge(sq_ready, 32)
                    copied(pool, ("ss", 3))
                z = zs[i % 2]
                pool.tensor_tensor(pq[0], z, bc(rcos[:, blk].unsqueeze(1), [P, 2, 4, JP]), ALU.mult)
                pool.memset(X[:, :, blk, 0:1], 0.0)
                link(pool.tensor_tensor(pq[1], z, bc(rsin[:, blk].unsqueeze(1), [P, 2, 4, JP]), ALU.mult))
                pool.tensor_tensor(X[:, 0, blk, 1:JP + 1], pq[0][:, 0], pq[1][:, 1], ALU.subtract)
                link(pool.tensor_tensor(X[:, 1, blk, 1:JP + 1], pq[0][:, 1], pq[1][:, 0], ALU.add))
                pool.tensor_copy(fin[:, :, blk], X[:, :, blk, JP]).then_inc(turned_back, 1)
            pool.wait_ge(states_ready, 1)
            pool.wait_ge(x_ready, 8)
            pool.dma_start(outs["s5_p"], arena[:, fin0:fin0 + 64]).then_inc(out_done, 16)
            pool.dma_start(outs["s5_s"], arena[:, vs0:vs0 + 512]).then_inc(out_done, 16)
            pool.dma_start(pT[:, :], ins["p"][1]).then_inc(p_in1, 16)
            pool.wait_ge(out_done, 16 * (2 + GH + 2))

        @block.tensor
        def _(pe):
            def bank(name):
                _, b, _, before, _ = g.of[name]
                if before:
                    pe.wait_ge(evacuated[b], before)
                return PS[b]

            def ready(ins, name):
                ins.then_inc(main_ready if g.of[name][0] == "main" else side_ready, 1)

            def unit(name):
                u = U[name]
                pe.wait_ge(unit_in[u % RING], 16 * (u // RING + 1))
                return ring[u % RING]

            def sumsq(k):
                ps = bank(("ss", k))
                for b in range(DB):
                    pe.wait_ge(sq_ready, 8 * k + b + 1)
                    mm = pe.matmul(ps[:, 0:T], o1024, sq3[:, b % 4], start=b == 0, stop=b == DB - 1)
                    if b == DB - 1:
                        ready(mm, ("ss", k))
                    else:
                        mm.then_inc(sumsq_step, 1)

            def split_unit(name):
                u = U[name]
                v = SPLITS.index(u)
                pe.wait_ge(unit_split, v + 1)
                return hi_part(v), lo_parts[u % RING]

            def project_split(name, w, col, width, rhs, wait=None, blocks=DB, last=True, first=True):
                ps = bank(name) if first else PS[g.of[name][1]]
                wh, wl = (x[:, 0:blocks * width].rearrange("p (k n) -> p k n", n=width) for x in w)
                for k in range(blocks):
                    if wait:
                        wait(k)
                    xh, xl = rhs(k)
                    pe.matmul(ps[:, 0:T], wh[:, k, col:col + P], xh, start=first and k == 0, stop=False)
                    pe.matmul(ps[:, 0:T], wh[:, k, col:col + P], xl, start=False, stop=False)
                    mm = pe.matmul(ps[:, 0:T], wl[:, k, col:col + P], xh, start=False, stop=last and k == blocks - 1)
                if last:
                    ready(mm, name)

            nsplit = lambda k: (nhi[:, k], nlo[:, k])
            up_split = lambda k: (up_nhi[:, k], nlo[:, k])
            in_split = lambda k: (in_nhi[:, k], nlo[:, k])

            def split_wait(k):
                return lambda b: pe.wait_ge(n_split, 8 * k + b + 1)

            def project(name, w, col, m, width, rhs, wait=None, base=0, off=0, blocks=DB, last=True, first=True):
                ps = bank(name) if first else PS[g.of[name][1]]
                wv = w[:, off:off + blocks * width].rearrange("p (k n) -> p k n", n=width)
                for k in range(blocks):
                    if wait:
                        wait(k)
                    mm = pe.matmul(ps[base:base + m, 0:T], wv[:, k, col:col + m], rhs(k), start=first and k == 0, stop=last and k == blocks - 1)
                if last:
                    ready(mm, name)

            nk = lambda k: n3[:, k]

            def norm_wait(k):
                return lambda b: pe.wait_ge(n_ready, 8 * k + b + 1)

            pe.wait_ge(ones_set, 4)
            sumsq(0)
            w = split_unit("cq01")
            project_split("cq0", w, 0, 256, in_split, split_wait(0))
            project_split("cq1", w, P, 256, in_split)
            w = split_unit("cq2kv0")
            project_split("cq2", w, 0, 256, in_split)
            project_split("ckv0", w, P, 256, in_split)
            w = split_unit("kv1x")
            project_split("ckv1", w, 0, 256, in_split)
            project_split("kpe", w, P, 256, in_split)
            for name, first, n in (("cqss", 0, QB), ("ckvss", QB, KB)):
                ps = bank(name)
                for i in range(n):
                    copied(pe, f"cq{i}" if first == 0 else f"ckv{i}")
                    mm = pe.matmul(ps[:, 0:T], o1, sqlat[:, first + i], start=i == 0, stop=i == n - 1)
                ready(mm, name)
            for n in ("gq", "gk"):
                for u in range(2):
                    w = split_unit(f"{n}{u}")
                    for c in range(2):
                        project_split((n, 2 * u + c), w, P * c, 256, in_split)
            for u in range(2):
                wh, wl = (x[:, 0:2048].rearrange("p (k n) -> p k n", n=256) for x in split_unit(f"gv{u}"))
                for tt in range(3):
                    lo = P * tt if tt < 2 else T - P
                    ps = bank(("gv", u, tt))
                    for k in range(DB):
                        xh, xl = in_nhi[:, k, lo:lo + P], nlo[:, k, lo:lo + P]
                        pe.matmul(ps[:, 0:256], xh, wh[:, k], start=k == 0, stop=False)
                        pe.matmul(ps[:, 0:256], xh, wl[:, k], start=False, stop=False)
                        mm = pe.matmul(ps[:, 0:256], xl, wh[:, k], start=False, stop=k == DB - 1)
                    ready(mm, ("gv", u, tt))
            for u in range(2):
                w = split_unit(f"gr{u}")
                for c in range(2):
                    project_split(("gr", 2 * u + c), w, P * c, 256, in_split)

            ps = bank("kpss")
            pe.wait_ge(const_in, 16)
            pe.wait_ge(ckpe_squared, 1)
            for i in range(NG):
                mm = pe.matmul(ps[:, 4 * i:4 * i + 4], kpesq[:, i], cst("page4"), start=i == 0, stop=i == NG - 1, skip_group_check=True)
            ready(mm, "kpss")
            perm = cst("perm")
            pe.wait_ge(ckpe_scaled, 1)
            for c in range(4):
                ps = bank(("krotc", c))
                ready(pe.matmul(ps[:, :], perm, kpe[:, 4 * c:4 * c + 4].rearrange("p g k -> p (g k)"), start=True, stop=True), ("krotc", c))
            pe.wait_ge(w_in, 16)
            pe.wait_ge(cqn_ready, 1)
            for h in range(H):
                ps = bank(("q", h))
                for k in range(QB):
                    mm = pe.matmul(ps[0:QK, 0:T], wuq[:, k, QK * h:QK * h + QK], cqn[:, k], start=k == 0, stop=k == QB - 1)
                ready(mm, ("q", h))
            pe.wait_ge(ckvn_ready, 1)
            for h in range(H):
                ps = bank(("k", h))
                for k in range(KB):
                    mm = pe.matmul(ps[0:NOPE, 0:T], wuk[:, k, NOPE * h:NOPE * h + NOPE], ckvn[:, k], start=k == 0, stop=k == KB - 1)
                ready(mm, ("k", h))
            for h in range(H):
                ps = bank(("qss", h))
                copied(pe, ("q", h))
                ready(pe.matmul(ps[0:QK, 0:T], o96[0:QK, 0:QK], sq96[0:QK, h], start=True, stop=True), ("qss", h))
                ps = bank(("qrot", h))
                ready(pe.matmul(ps[64:96, 0:T], perm[64:96, 64:96], qh[64:96, h], start=True, stop=True), ("qrot", h))
            ps = bank("krot")
            pe.wait_ge(kpeg_ready, 1)
            ready(pe.matmul(ps[64:96, 0:T], perm[64:96, 64:96], kh[64:96, 0], start=True, stop=True), "krot")
            for h in range(H):
                ps = bank(("kss", h))
                copied(pe, ("k", h))
                pe.wait_ge(kpe_squared, 1)
                ready(pe.matmul(ps[0:QK, 0:T], o96[0:QK, 0:QK], sq96k[0:QK, h], start=True, stop=True), ("kss", h))
            for tt in range(2):
                ps = bank(("v", tt))
                for k in range(KB):
                    mm = pe.matmul(ps[:, :], ckvn[:, k, tt * P:tt * P + P], wuv[:, k], start=k == 0, stop=k == KB - 1)
                ready(mm, ("v", tt))
            ident = cst("ident")
            ps = bank("ctok")
            for k in range(KB):
                mm = pe.transpose(ps[0:TN, k * P:k * P + P], ckvn[:, k, TP:T], ident)
            ready(mm, "ctok")

            pe.wait_ge(qh_ready, 1)
            pe.wait_ge(kh_ready, 2)
            ps = bank("snew")
            for h in range(H):
                mm = pe.matmul(ps[0:TN, h * TN:h * TN + TN], kh[0:QK, h, TP:T], qh[0:QK, h, TP:T], start=h == 0, stop=h == H - 1,
                               skip_group_check=True)
            ready(mm, "snew")

            def scores(h):
                ps = bank(("att", h))
                pe.matmul(ps[:, 0:P], qh[0:QK, h, 0:P], kh[0:QK, h, 0:P], start=True, stop=False, skip_group_check=True)
                ready(pe.matmul(ps[:, P:3 * P], qh[0:QK, h, P:TP], kh[0:QK, h, 0:TP], start=False, stop=True, skip_group_check=True), ("att", h))

            def turn(h):
                ps = bank(("attT", h))
                pe.wait_ge(p_ready, 2 * h + 2)
                for c in range(3):
                    mm = pe.transpose(ps[:, c * P:c * P + P], patt[:, h % 2, c * P:c * P + P], ident)
                ready(mm, ("attT", h))

            def values(h):
                if h % 2 == 0:
                    bank(("atto", h // 2))
                    copied(pe, ("v", 0))
                    copied(pe, ("v", 1))
                ps = PS[g.of[("atto", h // 2)][1]]
                lo = 64 * (h % 2)
                copied(pe, ("attT", h))
                pe.matmul(ps[lo:lo + 64, 0:TP], vtok[:, 0, VD * h:VD * h + VD], pTt[:, h % 2, 0:TP], start=True, stop=False, skip_group_check=True)
                mm = pe.matmul(ps[lo:lo + 64, P:TP], vtok[:, 1, VD * h:VD * h + VD], pTt[:, h % 2, TP:3 * P], start=False, stop=True, skip_group_check=True)
                if h % 2:
                    ready(mm, ("atto", h // 2))
                else:
                    mm.then_inc(atto_half, 1)

            ps = bank("qa")
            pe.wait_ge(wukT_in, 16)
            pe.wait_ge(qbd_ready, 2)
            for q in range(4):
                for k in range(KB):
                    at = (q * KB + k) * 64
                    mm = pe.matmul(ps[:, at:at + 64], wukT[:, q, P * k:P * k + P], qbd[:, :, q], start=q == 0 and k == 0,
                                   stop=q == 3 and k == KB - 1, skip_group_check=True)
            ready(mm, "qa")

            def pairs(lo, hi):
                for p in range(lo, hi):
                    if p == 0:
                        copied(pe, "qa")
                        pe.wait_ge(qpe_ready, 4)
                        pe.wait_ge(ckpe_ready, 4)
                    b = p // 4
                    pe.wait_ge(page_in[p % 4], 32 * (p // 4 + 1))
                    sc = bank(("sc", p))
                    pe.matmul(sc[:, 0:64], kpe[:, p // 2], qpe[:, b, 2 * (p % 2):2 * (p % 2) + 2].rearrange("p j c -> p (j c)"),
                              start=True, stop=False, skip_group_check=True)
                    for j in range(2):
                        ps = bank(("ke", p, j))
                        for k in range(KB):
                            mm = pe.matmul(ps[:, :], pages[:, p % 4, j, k], wuk[:, k], start=k == 0, stop=k == KB - 1)
                            if k == KB - 1:
                                ready(mm, ("ke", p, j))
                            mm = pe.matmul(sc[:, 32 * j:32 * j + 32], pages[:, p % 4, j, k], qabs[:, k, b], start=False,
                                           stop=j == 1 and k == KB - 1, skip_group_check=True)
                    ready(mm, ("sc", p))

            scores(0)
            for h in range(H):
                pairs(h, h + 1)
                if h:
                    values(h - 1)
                if h + 1 < H:
                    scores(h + 1)
                turn(h)
            values(H - 1)

            pe.wait_ge(lin_in, 16)
            copied(pe, "kpe")
            for tt in range(3):
                m = P if tt < 2 else TN
                ps = bank(("lg", tt))
                ready(pe.matmul(ps[0:m, :], ga[0:17, tt * P:tt * P + m], lin[0:17, :], start=True, stop=True), ("lg", tt))
            pairs(8, 10)
            tri, tri4 = cst("tri"), cst("tri4")
            pe.wait_ge(lg_ready, 3)
            for h in range(GH):
                ps = bank(("b", h))
                for tt in range(2):
                    pe.matmul(ps[:, tt * P:tt * P + P], lgs[:, tt, GD * h:GD * h + GD], tri, start=tt == 0, stop=False, skip_group_check=True)
                ready(pe.matmul(ps[:, TP:T], lgs[0:TN, 2, GD * h:GD * h + GD], tri4[0:TN, :], start=False, stop=True, skip_group_check=True), ("b", h))
            pairs(10, 13)
            pe.wait_ge(gla_ready, 4)
            for h in range(GH):
                ps = bank(("ktok", h))
                for tt in range(2):
                    pe.transpose(ps[:, tt * P:tt * P + P], kd[:, h, tt * P:tt * P + P], ident)
                ready(pe.transpose(ps[0:TN, TP:TP + P], kd[:, h, TP:T], ident), ("ktok", h))
                ps = bank(("gatt", h))
                for tt in range(2):
                    pe.matmul(ps[:, P * tt:P * tt + P], kt[:, h, P * tt:P * tt + P], qt[:, h, P * tt:P * tt + P],
                              start=tt == 0, stop=False, skip_group_check=True)
                ready(pe.matmul(ps[0:TN, TP:T], kt[:, h, TP:T], qt[:, h, TP:T], start=False, stop=True, skip_group_check=True), ("gatt", h))
            pairs(13, 14)
            for h in range(GH):
                copied(pe, ("ktok", h))
                for half in range(2):
                    ps = bank(("gs", h, half))
                    lo = 64 * half
                    for tt in range(2):
                        mm = pe.matmul(ps[:, tt * P:tt * P + P], ktok[lo:lo + 64, h, tt * P:tt * P + P], gv[lo:lo + 64, tt, GD * h:GD * h + GD],
                                       start=tt == 0, stop=tt == 1, skip_group_check=True)
                    ready(mm, ("gs", h, half))
            for h in range(GH):
                ps = bank(("go", h))
                copied(pe, ("gatt", h))
                for tt in range(2):
                    pe.matmul(ps[:, P * tt:P * tt + P], gv[:, tt, GD * h:GD * h + GD], attm[:, h, P * tt:P * tt + P],
                              start=tt == 0, stop=False, skip_group_check=True)
                pe.matmul(ps[:, TP:T], gv[0:TN, 2, GD * h:GD * h + GD], attm[0:TN, h, TP:T], start=False, stop=False, skip_group_check=True)
                pe.wait_ge(s0_in[h % 2], 16 * (h // 2 + 1))
                for b in range(NS):
                    lo = TP + TS * b
                    pe.matmul(ps[:, lo:lo + TS], s0[h % 2][:, b], qb[:, h, lo:lo + TS], start=False, stop=False, skip_group_check=True)
                copied(pe, ("gs", h, 0))
                copied(pe, ("gs", h, 1))
                for c in range(1, NCH):
                    mm = pe.matmul(ps[:, GC * c:GC * c + GC], st[:, h, c - 1], qb[:, h, GC * c:GC * c + GC], start=False, stop=c == NCH - 1,
                                   skip_group_check=True)
                ready(mm, ("go", h))
                pairs(14 + h, 15 + h)
                ps = bank(("oss", h))
                copied(pe, ("go", h))
                ready(pe.matmul(ps[:, 0:T], o128, dT[:, h], start=True, stop=True), ("oss", h))
                pe.wait_ge(vmask_ready, h + 1)
                for c in range(2):
                    ps = bank(("su", h, c))
                    ready(pe.matmul(ps[:, :], ktok[0:TN, h, TP:TP + P], vmask[0:TN, 4 * c:4 * c + 4].rearrange("p b v -> p (b v)"),
                                    start=True, stop=True), ("su", h, c))

            snf = ab("snew")

            def rows_of_maxima(c):
                pe.wait_ge(m_ready, c + 1)
                ps = bank(f"mT{c}")
                ready(pe.transpose(ps[:, 0:P], mx[:, P * c:P * c + P], ident), f"mT{c}")

            def maxima_everywhere(c):
                pe.wait_ge(diag_ready, c + 1)
                ps = bank(f"mB{c}")
                ready(pe.matmul(ps[:, 0:P], o1, diag[:, P * c:P * c + P], start=True, stop=True), f"mB{c}")

            def weighted_values(c):
                pe.wait_ge(p_all, 2 * c + 2)
                copied(pe, "ctok")
                pe.wait_ge(value_ones, 2)
                pe.wait_ge(values_in[c], 16 * (32 - c * len(odd_pages)))
                if c:
                    pe.wait_ge(values_in_odd, 16 * len(odd_pages))
                ps = bank(f"ol{c}")
                pe.matmul(ps[:, 0:257], snf[0:TN, P * c:P * c + P], ctok[0:TN, :], start=True, stop=False, skip_group_check=True)
                for n in range(32 * c, 32 * c + 32):
                    b, kk = n // NPG, n % NPG
                    at = 32 * (b - 4 * c)
                    last = n == 32 * c + 31
                    mm = pe.matmul(ps[at:at + 32, 0:257], S[:, kk, b], cpages[:, n % SLOTS], start=False, stop=last, skip_group_check=True)
                ready(mm, f"ol{c}")

            def latents_up(c):
                copied(pe, f"ol{c}")
                ps = bank(f"oT{c}")
                for k in range(KB):
                    mm = pe.transpose(ps[:, P * k:P * k + P], onorm[:, c, P * k:P * k + P], ident)
                ready(mm, f"oT{c}")

            pairs(18, 21)
            rows_of_maxima(0)
            pairs(21, 22)
            maxima_everywhere(0)
            pairs(22, 27)
            weighted_values(0)
            pairs(27, 28)
            latents_up(0)
            pairs(28, NP)
            rows_of_maxima(1)
            maxima_everywhere(1)
            weighted_values(1)
            latents_up(1)
            ps = bank("oa")
            copied(pe, "oT0")
            copied(pe, "oT1")
            for h in range(H):
                lo, co = 64 * (h % 2), TN * (h // 2)
                for k in range(KB):
                    mm = pe.matmul(ps[lo:lo + 64, co:co + TN], wuv[:, k, VD * h:VD * h + VD], olat[:, k, h].rearrange("p b t -> p (b t)"),
                                   start=h < 2 and k == 0, stop=k == KB - 1, skip_group_check=True)
            ready(mm, "oa")
            copied(pe, "oa")
            copied(pe, ("atto", 3))
            pe.wait_ge(gmix_ready, GH)
            for u in range(4):
                w = unit(f"out{u}")
                for c in range(2):
                    project(("out", 2 * u + c), w, P * c, P, 256, nk)

            def mlp(L):
                sumsq(1 + 3 * L)
                if L == 1:
                    for u in range(16):
                        w = split_unit(f"up{L}_{u}")
                        for c in range(2):
                            project_split(("up", L, 2 * u + c), w, P * c, 256, nsplit, split_wait(3) if u == 0 and c == 0 else None)
                    for i in range(8):
                        for half in range(2):
                            w = split_unit(f"down{L}_{2 * i + half}")
                            project_split(("down", L, i), w, 0, P, lambda k: (a2hi[:, 16 * half + k], a2lo[:, 16 * half + k]),
                                          (lambda k: pe.wait_ge(a_split, 16 * half + k + 1)) if i == 0 else None,
                                          blocks=16, first=half == 0, last=half == 1)
                    return
                for u in range(16):
                    w = split_unit(f"up{L}_{u}")
                    for c in range(2):
                        project_split(("up", L, 2 * u + c), w, P * c, 256, up_split, split_wait(1) if u == 0 and c == 0 else None)
                for i in range(8):
                    for half in range(2):
                        w = unit(f"down{L}_{2 * i + half}")
                        if i == 0:
                            for f in range(16 * half, 16 * half + 16):
                                copied(pe, ("up", L, f))
                        project(("down", L, i), w, 0, P, P, lambda k: a2[:, 16 * half + k], blocks=16, first=half == 0, last=half == 1)
                s5_matrices()

            def s5_matrices():
                pe.wait_ge(b_copied, 16)
                pe.wait_ge(c_copied, 20)
                for i in range(8):
                    ps = bank(("G", i))
                    for s in range(4):
                        for n, (bm, cm) in enumerate(((Bre, Cre), (Bim, Cim))):
                            blk = 4 * i + s
                            mm = pe.matmul(ps[0:32, P * s:P * s + P], bm[:, blk, 3], cm[:, blk, 0:4].rearrange("p i c -> p (i c)"),
                                           start=s == 0 and n == 0, stop=s == 3 and n == 1, skip_group_check=True)
                    ready(mm, ("G", i))
                for i in range(16):
                    ps = bank(("BT", i))
                    bm = (Bre, Bim)[i % 2]
                    for s in range(4):
                        mm = pe.transpose(ps[:, P * s:P * s + P], bm[:, 4 * (i // 2) + s].rearrange("p i c -> p (i c)"), ident)
                    ready(mm, ("BT", i))

            def ple(L):
                sumsq(2 + 3 * L)
                if L == 1:
                    wp = split_unit(f"proj{L}")
                    pe.wait_ge(p_split, 1)
                    for i in range(8):
                        project_split(("proj", L, i), wp, P * i, D, lambda k: (phi[:, k], plo[:, k]), blocks=2)
                        if i % 2 == 0:
                            w = split_unit(f"gate{L}_{i // 2}")
                        project_split(("gate", L, i), w, P * (i % 2), 256, nsplit, split_wait(4) if i == 0 else None)
                    return
                pe.wait_ge(p_in0, 16)
                wp = unit(f"proj{L}")
                for i in range(8):
                    project(("proj", L, i), wp, P * i, P, D, lambda k: p3[:, k], blocks=2)
                    if i % 2 == 0:
                        w = unit(f"gate{L}_{i // 2}")
                    project(("gate", L, i), w, P * (i % 2), P, 256, nk, norm_wait(2 + 3 * L) if i == 0 else None)

            mlp(0)
            ple(0)

            sumsq(3)
            for i in range(16):
                copied(pe, ("BT", i))
            for i in range(8):
                copied(pe, ("G", i))
            pe.wait_ge(toep_d, 8)

            def inputs(i):
                part = 0 if i // 2 < STACK[0][1] else 1
                pe.wait_ge(stack_in[part], 16 * (16 - len(POOL_MOVES)))
                pe.wait_ge(stack_in_pool[part], 16 * len(POOL_MOVES))
                ps = bank(("v5", i))
                for s in range(2):
                    for r, bm in enumerate((Bre, Bim)):
                        blk = 2 * i + s
                        mm = pe.matmul(ps[:, (2 * s + r) * J:(2 * s + r) * J + J], bm[:, blk].rearrange("p i c -> p (i c)"), ustk[:, blk],
                                       start=s == 0 and r == 0, stop=s == 1 and r == 1, skip_group_check=True)
                ready(mm, ("v5", i))

            def outputs(i):
                ps = bank(("y5", i))
                for s in range(4):
                    pe.matmul(ps[0:J, P * s:P * s + P], ustk[:, 4 * i + s], toep[:, 4 * i + s].rearrange("p i c -> p (i c)"),
                              start=s == 0, stop=False, skip_group_check=True)
                pe.wait_ge(x_ready, i + 1)
                for s in range(4):
                    blk = 4 * i + s
                    o = ps[0:J, P * s:P * s + P]
                    pe.matmul(o, X[:, 0, blk, 0:J], Cre[:, blk, 1:5].rearrange("p i c -> p (i c)"), start=False, stop=False, skip_group_check=True)
                    mm = pe.matmul(o, X[:, 1, blk, 0:J], Cim[:, blk, 1:5].rearrange("p i c -> p (i c)"), start=False, stop=s == 3, skip_group_check=True)
                ready(mm, ("y5", i))

            def turned(i):
                ps = bank(("yT", i))
                copied(pe, ("y5", i))
                for t in range(TS):
                    at = 256 * i + P * (t % 2)
                    mm = pe.transpose(ps[:, t * J:t * J + J], ystep[0:J, t // 2, at:at + P], ident[0:J, 0:J])
                ready(mm, ("yT", i))

            for i in range(-3, 8):
                if i + 3 < 8:
                    inputs(2 * i + 6)
                    inputs(2 * i + 7)
                if i >= 0:
                    outputs(i)
                if i >= 1:
                    turned(i - 1)
            turned(7)
            for i in range(8):
                w = split_unit(f"glu{i}")
                project_split(("glu_a", i), w, 0, 256, nsplit, split_wait(2) if i == 0 else None)
                project_split(("glu_g", i), w, P, 256, nsplit)
            mlp(1)
            ple(1)

        @block.scalar
        def _(act):
            step = [0]

            def link(ins):
                step[0] += 1
                ins.then_inc(act_step, 1)
                act.wait_ge(act_step, step[0])

            def squares(k):
                for b in range(DB):
                    square(k, b)

            def square(k, b):
                    if k == 0:
                        act.wait_ge(x_in[b // 4], 16)
                    elif k in (1, 2, 5):
                        copied(act, ("out", b) if k == 1 else ("down", k // 3, b))
                    else:
                        act.wait_ge(h_gated, 8 * (k - 3) + b + 1)
                    if b >= 4:
                        act.wait_ge(sumsq_step, 7 * k + b - 3)
                    act.activation(sq3[:, b % 4], h3[:, b], ACT.Square).then_inc(sq_ready, 1)

            def rsqrt(out, name, rows=P, scale=1.0):
                ps = result(act, name)
                link(act.activation(out, ps[0:rows, 0:T], ACT.Ln, scale=scale, bias=eps[0:rows, :]))
                act.activation(out, out, ACT.Exp, scale=-0.5).then_inc(bank_of(name), 1)

            def table_with_exp_and_ln():
                act.add_instruction(mybir.InstLoadActFuncSet(name=nc.get_next_instruction_name(), act_func_set_id=6, engine=mybir.EngineType.Activation))

            parts = [0]

            def hi_unit(u):
                while parts[0] < len(SPLITS) and SPLITS[parts[0]] <= u:
                    v = parts[0]
                    parts[0] += 1
                    first, slots, _ = phase(v)
                    act.wait_ge(unit_in[SPLITS[v] % RING], 16 * (SPLITS[v] // RING + 1))
                    if v - slots >= first:
                        act.wait_ge(main_ready, unit_done(SPLITS[v - slots]))
                    act.activation(hi_part(v)[:, :], ring[SPLITS[v] % RING][:, :], ACT.Copy).then_inc(hi_ready, 1)

            def n_hi_parts(wait, to=nhi):
                for b in range(DB):
                    wait(b)
                    act.activation(to[:, b], n3[:, b], ACT.Copy).then_inc(n_hi, 1)

            def in_ahead(name):
                hi_unit(min(U[name] + 2, NIN - 1))

            table_with_exp_and_ln()
            act.wait_ge(ones_set, 5)
            squares(0)
            hi_unit(0)
            rsqrt(rs[:, :], ("ss", 0))
            n_hi_parts(lambda b: act.wait_ge(n_ready, b + 1), in_nhi)
            hi_unit(1)
            for i, n in enumerate(("cq0", "cq1", "cq2", "ckv0", "ckv1")):
                in_ahead(("cq01", "cq01", "cq2kv0", "cq2kv0", "kv1x")[i])
                ps = result(act, n)
                act.activation(sqlat[:, i], ps[:, 0:T], ACT.Square).then_inc(bank_of(n), 1)
            ps = result(act, "kpe")
            act.activation(kpen[64:96, :], ps[0:32, 0:T], ACT.Copy).then_inc(bank_of("kpe"), 1)
            act.wait_ge(ga_one, 1)
            act.activation(ga[0:16, :], ps[32:48, 0:T], ACT.Copy).then_inc(bank_of("kpe"), 1)
            rsqrt(tA, "cqss", scale=1.0 / (QB * P))
            rsqrt(tB, "ckvss", scale=1.0 / (KB * P))
            for i in range(GH):
                in_ahead(f"gq{i // 2}")
                ps = result(act, ("gq", i))
                act.activation(gq[:, i], ps[:, 0:T], ACT.Copy, scale=float(GD) ** -0.5).then_inc(bank_of(("gq", i)), 1)
            in_ahead("gk0")
            in_ahead("gk1")
            in_ahead("gv0")
            for i in range(GH):
                in_ahead("gv1")
                ps = result(act, ("gr", i))
                act.activation(gr[:, i], ps[:, 0:T], ACT.Exp, scale=-1.0).then_inc(bank_of(("gr", i)), 1)
                copied(act, ("gr", i), 1)
                link(act.activation(gr[:, i], gr[:, i], ACT.Ln, bias=1.0))
                act.activation(gr[:, i], gr[:, i], ACT.Exp, scale=-1.0).then_inc(gr_gate, 1)
            act.wait_ge(kpe_in, 16 * NS * NPG)
            act.activation(kpesq.rearrange("p g k -> p (g k)"), ab("kpe"), ACT.Square).then_inc(ckpe_squared, 1)
            result(act, ("gr", GH - 1))
            copied(act, "kpe")
            act.activation(sq96k[64:96], bc(kpen[64:96, :].unsqueeze(1), [32, H, T]), ACT.Square).then_inc(kpe_squared, 1)
            for h in range(H):
                ps = result(act, ("q", h))
                act.activation(sq96[0:QK, h], ps[0:QK, 0:T], ACT.Square).then_inc(bank_of(("q", h)), 1)
            for h in range(H):
                ps = result(act, ("k", h))
                act.activation(sq96k[0:NOPE, h], ps[0:NOPE, 0:T], ACT.Square).then_inc(bank_of(("k", h)), 1)
            for h in range(H):
                rsqrt(r96[0:QK, h], ("qss", h), QK)
            act.wait_ge(qh_ready, 1)
            for h in range(H):
                rsqrt(r96[0:QK, h], ("kss", h), QK)
            for tt in range(2):
                ps = result(act, ("v", tt))
                act.activation(vtok[:, tt], ps[:, :], ACT.Copy).then_inc(bank_of(("v", tt)), 1)
            ps = result(act, "ctok")
            act.activation(ctok[0:TN, 0:256], ps[0:TN, 0:256], ACT.Copy).then_inc(bank_of("ctok"), 1)
            ps = result(act, "qa")
            for q in range(4):
                cp = act.activation(qabs[:, :, :, 8 * q:8 * q + 8], ps[:, 128 * q:128 * q + 128].rearrange("p (k b c) -> p k b c", k=KB, b=NS), ACT.Copy)
            cp.then_inc(bank_of("qa"), 1)

            def squared_keys(lo, hi):
                for n in range(2 * lo, 2 * hi):
                    name = ("ke", n // 2, n % 2)
                    ps = result(act, name)
                    if n >= 2:
                        act.wait_ge(ksum_ready, n - 1)
                    act.activation(ksq[:, n % 2].rearrange("p h n -> p (h n)"), ps[:, :], ACT.Square).then_inc(bank_of(name), 1)

            for h in range(H):
                o = 32 * (h % 2)
                act.wait_ge(negmax_ready, h + 1)
                for c, (lo, hi) in enumerate(((0, P), (P, 3 * P))):
                    act.activation(patt[:, h % 2, lo:hi], patt[:, h % 2, lo:hi], ACT.Exp, bias=stat[:, o + 2 + c:o + 3 + c], scale=SCALE,
                                   accum_out=stat[:, o + 4 + c:o + 5 + c]).then_inc(p_exp, 1)
                squared_keys(h, h + 1)
                ps = result(act, ("attT", h))
                if h >= 2:
                    if h % 2 == 0:
                        act.wait_ge(atto_half, h // 2)
                    else:
                        act.wait_ge(main_ready, g.of[("atto", (h - 2) // 2)][2])
                act.activation(pTt[:, h % 2], ps[:, 0:384], ACT.Copy).then_inc(bank_of(("attT", h)), 1)
            for tt in range(3):
                m = P if tt < 2 else TN
                ps = result(act, ("lg", tt))
                act.activation(lgs[0:m, tt], ps[0:m, :], ACT.Abs).then_inc(bank_of(("lg", tt)), 1)
                copied(act, ("lg", tt), 1)
                link(act.activation(lgs[0:m, tt], lgs[0:m, tt], ACT.Exp, scale=-1.0))
                act.activation(lgs[0:m, tt], lgs[0:m, tt], ACT.Ln, bias=1.0).then_inc(softplus_ready, 1)
            squared_keys(8, 10)
            act.wait_ge(diff_ready, 1)
            for h in range(GH):
                copied(act, ("b", h))
            act.activation(ebl, bT, ACT.Exp, scale=1 / 16).then_inc(decay_ready, 1)
            act.activation(kt, dT, ACT.Exp, scale=-1 / 16).then_inc(decay_ready, 1)
            act.activation(kd, kd, ACT.Exp, scale=1 / 16).then_inc(decay_ready, 1)
            act.wait_ge(decay_ready, 1)
            act.activation(qt, dT, ACT.Exp, scale=1 / 16).then_inc(decay_ready, 1)
            squared_keys(10, 13)
            for h in range(GH):
                ps = result(act, ("ktok", h))
                act.activation(ktok[:, h, 0:TP], ps[:, 0:TP], ACT.Copy).then_inc(bank_of(("ktok", h)), 1)
                act.activation(ktok[0:TN, h, TP:384], ps[0:TN, TP:384], ACT.Copy).then_inc(bank_of(("ktok", h)), 1)
            squared_keys(13, 14)
            act.wait_ge(decay_ready, 4)
            for h in range(GH):
                ps = result(act, ("go", h))
                act.activation(dT[:, h], ps[:, 0:T], ACT.Square).then_inc(bank_of(("go", h)), 1)
                squared_keys(14 + h, 15 + h)
                if h >= 2:
                    act.wait_ge(gmix_ready, h - 1)
                rsqrt((tA, tB)[h % 2], ("oss", h))

            def key_factors(c):
                r = ssq.rearrange("p (k b) h -> p k b h", b=NS)[:, :, 4 * c:4 * c + 4]
                act.wait_ge(ssq_ready, c + 1)
                link(act.activation(r, r, ACT.Ln, scale=1.0 / QK, bias=eps[:, :]))
                act.activation(r, r, ACT.Exp, scale=-0.5).then_inc(kfactor_ready, 1)

            def weights(c):
                copied(act, f"mB{c}")
                act.activation(S[:, :, 4 * c:4 * c + 4], S[:, :, 4 * c:4 * c + 4], ACT.Exp, scale=SCALE).then_inc(p_all, 1)
                new = ab("snew")[0:TN, P * c:P * c + P]
                act.activation(new, new, ACT.Exp, scale=SCALE).then_inc(p_all, 1)

            squared_keys(18, 19)
            key_factors(0)
            squared_keys(19, 22)
            weights(0)
            squared_keys(22, NP)
            key_factors(1)
            weights(1)

            def relu(L, i):
                if L == 0:
                    hi_unit(min(U["up0_0"] + i // 2 + 2, U["up0_15"]))
                ps = result(act, ("up", L, i))
                act.activation(a2[:, i], ps[:, 0:T], ACT.Relu).then_inc(bank_of(("up", L, i)), 1)

            def gates(base, names, unit_of=None):
                for i in range(8):
                    n = base + i
                    if unit_of:
                        hi_unit(unit_of(i) + 2)
                    ps = result(act, names[i])
                    if n >= 2:
                        act.wait_ge(h_gated, n - 1)
                    e = (tA, tB)[n % 2]
                    act.activation(e, ps[:, 0:T], ACT.Exp, scale=-1.0).then_inc(bank_of(names[i]), 1)
                    copied(act, names[i])
                    link(act.activation(e, e, ACT.Ln, bias=1.0))
                    act.activation(e, e, ACT.Exp, scale=-1.0).then_inc(gate_ready, 1)

            for b in range(4):
                square(1, b)
            copied(act, "oa")
            act.wait_ge(out_done, 16 * (2 + GH))
            for i in range(2):
                act.wait_ge(s0_out[i], 16 * GH // 2)
            for b in range(4, DB):
                square(1, b)
            hi_unit(U["up0_0"])
            rsqrt(rs[:, :], ("ss", 1))
            n_hi_parts(lambda b: act.wait_ge(n_ready, 8 + b + 1), up_nhi)
            hi_unit(U["up0_1"])
            act.wait_ge(params_in, 16)
            copied(act, "oa")
            act.wait_ge(out_done, 16 * (2 + GH))
            act.activation(cf(0), prm("log_dt"), ACT.Exp).then_inc(s5_exp, 1)
            relu(0, 0)
            relu(0, 1)
            act.wait_ge(s5_angle, 1)
            act.activation(cf(4), cf(1), ACT.Exp).then_inc(s5_sin, 1)
            act.activation(cf(5), cf(2), ACT.Sin).then_inc(s5_sin, 1)
            act.activation(cf(6), cf(2), ACT.Sin, scale=0.5).then_inc(s5_sin, 1)
            table_with_exp_and_ln()
            act.wait_ge(s5_zero, 1)
            for e in range(4):
                relu(0, 2 + 2 * e)
                relu(0, 3 + 2 * e)
                act.wait_ge(b_power, e + 1)
                src = (cur, braw)[e % 2]
                for r, dst in enumerate((Bre, Bim)):
                    for half in range(2):
                        lo = 64 * half
                        act.activation(dst[lo:lo + 64, :, 3 - e, 16 * half:16 * half + 16], src[r][lo:lo + 64], ACT.Copy).then_inc(b_copied, 1)
            for i in range(10, FB):
                relu(0, i)
            act.wait_ge(s5_zero, 2)
            for e in range(5):
                act.wait_ge(c_power, e + 1)
                src = craw if e == 0 else (cur, braw)[e % 2]
                for r, dst in enumerate((Cre, Cim)):
                    for half in range(2):
                        lo = 64 * half
                        act.activation(dst[lo:lo + 64, :, e, 16 * half:16 * half + 16], src[r][lo:lo + 64], ACT.Copy,
                                       scale=1.0 if r == 0 else -1.0).then_inc(c_copied, 1)
            for b in range(4):
                square(2, b)
            act.wait_ge(toep_zero, 1)
            for i in range(8):
                ps = result(act, ("G", i))
                copied(act, ("G", i), 2)
                for k in (2, 3):
                    act.activation(toep[32 * k:32 * k + 32, 4 * i:4 * i + 4, k:4], ps[0:32, :].rearrange("p (s i c) -> p s i c", s=4, i=4)[:, :, 0:4 - k],
                                   ACT.Copy).then_inc(bank_of(("G", i)), 1)
            for i in range(0, 16, 2):
                ps = result(act, ("BT", i))
                act.activation(Bre[:, 2 * i:2 * i + 4].rearrange("p s i c -> p (s i c)"), ps[:, :], ACT.Copy).then_inc(bank_of(("BT", i)), 1)
            for b in range(4, DB):
                square(2, b)
            rsqrt(rs[:, :], ("ss", 2))
            gates(0, [("gate", 0, i) for i in range(8)])
            squares(3)
            rsqrt(rs[:, :], ("ss", 3))
            for part in range(2):
                stack(act, ACT_MOVES, part, stack_in)
            act.wait_ge(x0_in, 16)

            def mixed(i):
                if i == 0:
                    act.wait_ge(stack_in_pool[1], 16 * len(POOL_MOVES))
                    act.wait_ge(stack_in[1], 16 * (16 - len(POOL_MOVES)))
                if i == 6:
                    act.wait_ge(scan_ready, 8)
                ps = result(act, ("yT", i))
                act.activation(n3[:, i], ps[:, 0:T], ACT.Copy).then_inc(bank_of(("yT", i)), 1)

            def sample_inputs(i):
                ps = result(act, ("v5", i))
                act.activation(vs[:, :, 2 * i:2 * i + 2], ps[:, 0:4 * J].rearrange("p (s r j) -> p r s j", s=2, r=2)[:, :, :, JP:J],
                               ACT.Copy).then_inc(bank_of(("v5", i)), 1)

            for i in range(-3, 8):
                if i + 3 < 8:
                    sample_inputs(2 * i + 6)
                    sample_inputs(2 * i + 7)
                if i >= 0:
                    act.wait_ge(turned_back, i + 1)
                    act.activation(X[:, :, 4 * i:4 * i + 4, JP:J], x0v[:, :, 4 * i:4 * i + 4], ACT.Copy).then_inc(x_ready, 1)
                    ps = result(act, ("y5", i))
                    for h in range(2):
                        act.activation(ystep[0:J, h, 256 * i:256 * i + 256].rearrange("p (t s c) -> p t s c", t=2, s=4),
                                       ps[0:J, :].rearrange("p (s h t c) -> p h t s c", s=4, h=2, t=2)[:, h], ACT.Gelu_apprx_tanh).then_inc(bank_of(("y5", i)), 1)
                if i >= 1:
                    mixed(i - 1)
            for i in range(8):
                copied(act, ("y5", i))
            hi_unit(U["glu0"])
            mixed(7)
            table_with_exp_and_ln()
            n_hi_parts(lambda b: copied(act, ("yT", b)))
            hi_unit(U["glu2"])
            gates(8, [("glu_g", i) for i in range(8)], lambda i: U[f"glu{i}"])
            squares(4)
            rsqrt(rs[:, :], ("ss", 4))
            n_hi_parts(lambda b: act.wait_ge(n_ready, 32 + b + 1))

            def a_hi_part(i):
                copied(act, ("up", 1, i))
                act.activation(a2hi[:, i], a2[:, i], ACT.Copy).then_inc(a_hi, 1)

            for i in range(FB):
                hi_unit(U["up1_0"] + i // 2 + 2)
                relu(1, i)
                if i:
                    a_hi_part(i - 1)
            a_hi_part(FB - 1)
            act.wait_ge(p_in1, 16)
            act.activation(phi, p3, ACT.Copy).then_inc(p_hi, 1)
            for i in range(8):
                hi_unit(U["down1_0"] + 2 * i + 3)
                if i < 4:
                    square(5, i)
            for i in range(4, 8):
                square(5, i)
            rsqrt(rs[:, :], ("ss", 5))
            n_hi_parts(lambda b: act.wait_ge(n_ready, 40 + b + 1))
            gates(16, [("gate", 1, i) for i in range(8)], lambda i: U[f"gate1_{i // 2}"])

        @block.vector
        def _(dve):
            step = [0]
            V = nc.vector

            def link(ins):
                step[0] += 1
                ins.then_inc(dve_step, 1)
                dve.wait_ge(dve_step, step[0])

            def norm(k, gain):
                copied(dve, ("ss", k))
                for b in range(DB):
                    if k == 3:
                        o, x, r = n3[:, b].rearrange("p (i j) -> p j i", i=TS), h3[:, b].rearrange("p (j i) -> p j i", i=TS), rs[:, :].rearrange("p (j i) -> p j i", i=TS)
                    else:
                        o, x, r = n3[:, b], h3[:, b], rs[:, :]
                    V.scalar_tensor_tensor(o, x, gain[:, b:b + 1], r, ALU.mult, ALU.mult).then_inc(n_ready, 1)

            dve.wait_ge(params_in, 16)
            for i in range(2):
                dve.wait_ge(x_in[i], 16)
            parts = [0]

            def lo_unit(u):
                while parts[0] < len(SPLITS) and SPLITS[parts[0]] <= u:
                    v = parts[0]
                    parts[0] += 1
                    dve.wait_ge(hi_ready, v + 1)
                    slot = SPLITS[v] % RING
                    V.tensor_tensor(lo_parts[slot][:, :], ring[slot][:, :], as_whole(hi_part(v)[:, :]), ALU.subtract).then_inc(unit_split, 1)

            def n_lo(k, b, of=nhi):
                dve.wait_ge(n_hi, 8 * k + b + 1)
                V.tensor_tensor(nlo[:, b], n3[:, b], as_whole(of[:, b]), ALU.subtract).then_inc(n_split, 1)

            def norm_split(k, gain, use, of=nhi):
                copied(dve, ("ss", k))
                for b in range(DB + 1):
                    if b < DB:
                        V.scalar_tensor_tensor(n3[:, b], h3[:, b], gain[:, b:b + 1], rs[:, :], ALU.mult, ALU.mult).then_inc(n_ready, 1)
                    if b:
                        n_lo(use, b - 1, of)

            def in_ahead(name):
                lo_unit(min(U[name] + 2, NIN - 1))

            lo_unit(0)
            norm_split(0, prm("g_ab"), 0, in_nhi)
            lo_unit(1)
            for i in range(3):
                in_ahead(("cq01", "cq01", "cq2kv0")[i])
                ps = result(dve, f"cq{i}")
                copied(dve, f"cq{i}", 1)
                V.tensor_scalar(cqn[:, i], ps[:, 0:T], prm("g_qlat")[:, i:i + 1], None, ALU.mult).then_inc(bank_of(f"cq{i}"), 1)
            for i in range(2):
                in_ahead(("cq2kv0", "kv1x")[i])
                ps = result(dve, f"ckv{i}")
                copied(dve, f"ckv{i}", 1)
                V.tensor_scalar(ckvn[:, i], ps[:, 0:T], prm("g_kvlat")[:, i:i + 1], None, ALU.mult).then_inc(bank_of(f"ckv{i}"), 1)
            for name, n, x, done in (("cqss", QB, cqn, cqn_ready), ("ckvss", KB, ckvn, ckvn_ready)):
                copied(dve, name)
                V.tensor_tensor(x, x, bc((tA if n == QB else tB).unsqueeze(1), [P, n, T]), ALU.mult).then_inc(done, 1)
            in_ahead("gq0")
            in_ahead("gq1")
            for i in range(GH):
                in_ahead(f"gk{i // 2}")
                ps = result(dve, ("gk", i))
                V.tensor_copy(gk[:, i], ps[:, 0:T]).then_inc(bank_of(("gk", i)), 1)
            for u in range(2):
                for tt in range(3):
                    in_ahead(f"gv{u}")
                    m, lo = (P, 0) if tt < 2 else (TN, P - TN)
                    ps = result(dve, ("gv", u, tt))
                    V.tensor_copy(gv[0:m, tt, 256 * u:256 * u + 256], ps[lo:lo + m, 0:256]).then_inc(bank_of(("gv", u, tt)), 1)
            for i in range(GH):
                ps = result(dve, ("gr", i))
                dve.wait_ge(gr_gate, i + 1)
                V.tensor_tensor(gr[:, i], gr[:, i], ps[:, 0:T], ALU.mult).then_inc(bank_of(("gr", i)), 1)
            dve.wait_ge(const_in, 16)
            ps = result(dve, "kpss")
            V.tensor_copy(kpss.rearrange("p (h j b) -> p h j b", h=2, j=4), ps[:, 0:64].rearrange("p (b h j) -> p h j b", b=NS, h=2)).then_inc(bank_of("kpss"), 1)
            V.tensor_scalar(ab("kpe"), ab("kpe"), prm("g_kpe"), None, ALU.mult).then_inc(ckpe_scaled, 1)
            dve.wait_ge(ckpe_scaled, 1)
            kpc = ab("kpe", c=4, b=2, n=256)
            for c in range(4):
                if c >= 2:
                    dve.wait_ge(ckpe_ready, c - 1)
                ps = result(dve, ("krotc", c))
                V.tensor_tensor(krt[:, c % 2], ps[:, :].rearrange("p (b n) -> p b n", b=2), bc(cst("sinC").unsqueeze(1), [P, 2, 256]), ALU.mult).then_inc(bank_of(("krotc", c)), 1)
                link(V.tensor_tensor(kpc[:, c], kpc[:, c], bc(cst("cosC").unsqueeze(1), [P, 2, 256]), ALU.mult))
                copied(dve, ("krotc", c))
                V.tensor_tensor(kpc[:, c], kpc[:, c], krt[:, c % 2], ALU.add).then_inc(ckpe_ready, 1)
            for h in range(H):
                ps = result(dve, ("q", h))
                copied(dve, ("q", h), 1)
                V.tensor_scalar(qh[0:QK, h], ps[0:QK, 0:T], prm("g_qh")[0:QK], None, ALU.mult).then_inc(bank_of(("q", h)), 1)
            copied(dve, "kpe")
            V.tensor_scalar(kh[64:96, 0], kpen[64:96, :], prm("g_kh")[64:96], None, ALU.mult).then_inc(kpeg_ready, 1)
            for h in range(H):
                ps = result(dve, ("k", h))
                copied(dve, ("k", h), 1)
                V.tensor_scalar(kh[0:NOPE, h], ps[0:NOPE, 0:T], prm("g_kh")[0:NOPE], None, ALU.mult).then_inc(bank_of(("k", h)), 1)
            cosN, sinN = cst("cosN")[64:96], cst("sinN")[64:96]
            dve.wait_ge(const_in, 16)
            for h in range(H):
                ps = result(dve, ("qrot", h))
                V.tensor_tensor(tA[64:96], ps[64:96, 0:T], sinN, ALU.mult).then_inc(bank_of(("qrot", h)), 1)
                link(V.tensor_tensor(qh[64:96, h], qh[64:96, h], cosN, ALU.mult))
                copied(dve, ("qrot", h))
                link(V.tensor_tensor(qh[64:96, h], qh[64:96, h], tA[64:96], ALU.add))
            for h in range(H):
                copied(dve, ("qss", h))
            V.tensor_tensor(qh[0:QK], qh[0:QK], r96[0:QK], ALU.mult).then_inc(qh_ready, 1)
            ps = result(dve, "krot")
            V.tensor_tensor(tA[64:96], ps[64:96, 0:T], sinN, ALU.mult).then_inc(bank_of("krot"), 1)
            dve.wait_ge(kpeg_ready, 1)
            link(V.tensor_tensor(tB[64:96], kh[64:96, 0], cosN, ALU.mult))
            copied(dve, "krot")
            link(V.tensor_tensor(tB[64:96], tB[64:96], tA[64:96], ALU.add))
            for h in range(H):
                copied(dve, ("kss", h))
            V.tensor_tensor(kh[0:NOPE], kh[0:NOPE], r96[0:NOPE], ALU.mult).then_inc(kh_ready, 1)
            V.tensor_tensor(kh[64:96], r96[64:96], bc(tB[64:96].unsqueeze(1), [32, H, T]), ALU.mult).then_inc(kh_ready, 1)
            dve.wait_ge(qbd_zero, 2)
            for par2 in range(2):
                lo = 64 * par2
                for b in range(NS):
                    q = V.tensor_scalar(qbd[lo:lo + 64, b, :, 4 * par2:4 * par2 + 4],
                                        qh[0:64, par2::2, TP + TS * b:TP + TS * b + TS], prm("g_kh")[0:64], None, ALU.mult)
                q.then_inc(qbd_ready, 1)
            for j in range(4):
                for b in range(NS):
                    q = V.tensor_copy(qpe[32 * j:32 * j + 32, b, j].rearrange("p (h t) -> p h t", t=TS), qh[64:96, :, TP + TS * b:TP + TS * b + TS])
                q.then_inc(qpe_ready, 1)
            ps = result(dve, "snew")
            nm = cst("newmask")[0:TN].rearrange("p (b t) -> p b t", t=TS)
            for h in range(H):
                V.tensor_tensor(snew[0:TN, :, h], ps[0:TN, TN * h:TN * h + TN].rearrange("p (b t) -> p b t", t=TS), nm, ALU.add).then_inc(bank_of("snew"), 1)

            def key_sums(lo, hi):
                for p in range(lo, hi):
                    b, k = p // 4, 2 * (p % 4)
                    for j in range(2):
                        copied(dve, ("ke", p, j))
                        V.tensor_reduce(ssq[:, (k + j) * NS + b], ksq[:, j], AX.X, ALU.add).then_inc(ksum_ready, 1)
                    ps = result(dve, ("sc", p))
                    V.tensor_copy(S[:, k:k + 2, b], ps[:, 0:64].rearrange("p (j c) -> p j c", j=2)).then_inc(bank_of(("sc", p)), 1)

            for h in range(H):
                o = 32 * (h % 2)
                ps = result(dve, ("att", h))
                if h >= 2:
                    dve.wait_ge(side_ready, g.of[("attT", h - 2)][2])
                V.tensor_tensor(patt[:, h % 2], ps[:, 0:384], cst("causal"), ALU.add).then_inc(bank_of(("att", h)), 1)
                copied(dve, ("att", h))
                V.tensor_reduce(stat[:, o:o + 1], patt[:, h % 2, 0:P], AX.X, ALU.max)
                link(V.tensor_reduce(stat[:, o + 1:o + 2], patt[:, h % 2, P:384], AX.X, ALU.max))
                V.tensor_scalar(stat[:, o + 2:o + 4], stat[:, o:o + 2], -SCALE, None, ALU.mult).then_inc(negmax_ready, 1)
                dve.wait_ge(p_exp, 2 * h + 2)
                link(V.reciprocal(stat[:, o + 6:o + 8], stat[:, o + 4:o + 6]))
                V.tensor_scalar(patt[:, h % 2, 0:P], patt[:, h % 2, 0:P], stat[:, o + 6:o + 7], None, ALU.mult).then_inc(p_ready, 1)
                V.tensor_scalar(patt[:, h % 2, P:384], patt[:, h % 2, P:384], stat[:, o + 7:o + 8], None, ALU.mult).then_inc(p_ready, 1)
                key_sums(h, h + 1)
                if h and h % 2 == 0 or h == H - 1:
                    q = (h - 1) // 2 if h < H - 1 else 3
                    ps = result(dve, ("atto", q))
                    V.tensor_copy(mix[:, q, 0:TP], ps[:, 0:TP]).then_inc(bank_of(("atto", q)), 1)
            for tt in range(3):
                m = P if tt < 2 else TN
                ps = result(dve, ("lg", tt))
                copied(dve, ("lg", tt), 1)
                V.tensor_scalar(lgmin[0:m, tt], ps[0:m, :], 0.0, None, ALU.min).then_inc(bank_of(("lg", tt)), 1)
                copied(dve, ("lg", tt))
                dve.wait_ge(softplus_ready, tt + 1)
                V.tensor_tensor(lgs[0:m, tt], lgmin[0:m, tt], lgs[0:m, tt], ALU.subtract).then_inc(lg_ready, 1)
            key_sums(8, 10)
            for h in range(GH):
                ps = result(dve, ("b", h))
                V.tensor_copy(bT[:, h], ps[:, 0:T]).then_inc(bank_of(("b", h)), 1)
            for h in range(GH):
                copied(dve, ("b", h))
            for c in range(NCH):
                lo = GC * c
                V.tensor_tensor(dT[:, :, lo:lo + GC], bT[:, :, lo:lo + GC], bc(bT[:, :, lo + GC // 2 - 1:lo + GC // 2], [P, GH, GC]), ALU.subtract)
                V.tensor_tensor(kd[:, :, lo:lo + GC], bc(bT[:, :, lo + GC - 1:lo + GC], [P, GH, GC]), bT[:, :, lo:lo + GC], ALU.subtract)
            for b in range(NS):
                lo = TP + TS * b
                V.tensor_tensor(kd[:, :, lo:lo + TS], bc(bT[:, :, lo + TS - 1:lo + TS], [P, GH, TS]), bT[:, :, lo:lo + TS], ALU.subtract)
            V.tensor_copy(dT[:, :, TP:T], bT[:, :, TP:T]).then_inc(diff_ready, 1)
            for i, (o, x) in enumerate(((kt, gk), (kd, gk), (qt, gq))):
                dve.wait_ge(decay_ready, i + 2)
                V.tensor_tensor(o, o, x, ALU.mult).then_inc(gla_ready, 1)
            dve.wait_ge(gla_ready, 3)
            V.tensor_tensor(qb, ebl, gq, ALU.mult).then_inc(gla_ready, 1)
            key_sums(10, 13)
            for h in range(GH):
                ps = result(dve, ("gatt", h))
                V.tensor_tensor(attm[:, h, 0:TP].rearrange("p (c t) -> p c t", c=2), ps[:, 0:TP].rearrange("p (c t) -> p c t", c=2),
                                bc(cst("tri").unsqueeze(1), [P, 2, P]), ALU.mult).then_inc(bank_of(("gatt", h)), 1)
                V.tensor_tensor(attm[0:TN, h, TP:T], ps[0:TN, TP:T], cst("tri4")[0:TN], ALU.mult).then_inc(bank_of(("gatt", h)), 1)
            key_sums(13, 14)
            for h in range(GH):
                for c in range(NCH):
                    name = ("gs", h, c % 2)
                    ps = result(dve, name)
                    add = ps[:, P * (c // 2):P * (c // 2) + P]
                    if c == 0:
                        V.tensor_copy(st[:, h, 0], add).then_inc(bank_of(name), 1)
                    else:
                        copied(dve, ("gs", h, 1 - c % 2), (c + 1) // 2)
                        V.scalar_tensor_tensor(st[:, h, c], st[:, h, c - 1], ebl[:, h, GC * c + GC - 1:GC * c + GC], add,
                                               ALU.mult, ALU.add).then_inc(bank_of(name), 1)
            for h in range(GH):
                if h >= 1:
                    dve.wait_ge(side_ready, g.of[("su", h - 1, 1)][2])
                V.tensor_tensor(vmask[0:TN], bc(gv[0:TN, 2, GD * h:GD * h + GD].unsqueeze(1), [TN, NS, GD]),
                                bc(cst("seqmask")[0:TN].unsqueeze(2), [TN, NS, GD]), ALU.mult).then_inc(vmask_ready, 1)
                ps = result(dve, ("go", h))
                copied(dve, ("go", h), 1)
                V.tensor_scalar(ogt[:, h], ps[:, 0:T], prm("g_o"), None, ALU.mult).then_inc(bank_of(("go", h)), 1)
                copied(dve, ("go", h))
                key_sums(14 + h, 15 + h)
                copied(dve, ("oss", h))
                link(V.tensor_tensor(ogt[:, h], ogt[:, h], (tA, tB)[h % 2], ALU.mult))
                V.tensor_tensor(mix[:, 4 + h], ogt[:, h], gr[:, h], ALU.mult).then_inc(gmix_ready, 1)
                link(V.tensor_tensor(s0[h % 2], s0[h % 2], bc(ebl[:, h, TP + TS - 1:T:TS].unsqueeze(2), [P, NS, GD]), ALU.mult))
                for c in range(2):
                    ps = result(dve, ("su", h, c))
                    V.tensor_tensor(s0[h % 2][:, 4 * c:4 * c + 4], s0[h % 2][:, 4 * c:4 * c + 4], ps[:, :].rearrange("p (b v) -> p b v", v=GD),
                                    ALU.add).then_inc(bank_of(("su", h, c)), 1)

            def four(x, c):
                return x[:, :, 4 * c:4 * c + 4]

            def key_squares(c):
                last = ("sc", 16 * c + 15)
                copied(dve, last)
                dve.wait_ge(ksum_ready, 32 * c + 32)
                ss = ssq.rearrange("p (k b) h -> p k b h", b=NS)
                kp = kpss.rearrange("p (k b) -> p k b", b=NS)
                V.tensor_tensor(four(ss, c), four(ss, c), bc(four(kp, c).unsqueeze(3), [P, NPG, 4, H]), ALU.add).then_inc(ssq_ready, 1)

            def scaled_scores(c):
                dve.wait_ge(kfactor_ready, c + 1)
                f = ssq.rearrange("p (k b) h -> p k b h", b=NS)
                for k in range(NPG):
                    w = V.tensor_tensor(S[:, k, 4 * c:4 * c + 4].rearrange("p b (h t) -> p b h t", t=TS), S[:, k, 4 * c:4 * c + 4].rearrange("p b (h t) -> p b h t", t=TS),
                                    bc(f[:, k, 4 * c:4 * c + 4].unsqueeze(3), [P, 4, H, TS]), ALU.mult)
                link(w)
                m = mx[:, P * c:P * c + P]
                link(V.tensor_reduce(m, four(S, c).rearrange("p k b c -> p b c k"), AX.X, ALU.max))
                V.tensor_tensor(m[0:TN], m[0:TN], ab("snew")[0:TN, P * c:P * c + P], ALU.max).then_inc(m_ready, 1)

            def maxima(c):
                ps = result(dve, f"mT{c}")
                V.tensor_reduce(stat[:, c:c + 1], ps[:, 0:P], AX.X, ALU.max).then_inc(bank_of(f"mT{c}"), 1)
                copied(dve, f"mT{c}")
                V.tensor_scalar(diag[:, P * c:P * c + P], cst("ident"), stat[:, c:c + 1], None, ALU.mult).then_inc(diag_ready, 1)

            def less_maxima(c):
                ps = result(dve, f"mB{c}")
                Sc = four(S, c).rearrange("p k b c -> p k (b c)")
                V.tensor_tensor(Sc, Sc, bc(ps[:, 0:P].unsqueeze(1), [P, NPG, P]), ALU.subtract).then_inc(bank_of(f"mB{c}"), 1)
                new = ab("snew")[0:TN, P * c:P * c + P]
                V.tensor_tensor(new, new, ps[0:TN, 0:P], ALU.subtract).then_inc(bank_of(f"mB{c}"), 1)

            def over_sums(c):
                ps = result(dve, f"ol{c}")
                link(V.reciprocal(rl[:, c:c + 1], ps[:, 256:257]))
                V.tensor_scalar(onorm[:, c], ps[:, 0:256], rl[:, c:c + 1], None, ALU.mult).then_inc(bank_of(f"ol{c}"), 1)

            def latents(c):
                ps = result(dve, f"oT{c}")
                for k in range(KB):
                    V.tensor_copy(olat[:, k, :, 4 * c:4 * c + 4].rearrange("p h b t -> p b h t"),
                                  ps[:, P * k:P * k + P].rearrange("p (b h t) -> p b h t", b=4, h=H)).then_inc(bank_of(f"oT{c}"), 1)

            key_sums(18, 19)
            key_squares(0)
            key_sums(19, 20)
            scaled_scores(0)
            key_sums(20, 21)
            maxima(0)
            key_sums(21, 22)
            less_maxima(0)
            key_sums(22, 27)
            over_sums(0)
            key_sums(27, 28)
            latents(0)
            key_sums(28, NP)
            key_squares(1)
            scaled_scores(1)
            maxima(1)
            less_maxima(1)
            over_sums(1)
            latents(1)
            ps = result(dve, "oa")
            V.tensor_copy(mix[:, 0:4, TP:T], ps[:, 0:128].rearrange("p (k t) -> p k t", k=4)).then_inc(bank_of("oa"), 1)

            def add_to_h(names, at=0):
                for i, n in enumerate(names, at):
                    ps = result(dve, n)
                    V.tensor_tensor(h3[:, i], h3[:, i], ps[:, 0:T], ALU.add).then_inc(bank_of(n), 1)

            def up(L, which):
                for i in which:
                    lo_unit(min(U["up0_0"] + i // 2 + 2, U["up0_15"]))
                    ps = result(dve, ("up", L, i))
                    copied(dve, ("up", L, i), 1)
                    V.tensor_tensor(a2[:, i], a2[:, i], ps[:, 0:T], ALU.mult).then_inc(bank_of(("up", L, i)), 1)

            def up_split(i):
                if i < FB:
                    lo_unit(U["up1_0"] + i // 2 + 2)
                    ps = result(dve, ("up", 1, i))
                    copied(dve, ("up", 1, i), 1)
                    V.tensor_tensor(a2[:, i], a2[:, i], ps[:, 0:T], ALU.mult).then_inc(bank_of(("up", 1, i)), 1)
                if i:
                    dve.wait_ge(a_hi, i)
                    V.tensor_tensor(a2lo[:, i - 1], a2[:, i - 1], as_whole(a2hi[:, i - 1]), ALU.subtract).then_inc(a_split, 1)

            def gated(base, values, gates, permuted=False, unit_of=None, after=None):
                for i in range(8):
                    if unit_of:
                        lo_unit(unit_of(i) + 2)
                    e = (tA, tB)[(base + i) % 2]
                    ps = result(dve, values[i])
                    dve.wait_ge(gate_ready, base + i + 1)
                    V.tensor_tensor(e, e, ps[:, 0:T], ALU.mult).then_inc(bank_of(values[i]), 1)
                    copied(dve, values[i])
                    h, x = h3[:, i], e
                    if permuted:
                        h, x = h.rearrange("p (j i) -> p i j", i=TS), e.rearrange("p (i j) -> p i j", i=TS)
                    V.tensor_tensor(h, h, x, ALU.add).then_inc(h_gated, 1)
                    if after:
                        after(i)

            add_to_h([("out", i) for i in range(8)])
            lo_unit(U["up0_0"])
            norm_split(1, prm("g_mlp0"), 1, up_nhi)
            lo_unit(U["up0_1"])

            def s5_prepare():
                TWO_PI = 2 * np.pi
                C1 = 6.28125
                C2 = float(TWO_PI - C1)
                MAGIC = 12582912.0
                are, aim = prm("a_re"), prm("a_im")
                t0, t1 = tA[:, 0:32], tA[:, 32:64]
                tt = lambda o, a, b, op: link(V.tensor_tensor(o, a, b, op))
                dve.wait_ge(s5_exp, 1)
                tt(cf(1), are, cf(0), ALU.mult)
                tt(cf(2), aim, cf(0), ALU.mult)
                link(V.tensor_scalar(cf(3), cf(2), float(1 / TWO_PI), MAGIC, ALU.mult, ALU.add))
                link(V.tensor_scalar(cf(3), cf(3), MAGIC, None, ALU.subtract))
                link(V.scalar_tensor_tensor(cf(2), cf(3), -C1, cf(2), ALU.mult, ALU.add))
                link(V.scalar_tensor_tensor(cf(2), cf(3), -C2, cf(2), ALU.mult, ALU.add))
                V.tensor_scalar(cf(2), cf(2), 3.1415925, -3.1415925, ALU.min, ALU.max).then_inc(s5_angle, 1)
                up(0, range(0, 2))
                dve.wait_ge(s5_sin, 3)
                tt(cf(6), cf(6), cf(6), ALU.mult)
                link(V.tensor_scalar(cf(6), cf(6), -2.0, 1.0, ALU.mult, ALU.add))
                lr, li, l2r, l2i, l4r, l4i = (cf(i) for i in range(7, 13))
                tt(lr, cf(4), cf(6), ALU.mult)
                tt(li, cf(4), cf(5), ALU.mult)
                for (pr, pi), (xr, xi) in (((l2r, l2i), (lr, li)), ((l4r, l4i), (l2r, l2i))):
                    tt(t0, xr, xr, ALU.mult)
                    tt(t1, xi, xi, ALU.mult)
                    tt(pr, t0, t1, ALU.subtract)
                    tt(t0, xr, xi, ALU.mult)
                    tt(pi, t0, t0, ALU.add)
                for i, (x, s) in enumerate(((l4r, 1.0), (l4i, -1.0), (l4i, 1.0), (l4r, 1.0))):
                    link(V.tensor_scalar(cf(16 + i), x, s, None, ALU.mult))
                tt(t0, are, are, ALU.mult)
                tt(t1, aim, aim, ALU.mult)
                tt(cf(13), t0, t1, ALU.add)
                link(V.reciprocal(cf(13), cf(13)))
                link(V.tensor_scalar(cf(14), lr, -1.0, None, ALU.add))
                tt(t0, cf(14), are, ALU.mult)
                tt(t1, li, aim, ALU.mult)
                tt(cf(15), t0, t1, ALU.add)
                tt(cf(15), cf(15), cf(13), ALU.mult)
                tt(t0, li, are, ALU.mult)
                tt(t1, cf(14), aim, ALU.mult)
                tt(t0, t0, t1, ALU.subtract)
                tt(cf(14), t0, cf(13), ALU.mult)

                def cmul(out, x, cr, ci, done):
                    cr, ci = (bc(c.unsqueeze(2), [P, SB, 16]) for c in (cr, ci))
                    tt(t16[0], x[0], cr, ALU.mult)
                    tt(t16[1], x[1], ci, ALU.mult)
                    tt(out[0], t16[0], t16[1], ALU.subtract)
                    tt(t16[0], x[0], ci, ALU.mult)
                    tt(t16[1], x[1], cr, ALU.mult)
                    V.tensor_tensor(out[1], t16[0], t16[1], ALU.add).then_inc(done, 1)

                dve.wait_ge(s5raw_in, 64)
                cmul(cur, braw, cf(15), cf(14), b_power)
                up(0, range(2, 4))
                for e in range(1, 4):
                    dve.wait_ge(b_power, e)
                    if e >= 2:
                        dve.wait_ge(b_copied, 4 * (e - 1))
                    cmul((cur, braw)[e % 2], (cur, braw)[1 - e % 2], lr, li, b_power)
                    up(0, range(2 + 2 * e, 4 + 2 * e))
                up(0, range(10, FB))
                V.tensor_copy(t0[:, 0:1], cf(0)[:, 0:1]).then_inc(c_power, 1)
                dve.wait_ge(b_copied, 16)
                for e in range(1, 5):
                    dve.wait_ge(c_power, e)
                    if e >= 3:
                        dve.wait_ge(c_copied, 4 * (e - 1))
                    cmul((cur, braw)[e % 2], craw if e == 1 else (cur, braw)[1 - e % 2], lr, li, c_power)

            def add_d(i):
                copied(dve, ("G", i))
                for s in range(4 * i, 4 * i + 4):
                    t = toep[:, s].rearrange("p i c -> p (i c)")
                    w = V.scalar_tensor_tensor(t, cst("ident"), prm("s5_d")[:, s:s + 1], t, ALU.mult, ALU.add)
                w.then_inc(toep_d, 1)

            s5_prepare()
            add_to_h([("down", 0, i) for i in range(8)])
            dve.wait_ge(toep_zero, 1)
            for i in range(8):
                ps = result(dve, ("G", i))
                for k in (0, 1):
                    V.tensor_copy(toep[32 * k:32 * k + 32, 4 * i:4 * i + 4, k:4], ps[0:32, :].rearrange("p (s i c) -> p s i c", s=4, i=4)[:, :, 0:4 - k]
                                  ).then_inc(bank_of(("G", i)), 1)
            for i in range(1, 16, 2):
                ps = result(dve, ("BT", i))
                V.tensor_copy(Bim[:, 2 * i - 2:2 * i + 2].rearrange("p s i c -> p (s i c)"), ps[:, :]).then_inc(bank_of(("BT", i)), 1)
            norm(2, prm("g_ple0"))
            gated(0, [("proj", 0, i) for i in range(8)], [("gate", 0, i) for i in range(8)], after=add_d)
            norm(3, prm("g_c"))
            dve.wait_ge(rotation_ready, 1)
            for i in range(8):
                if i == 1:
                    dve.wait_ge(stack_in_pool[1], 16 * len(POOL_MOVES))
                    dve.wait_ge(stack_in[1], 16 * (16 - len(POOL_MOVES)))
                z = zq[i % 2]
                for j in range(2):
                    name = ("v5", 2 * i + j)
                    ps = result(dve, name)
                    copied(dve, name, 1)
                    blk = slice(4 * i + 2 * j, 4 * i + 2 * j + 2)
                    v = ps[:, 0:4 * J].rearrange("p (s r j) -> p r s j", s=2, r=2)[:, :, :, 0:JP]
                    two = slice(2 * j, 2 * j + 2)
                    V.tensor_tensor(z[:, :, two], v, bc(rcos[:, blk].unsqueeze(1), [P, 2, 2, JP]), ALU.mult).then_inc(bank_of(name), 1)
                    for r in range(2):
                        V.tensor_tensor(zt[:, r, two], v[:, 1 - r], rsin[:, blk], ALU.mult).then_inc(bank_of(name), 1)
                for j in range(2):
                    copied(dve, ("v5", 2 * i + j))
                V.tensor_tensor(z[:, 0], z[:, 0], zt[:, 0], ALU.add)
                link(V.tensor_tensor(z[:, 1], z[:, 1], zt[:, 1], ALU.subtract))
                if i >= 2:
                    dve.wait_ge(turned_back, i - 1)
                flat = lambda x: x.rearrange("p s j -> p (s j)")
                for r in range(2):
                    w = V.tensor_tensor_scan(flat(zs[i % 2][:, r]), flat(mag[:, 4 * i:4 * i + 4]), flat(z[:, r]), 0.0, ALU.mult, ALU.add)
                    if r == 0:
                        link(w)
                w.then_inc(scan_ready, 1)
            M = coef[:, 16 * 32:20 * 32].rearrange("p (o r s) -> p o r s", o=2, r=2)
            dve.wait_ge(turned_back, 8)
            for i in range(12, 16):
                copied(dve, ("v5", i), 1)
            for o in range(2):
                link(V.tensor_tensor(xt[:, o], x0v, bc(M[:, o].unsqueeze(3), [P, 2, SB, NS]), ALU.mult))
            link(V.tensor_tensor(vs, vs, xt[:, :, 0], ALU.add))
            V.tensor_tensor(vs, vs, xt[:, :, 1], ALU.add).then_inc(states_ready, 1)
            lo_unit(U["glu0"])
            for b in range(DB):
                n_lo(2, b)
            lo_unit(U["glu2"])
            gated(8, [("glu_a", i) for i in range(8)], [("glu_g", i) for i in range(8)], permuted=True, unit_of=lambda i: U[f"glu{i}"])
            norm_split(4, prm("g_mlp1"), 3)
            dve.wait_ge(out_done, 16 * (2 + GH + 2))
            for i in range(FB + 1):
                up_split(i)
            dve.wait_ge(p_hi, 1)
            V.tensor_tensor(plo, p3, as_whole(phi), ALU.subtract).then_inc(p_split, 1)
            for i in range(8):
                lo_unit(U["down1_0"] + 2 * i + 3)
                add_to_h([("down", 1, i)], i)
            norm_split(5, prm("g_ple1"), 4)
            gated(16, [("proj", 1, i) for i in range(8)], [("gate", 1, i) for i in range(8)], unit_of=lambda i: U[f"gate1_{i // 2}"])


def constants():
    c = np.zeros((P, NCONST), np.float32)

    def put(name, rows, a):
        at, n = CONST[name]
        c[rows, at:at + n] = a

    p = np.arange(P)
    put("ident", slice(None), np.eye(P))
    put("tri", slice(None), (p[:, None] <= p[None, :]) & (p[:, None] // GC == p[None, :] // GC))
    q = np.arange(TN)
    same = (q[:, None] // TS == q[None, :] // TS) & (q[:, None] <= q[None, :])
    put("tri4", slice(0, TN), same)
    put("newmask", slice(0, TN), np.where(same, 0.0, NEG))
    causal = np.where(p[None, :] <= p[:, None], 0.0, NEG)
    put("causal", slice(None), np.concatenate([causal, np.zeros((P, P)), causal], 1))
    half = ROPE // 2
    perm = np.zeros((P, P))
    for j in range(0, P, ROPE):
        for m in range(half):
            perm[j + m + half, j + m] = -1
            perm[j + m, j + m + half] = 1
    put("perm", slice(None), perm)
    freqs = np.float32(10000.0) ** (-np.arange(half, dtype=np.float32) / np.float32(half))
    posn = np.concatenate([np.arange(TP), np.tile(NPG * PAGE + np.arange(TS), NS)]).astype(np.float32)
    ang = np.tile(freqs, 2)[:, None] * posn[None, :]
    put("cosN", slice(64, 96), np.cos(ang))
    put("sinN", slice(64, 96), np.sin(ang))
    for j in range(4):
        posc = ((4 * np.arange(2)[:, None] + j) * PAGE + np.arange(PAGE)[None, :]).reshape(-1).astype(np.float32)
        ang = np.tile(freqs, 2)[:, None] * posc[None, :]
        put("cosC", slice(32 * j, 32 * j + 32), np.cos(ang))
        put("sinC", slice(32 * j, 32 * j + 32), np.sin(ang))
    put("page4", slice(None), p[:, None] // 32 == np.arange(4)[None, :])
    put("seqmask", slice(0, TN), q[:, None] // TS == np.arange(NS)[None, :])
    return c


def arrays(a):
    a = {k: np.asarray(v) for k, v in a.items()}
    f = np.float32

    def blocks(w):
        k, n = w.shape
        return w.reshape(k // P, P, n).transpose(1, 0, 2).reshape(P, -1)

    def cols(v):
        return v.reshape(-1, P).T

    def units(w, width):
        return [blocks(w[:, i:i + width]) for i in range(0, w.shape[1], width)]

    win = a["w_in_ab"][0]
    at = np.cumsum([0, 384, 256, 32, 512, 512, 512, 16, 512])
    cq, ckv, kpe, gq, gk, gv, ga, gr = (win[:, at[i]:at[i + 1]] for i in range(8))
    third = blocks(np.concatenate([ckv[:, P:], kpe, ga, np.zeros((D, 2 * P - P - 48), f)], 1))
    stream = [blocks(cq[:, 0:256]), blocks(np.concatenate([cq[:, 256:], ckv[:, :P]], 1)),
              third]
    for w in (gq, gk, gv, gr):
        stream += units(w, 256)
    stream += units(a["w_out_ab"][0], 256)

    def layer(i):
        out = units(a["w_up"][i], 256)
        for n in range(8):
            w = blocks(a["w_down"][i][:, P * n:P * n + P])
            out += [w[:, :UNIT], w[:, UNIT:]]
        out += [blocks(a["w_ple_proj"][i])] + units(a["w_ple_gate"][i], 256)
        return out

    stream += layer(0)
    glu = a["w_glu"][0]
    for i in range(8):
        stream.append(blocks(np.concatenate([glu[:, P * i:P * i + P], glu[:, D + P * i:D + P * i + P]], 1)))
    stream += layer(1)
    par = np.zeros((P, NPARAM), f)

    def put(name, v, rows=slice(None)):
        o, n = PARAM[name]
        par[rows, o:o + n] = v

    put("g_ab", cols(a["g_norm_ab"][0]))
    put("g_c", cols(a["g_norm_c"][0]))
    for i in range(2):
        put(f"g_mlp{i}", cols(a["g_norm_mlp"][i]))
        put(f"g_ple{i}", cols(a["g_norm_ple"][i]))
    put("g_qlat", cols(a["g_qlat"][0]))
    put("g_kvlat", cols(a["g_kvlat"][0]))
    put("g_qh", a["g_qh"][0][:, None], slice(0, QK))
    put("g_kh", a["g_kh"][0][:, None], slice(0, QK))
    put("g_kpe", np.tile(a["g_kh"][0][NOPE:], 4)[:, None])
    put("g_o", a["g_gla_o"][0][:, None])
    put("s5_d", np.tile(a["s5_d"][0].reshape(SB, 32).T, (4, 1)))
    put("a_re", cols(a["s5_a_re"][0].reshape(-1)))
    put("a_im", cols(a["s5_a_im"][0].reshape(-1)))
    put("log_dt", cols(np.repeat(a["s5_log_dt"][0], 64)))
    x = np.concatenate([a["x_prompt"][0], a["x_sample"].reshape(TN, D)], 0)
    ukv = a["w_ukv"][0].reshape(256, H, NOPE + VD)
    wu = [blocks(a["w_uq"][0]), blocks(np.ascontiguousarray(ukv[:, :, :NOPE]).reshape(256, 512)), blocks(np.ascontiguousarray(ukv[:, :, NOPE:]).reshape(256, 512))]
    pool = a["cache_ckv"].shape[1]
    states = lambda w: w.reshape(SB, P, 16).transpose(1, 0, 2).reshape(P, -1)
    r = {
        "const": constants(), "param": par, "x": blocks(x.T), "stream": np.stack(stream),
        "table": a["page_table"].reshape(1, -1),
        "wu": np.concatenate(wu, 1),
        "p": np.stack([blocks(np.concatenate([a["p_prompt"][i][0], a["p_sample"][i].reshape(TN, -1)], 0).T) for i in range(2)]),
        "kpeT": a["cache_kpe"][0].transpose(0, 2, 1),
        "ckvT": a["cache_ckv"][0].reshape(pool, PAGE, KB, P).transpose(0, 3, 2, 1).reshape(pool, P, KB * PAGE),
        "ckv": a["cache_ckv"][0],
        "lin": np.concatenate([a["w_gla_a2"][0], a["b_gla_a"]], 0),
        "wukT": ukv[:, :, :NOPE].reshape(256, 4, P).transpose(2, 1, 0).reshape(P, -1),
        "s0": a["state_gla"][0].transpose(1, 2, 0, 3).reshape(GH, P, NS * GD),
        "b_re": states(a["s5_b_re"][0]), "b_im": states(a["s5_b_im"][0]),
        "c_re": states(a["s5_c_re"][0].transpose(0, 2, 1)), "c_im": states(a["s5_c_im"][0].transpose(0, 2, 1)),
        "x0": np.concatenate([a[n][0].reshape(NS, SB, P).transpose(2, 1, 0).reshape(P, -1) for n in ("state_s5_re", "state_s5_im")], 1),
    }
    return {k: np.ascontiguousarray(v) for k, v in r.items()}


OUTS = {"y": (P, DB * T), "ckv": (P, KB * T), "kpe": (32, T), "gla_p": (GH, P, GD), "gla_s": (GH, P, NS * GD),
        "s5_p": (P, 64), "s5_s": (P, 512)}


def kernel(**inputs):
    import concourse.bacc as bacc
    from concourse.bass_utils import run_bass_kernel_spmd

    nc = bacc.Bacc("TRN2", target_bir_lowering=False, num_devices=1)
    data = arrays(inputs)
    ins = {k: nc.dram_tensor(f"in_{k}", v.shape, mybir.dt.from_np(v.dtype), kind="ExternalInput").ap() for k, v in data.items()}
    outs = {k: nc.dram_tensor(f"out_{k}", s, F32, kind="ExternalOutput").ap() for k, s in OUTS.items()}
    program(nc, ins, outs)
    got = run_bass_kernel_spmd(nc, [{f"in_{k}": v for k, v in data.items()}], core_ids=[0]).results[0]
    got = {k: np.asarray(got[f"out_{k}"]) for k in OUTS}

    def tokens(m, b):
        return m.reshape(-1, b, T).transpose(2, 1, 0).reshape(T, -1)

    y, ckv, kpe = tokens(got["y"], DB), tokens(got["ckv"], KB), got["kpe"].T
    c = np.ascontiguousarray
    s5p = got["s5_p"].reshape(P, 2, SB).transpose(1, 2, 0).reshape(2, 1, 1, 64, 64)
    s5s = got["s5_s"].reshape(P, 2, SB, NS).transpose(1, 3, 2, 0).reshape(2, 1, NS, 64, 64)
    return (c(y[:TP])[None], c(y[TP:]).reshape(NS, TS, D), c(ckv[:TP])[None, None], c(kpe[:TP])[None, None],
            c(got["gla_p"])[None, None], c(s5p[0]), c(s5p[1]),
            c(ckv[TP:]).reshape(1, NS, TS, 256), c(kpe[TP:]).reshape(1, NS, TS, 32),
            c(got["gla_s"].reshape(GH, P, NS, GD).transpose(2, 0, 1, 3))[None], c(s5s[0]), c(s5s[1]))
```
